# Optimizing a Trainium2 kernel written in Bass

```python
import math
import jax
import jax.numpy as jnp
from jax import lax
import numpy as np

D_MODEL = 1024
BATCH = 1
SEQ = 512
DEPTH = 2

EPS = 1e-6
CONV_WIDTH = 4
N_BRANCHES = 4
BRANCH_WIDTH = D_MODEL // 2

SSM_HEADS = 8
SSM_HEAD_DIM = BRANCH_WIDTH // SSM_HEADS
SSM_GROUPS = 2
SSM_STATE = 64
SSM_CHUNK = 64
SSM_XBC = BRANCH_WIDTH + 2 * SSM_GROUPS * SSM_STATE

GDN_HEADS = 4
GDN_HEAD_DIM = BRANCH_WIDTH // GDN_HEADS
GDN_CHUNK = 64

GLA_HEADS = 4
GLA_VAL_DIM = BRANCH_WIDTH // GLA_HEADS
GLA_KEY_DIM = GLA_VAL_DIM // 2
GLA_GATE_RANK = 16
GLA_GATE_TAU = 16.0
GLA_CHUNK = 16

LRU_BLOCKS = 8
LRU_BLOCK_DIM = BRANCH_WIDTH // LRU_BLOCKS
LRU_C = 8.0

PEER_HEADS = 8
PEER_N_KEYS = 128
PEER_N_EXPERTS = PEER_N_KEYS * PEER_N_KEYS
PEER_QUERY_DIM = 256
PEER_HALF_DIM = PEER_QUERY_DIM // 2
PEER_TOPK = 16
PEER_TOKEN_BLOCK = 128

IN_SIZES = (
    BRANCH_WIDTH,
    SSM_XBC,
    SSM_HEADS,
    3 * BRANCH_WIDTH,
    BRANCH_WIDTH,
    GDN_HEADS,
    GDN_HEADS,
    GLA_HEADS * GLA_KEY_DIM,
    GLA_HEADS * GLA_KEY_DIM,
    BRANCH_WIDTH,
    BRANCH_WIDTH,
    GLA_GATE_RANK,
    BRANCH_WIDTH,
    BRANCH_WIDTH,
    N_BRANCHES * D_MODEL,
)
D_IN = sum(IN_SIZES)

kernel_name = "hybrid_ssd_gdn_gla_rglru_peer_adaln"

def _split(t, sizes):
    out, o = [], 0
    for s in sizes:
        out.append(t[..., o:o + s])
        o += s
    return out

def _rmsnorm(t, w):
    tf = t.astype(jnp.float32)
    tf = tf * lax.rsqrt(jnp.mean(tf * tf, axis=-1, keepdims=True) + EPS)
    return (tf * w.astype(jnp.float32)).astype(t.dtype)

def _l2norm(t):
    return t * lax.rsqrt(jnp.sum(t * t, axis=-1, keepdims=True) + EPS)

def _causal_dwconv(t, w, b=None):
    k_w, ch = w.shape
    y = lax.conv_general_dilated(t, w[:, None, :].astype(t.dtype), window_strides=(1,),
                                 padding=((k_w - 1, 0),), dimension_numbers=("NWC", "WIO", "NWC"),
                                 feature_group_count=ch)
    return y if b is None else y + b

def _ssd_mixer(z, xbc, dt_raw, conv_w, conv_b, dt_bias, a_log, d_skip, norm_w):
    f32 = jnp.float32
    bsz, T, _ = xbc.shape
    nc, L, H = T // SSM_CHUNK, SSM_CHUNK, SSM_HEADS
    xbc = jax.nn.silu(_causal_dwconv(xbc, conv_w, conv_b)).astype(f32)
    xs, bm, cm = _split(xbc, (BRANCH_WIDTH, SSM_GROUPS * SSM_STATE, SSM_GROUPS * SSM_STATE))
    xs = xs.reshape(bsz, T, H, SSM_HEAD_DIM)
    rep = H // SSM_GROUPS
    bm = jnp.repeat(bm.reshape(bsz, T, SSM_GROUPS, SSM_STATE), rep, axis=2)
    cm = jnp.repeat(cm.reshape(bsz, T, SSM_GROUPS, SSM_STATE), rep, axis=2)
    dt = jax.nn.softplus(dt_raw.astype(f32) + dt_bias.astype(f32))
    da = dt * (-jnp.exp(a_log.astype(f32)))
    shp = (bsz, nc, L)
    xdt = (xs * dt[..., None]).reshape(shp + (H, SSM_HEAD_DIM))
    bc = bm.reshape(shp + (H, SSM_STATE))
    cc = cm.reshape(shp + (H, SSM_STATE))
    cs = jnp.cumsum(da.reshape(shp + (H,)), axis=2)
    causal = jnp.tril(jnp.ones((L, L), bool))[None, None, :, :, None]
    seg = jnp.exp(jnp.where(causal, cs[:, :, :, None, :] - cs[:, :, None, :, :], -jnp.inf))
    y_diag = jnp.einsum("bcijh,bcjhp->bcihp", jnp.einsum("bcihn,bcjhn->bcijh", cc, bc) * seg, xdt)
    states = jnp.einsum("bcjhn,bcjh,bcjhp->bchpn", bc, jnp.exp(cs[:, :, -1:, :] - cs), xdt)
    chunk_decay = jnp.exp(cs[:, :, -1, :])

    def step(s, inp):
        st, dec = inp
        return s * dec[:, :, None, None] + st, s

    s0 = jnp.zeros((bsz, H, SSM_HEAD_DIM, SSM_STATE), f32)
    _, s_in = lax.scan(step, s0, (jnp.moveaxis(states, 1, 0), jnp.moveaxis(chunk_decay, 1, 0)))
    s_in = jnp.moveaxis(s_in, 0, 1)
    y_off = jnp.einsum("bcihn,bchpn,bcih->bcihp", cc, s_in, jnp.exp(cs))
    y = (y_diag + y_off).reshape(bsz, T, H, SSM_HEAD_DIM) + xs * d_skip.astype(f32)[:, None]
    y = y.reshape(bsz, T, BRANCH_WIDTH) * jax.nn.silu(z.astype(f32))
    return _rmsnorm(y, norm_w)

def _gdn_mixer(qkv, z, beta_raw, decay_raw, conv_w, a_log, dt_bias, norm_w):
    f32 = jnp.float32
    bsz, T, _ = qkv.shape
    L, H, dh = GDN_CHUNK, GDN_HEADS, GDN_HEAD_DIM
    nc = T // L
    qkv = jax.nn.silu(_causal_dwconv(qkv, conv_w)).astype(f32)
    q, k, v = [t.reshape(bsz, T, H, dh) for t in _split(qkv, (BRANCH_WIDTH,) * 3)]
    q = _l2norm(q) * (dh ** -0.5)
    k = _l2norm(k)
    beta = jax.nn.sigmoid(beta_raw.astype(f32))
    g = -jnp.exp(a_log.astype(f32)) * jax.nn.softplus(decay_raw.astype(f32) + dt_bias.astype(f32))

    def chunks(t):
        return jnp.moveaxis(t.reshape(bsz, nc, L, H, -1), 3, 1)

    q, k, v = chunks(q), chunks(k), chunks(v)
    beta = chunks(beta[..., None])[..., 0]
    gc = jnp.cumsum(chunks(g[..., None])[..., 0], axis=-1)
    incl = jnp.tril(jnp.ones((L, L), bool))
    strict = jnp.tril(jnp.ones((L, L), bool), k=-1)
    decay = jnp.exp(jnp.where(incl, gc[..., :, None] - gc[..., None, :], -jnp.inf))
    kb = k * beta[..., None]
    m = jnp.where(strict, jnp.einsum("bhcid,bhcjd->bhcij", kb, k) * decay, 0.0)
    rhs = jnp.concatenate([v * beta[..., None], kb * jnp.exp(gc)[..., None]], axis=-1)
    sol = lax.linalg.triangular_solve(m + jnp.eye(L, dtype=f32), rhs, left_side=True,
                                      lower=True, unit_diagonal=True)
    u, w = sol[..., :dh], sol[..., dh:]
    attn = jnp.einsum("bhcid,bhcjd->bhcij", q, k) * decay
    qg = q * jnp.exp(gc)[..., None]
    kd = k * jnp.exp(gc[..., -1:] - gc)[..., None]
    dec = jnp.exp(gc[..., -1])

    def step(s, inp):
        qg_c, kd_c, u_c, w_c, a_c, d_c = inp
        v_new = u_c - w_c @ s
        o = qg_c @ s + a_c @ v_new
        s = s * d_c[..., None, None] + jnp.swapaxes(kd_c, -1, -2) @ v_new
        return s, o

    s0 = jnp.zeros((bsz, H, dh, dh), f32)
    _, o = lax.scan(step, s0, tuple(jnp.moveaxis(t, 2, 0) for t in (qg, kd, u, w, attn, dec)))
    o = o.transpose(1, 0, 3, 2, 4).reshape(bsz, T, H, dh)
    o = _rmsnorm(o, norm_w) * jax.nn.silu(z.astype(f32).reshape(bsz, T, H, dh))
    return o.reshape(bsz, T, BRANCH_WIDTH)

def _gla_mixer(q, k, v, r, gate_low, w_gate, b_gate, norm_w):
    f32 = jnp.float32
    bsz, T, _ = q.shape
    L, H, dk, dv = GLA_CHUNK, GLA_HEADS, GLA_KEY_DIM, GLA_VAL_DIM
    nc = T // L
    log_a = jax.nn.log_sigmoid((gate_low @ w_gate + b_gate).astype(f32)) / GLA_GATE_TAU

    def chunks(t, d):
        return jnp.moveaxis(t.astype(f32).reshape(bsz, nc, L, H, d), 3, 1)

    q = chunks(q, dk) * (dk ** -0.5)
    k = chunks(k, dk)
    v = chunks(v, dv)
    G = jnp.cumsum(chunks(log_a, dk), axis=3)
    incl = jnp.tril(jnp.ones((L, L), bool))[:, :, None]
    decay = jnp.exp(jnp.where(incl, G[..., :, None, :] - G[..., None, :, :], -jnp.inf))
    attn = jnp.einsum("bhcid,bhcjd,bhcijd->bhcij", q, k, decay)
    o_intra = jnp.einsum("bhcij,bhcjv->bhciv", attn, v)
    qg = q * jnp.exp(G)
    kd = k * jnp.exp(G[..., -1:, :] - G)
    dec = jnp.exp(G[..., -1, :])

    def step(s, inp):
        qg_c, kd_c, v_c, d_c = inp
        o = qg_c @ s
        s = s * d_c[..., :, None] + jnp.swapaxes(kd_c, -1, -2) @ v_c
        return s, o

    s0 = jnp.zeros((bsz, H, dk, dv), f32)
    _, o_inter = lax.scan(step, s0, tuple(jnp.moveaxis(t, 2, 0) for t in (qg, kd, v, dec)))
    o = o_intra + jnp.moveaxis(o_inter, 0, 2)
    o = jnp.moveaxis(o, 1, 3).reshape(bsz, T, H, dv)
    o = _rmsnorm(o, norm_w) * jax.nn.silu(r.astype(f32).reshape(bsz, T, H, dv))
    return o.reshape(bsz, T, BRANCH_WIDTH)

def _rglru_mixer(xb, gate_b, conv_w, conv_b, w_a, b_a, w_x, b_x, lam):
    f32 = jnp.float32
    bsz, T, _ = xb.shape
    xc = _causal_dwconv(xb, conv_w, conv_b).astype(f32)
    xblk = xc.reshape(bsz, T, LRU_BLOCKS, LRU_BLOCK_DIM)
    gate_r = jax.nn.sigmoid(jnp.einsum("btnd,nde->btne", xblk, w_a.astype(f32)).reshape(bsz, T, BRANCH_WIDTH) + b_a.astype(f32))
    gate_i = jax.nn.sigmoid(jnp.einsum("btnd,nde->btne", xblk, w_x.astype(f32)).reshape(bsz, T, BRANCH_WIDTH) + b_x.astype(f32))
    log_a = -LRU_C * gate_r * jax.nn.softplus(-lam.astype(f32))
    a = jnp.exp(log_a)
    u = jnp.sqrt(-jnp.expm1(2.0 * log_a)) * (gate_i * xc)

    def combine(left, right):
        a_l, h_l = left
        a_r, h_r = right
        return a_l * a_r, a_r * h_l + h_r

    _, h = lax.associative_scan(combine, (a, u), axis=1)
    return h * jax.nn.gelu(gate_b.astype(f32))

def _peer_ffn(h, w_q, sub_keys, u_tab, v_tab):
    f32 = jnp.float32
    bsz, T, D = h.shape
    n_tok = bsz * T
    tok = h.reshape(n_tok, D)
    q = (tok @ w_q).reshape(n_tok, PEER_HEADS, 2, PEER_HALF_DIM)
    s = jnp.einsum("thpd,hpkd->thpk", q, sub_keys).astype(f32)
    s1, i1 = lax.top_k(s[:, :, 0], PEER_TOPK)
    s2, i2 = lax.top_k(s[:, :, 1], PEER_TOPK)
    n_cand = PEER_TOPK * PEER_TOPK
    cand_s = (s1[..., :, None] + s2[..., None, :]).reshape(n_tok, PEER_HEADS, n_cand)
    cand_i = (i1[..., :, None] * PEER_N_KEYS + i2[..., None, :]).reshape(n_tok, PEER_HEADS, n_cand)
    top_s, pos = lax.top_k(cand_s, PEER_TOPK)
    idx = jnp.take_along_axis(cand_i, pos, axis=-1)
    gate = jax.nn.softmax(top_s, axis=-1)
    nblk = n_tok // PEER_TOKEN_BLOCK
    k_all = PEER_HEADS * PEER_TOPK

    def expert_block(args):
        x_b, i_b, g_b = args
        act = jax.nn.gelu(jnp.einsum("td,tkd->tk", x_b, u_tab[i_b]).astype(f32)) * g_b
        return jnp.einsum("tk,tkd->td", act.astype(x_b.dtype), v_tab[i_b])

    out = lax.map(expert_block, (tok.reshape(nblk, PEER_TOKEN_BLOCK, D),
                                 idx.reshape(nblk, PEER_TOKEN_BLOCK, k_all),
                                 gate.reshape(nblk, PEER_TOKEN_BLOCK, k_all)))
    return out.reshape(bsz, T, D)

def setup_inputs(seed: int = 0) -> dict:
    key = jax.random.key(seed)
    keys = iter(jax.random.split(key, 48))
    f32 = jnp.float32
    L, D = DEPTH, D_MODEL

    def nrm(shape, scale):
        return jax.random.normal(next(keys), shape, f32) * scale

    def gain(shape):
        return 1.0 + nrm(shape, 0.02)

    def unif(shape, lo, hi):
        return jax.random.uniform(next(keys), shape, f32, lo, hi)

    def dt_bias(shape):
        dt = jnp.exp(unif(shape, math.log(1e-3), math.log(1e-1)))
        return dt + jnp.log(-jnp.expm1(-dt))

    a_c = unif((L, BRANCH_WIDTH), 0.9, 0.999)
    s = a_c ** (1.0 / LRU_C)
    return {
        "x": nrm((BATCH, SEQ, D), 1.0),
        "c": nrm((BATCH, D), 1.0),
        "w_ada": nrm((L, D, 6 * D), D ** -0.5),
        "b_ada": nrm((L, 6 * D), 0.02),
        "norm_mix_w": gain((L, D)),
        "norm_ffn_w": gain((L, D)),
        "w_in": nrm((L, D, D_IN), D ** -0.5),
        "ssm_conv_w": nrm((L, CONV_WIDTH, SSM_XBC), CONV_WIDTH ** -0.5),
        "ssm_conv_b": nrm((L, SSM_XBC), 0.02),
        "ssm_dt_bias": dt_bias((L, SSM_HEADS)),
        "ssm_a_log": jnp.log(unif((L, SSM_HEADS), 1.0, 16.0)),
        "ssm_d": gain((L, SSM_HEADS)),
        "ssm_norm_w": gain((L, BRANCH_WIDTH)),
        "gdn_conv_w": nrm((L, CONV_WIDTH, 3 * BRANCH_WIDTH), CONV_WIDTH ** -0.5),
        "gdn_a_log": jnp.log(unif((L, GDN_HEADS), 1.0, 16.0)),
        "gdn_dt_bias": dt_bias((L, GDN_HEADS)),
        "gdn_norm_w": gain((L, GDN_HEAD_DIM)),
        "gla_w_gate": nrm((L, GLA_GATE_RANK, GLA_HEADS * GLA_KEY_DIM), GLA_GATE_RANK ** -0.5),
        "gla_b_gate": nrm((L, GLA_HEADS * GLA_KEY_DIM), 0.02),
        "gla_norm_w": gain((L, GLA_VAL_DIM)),
        "lru_conv_w": nrm((L, CONV_WIDTH, BRANCH_WIDTH), CONV_WIDTH ** -0.5),
        "lru_conv_b": nrm((L, BRANCH_WIDTH), 0.02),
        "lru_w_a": nrm((L, LRU_BLOCKS, LRU_BLOCK_DIM, LRU_BLOCK_DIM), LRU_BLOCK_DIM ** -0.5),
        "lru_b_a": nrm((L, BRANCH_WIDTH), 0.02),
        "lru_w_x": nrm((L, LRU_BLOCKS, LRU_BLOCK_DIM, LRU_BLOCK_DIM), LRU_BLOCK_DIM ** -0.5),
        "lru_b_x": nrm((L, BRANCH_WIDTH), 0.02),
        "lru_lambda": jnp.log(s) - jnp.log1p(-s),
        "w_branch": nrm((L, N_BRANCHES, BRANCH_WIDTH, D), BRANCH_WIDTH ** -0.5),
        "w_out": nrm((L, D, D), D ** -0.5),
        "peer_w_q": nrm((L, D, PEER_HEADS * PEER_QUERY_DIM), D ** -0.5),
        "peer_sub_keys": nrm((L, PEER_HEADS, 2, PEER_N_KEYS, PEER_HALF_DIM), PEER_HALF_DIM ** -0.5),
        "peer_u": nrm((L, PEER_N_EXPERTS, D), D ** -0.5),
        "peer_v": nrm((L, PEER_N_EXPERTS, D), PEER_HEADS ** -0.5),
        "final_norm_w": gain((D,)),
    }

def reference(x, c, w_ada, b_ada, norm_mix_w, norm_ffn_w, w_in, ssm_conv_w, ssm_conv_b,
              ssm_dt_bias, ssm_a_log, ssm_d, ssm_norm_w, gdn_conv_w, gdn_a_log, gdn_dt_bias,
              gdn_norm_w, gla_w_gate, gla_b_gate, gla_norm_w, lru_conv_w, lru_conv_b, lru_w_a,
              lru_b_a, lru_w_x, lru_b_x, lru_lambda, w_branch, w_out, peer_w_q, peer_sub_keys,
              peer_u, peer_v, final_norm_w):
    bsz, T, _ = x.shape
    c_act = jax.nn.silu(c)
    for l in range(DEPTH):
        mod = c_act @ w_ada[l] + b_ada[l]
        sh1, sc1, g1, sh2, sc2, g2 = jnp.split(mod[:, None, :], 6, axis=-1)
        h = _rmsnorm(x, norm_mix_w[l]) * (1.0 + sc1) + sh1
        proj = h @ w_in[l]
        (ssm_z, ssm_xbc, ssm_dt, gdn_qkv, gdn_z, gdn_beta, gdn_decay, gla_q, gla_k, gla_v,
         gla_r, gla_low, lru_x, lru_gate, merge_logits) = _split(proj, IN_SIZES)
        y_ssm = _ssd_mixer(ssm_z, ssm_xbc, ssm_dt, ssm_conv_w[l], ssm_conv_b[l], ssm_dt_bias[l],
                           ssm_a_log[l], ssm_d[l], ssm_norm_w[l])
        y_gdn = _gdn_mixer(gdn_qkv, gdn_z, gdn_beta, gdn_decay, gdn_conv_w[l], gdn_a_log[l],
                           gdn_dt_bias[l], gdn_norm_w[l])
        y_gla = _gla_mixer(gla_q, gla_k, gla_v, gla_r, gla_low, gla_w_gate[l], gla_b_gate[l],
                           gla_norm_w[l])
        y_lru = _rglru_mixer(lru_x, lru_gate, lru_conv_w[l], lru_conv_b[l], lru_w_a[l], lru_b_a[l],
                             lru_w_x[l], lru_b_x[l], lru_lambda[l])
        branches = (y_ssm, y_gdn, y_gla, y_lru)
        gates = jax.nn.sigmoid(merge_logits.astype(jnp.float32)).reshape(bsz, T, N_BRANCHES, D_MODEL)
        merged = sum(gates[:, :, i] * (branches[i].astype(x.dtype) @ w_branch[l, i])
                     for i in range(N_BRANCHES))
        x = x + g1 * (merged.astype(x.dtype) @ w_out[l])
        h2 = _rmsnorm(x, norm_ffn_w[l]) * (1.0 + sc2) + sh2
        x = x + g2 * _peer_ffn(h2, peer_w_q[l], peer_sub_keys[l], peer_u[l], peer_v[l]).astype(x.dtype)
    return _rmsnorm(x, final_norm_w)


_drawn_inputs = setup_inputs


def setup_inputs(seed=0):
    import zlib

    import numpy as np

    out = dict(_drawn_inputs(seed))
    spreads = {}
    factors = {'norm_ffn_w': 21.923,
     'ssm_conv_b': 5.23,
     'ssm_d': 115.113,
     'ssm_norm_w': 52.856,
     'gdn_norm_w': 66.008,
     'gla_b_gate': 6.942,
     'gla_norm_w': 59.22,
     'lru_b_a': 107.802,
     'lru_b_x': 51.858,
     'final_norm_w': 22.944,
     'lru_conv_b': 11.253}
    for name, (base, spread) in spreads.items():
        noise = np.random.default_rng([zlib.crc32(name.encode()), seed]).standard_normal(out[name].shape)
        drawn = base * np.exp(spread * noise) if base else spread * noise
        out[name] = jnp.asarray(drawn.astype(out[name].dtype))
    for name, factor in factors.items():
        out[name] = (out[name] * factor).astype(out[name].dtype)
    return out
```

```python
from contextlib import ExitStack

import numpy as np
import concourse.bass as bass
from concourse import mybir

F32 = mybir.dt.float32
U32 = mybir.dt.uint32
ALU = mybir.AluOpType
ACT = mybir.ActivationFunctionType
AX = mybir.AxisListType

P = 128
DEPTH, D, T = 2, 1024, 512
KD = D // P
NC = T // P
WIDTH = D // 2
NW = WIDTH // P
EPS = 1e-6
SSM_H, SSM_P, SSM_G = 8, 64, 2
GDN_H, GLA_H, GLA_K = 4, 4, 64
NHEAD = SSM_H + GDN_H
GLA_TAU, LRU_C = 16.0, 8.0
RANK = 16
PEER_H, KEYS, TOPK = 8, 128, 16
NHK = PEER_H * TOPK
QT = PEER_H * 2

XBC, QKV, LRUX, GQK, LRUG = 6, 12, 4, 4, 4
T_SSM, T_GDN, T_LRUX, T_GLAQ, T_LRUG = 0, 6, 18, 22, 26
N_SILU, N_CONV, N_CH = 18, 22, 30
N_ZT, N_MERGE = 16, 32
SMALL = 32

_V = [("b_ada", 48), ("nmix", 8), ("nffn", 8), ("taps", N_CONV * 4), ("cbias", N_CONV), ("gla_b", 2),
      ("lru_ba", 4), ("lru_bx", 4), ("lru_lam", 4), ("ssm_d", 4), ("ssm_nw", 4), ("gdn_nw", 1),
      ("gla_nw", 1), ("dt_bias", NHEAD), ("a_log", NHEAD)]
V, NV = {}, 0
for _n, _w in _V:
    V[_n] = (NV, NV + _w)
    NV += _w

LEVELS = [2, 4, 8, 16, 32, 64]
CONSTS = ["ident", "ones", "tri", "neg", "iota", "lv1"] + [f"lv{s}" for s in LEVELS]
C_OFF = {n: i * P for i, n in enumerate(CONSTS)}
C_RESET = len(CONSTS) * P
C_EPS = C_RESET + T
C_J16 = C_EPS + 2
NCONST = C_J16 + 256


def constants():
    j, i = np.arange(P)[:, None], np.arange(P)[None, :]
    c = np.zeros((P, NCONST), np.float32)
    c[:, 0:P] = np.eye(P)
    c[:, C_OFF["ones"]:][:, :P] = 1
    c[:, C_OFF["tri"]:][:, :P] = j <= i
    c[:, C_OFF["neg"]:][:, :P] = np.where(j <= i, 0, -1e30)
    c[:, C_OFF["iota"]:][:, :P] = i
    for s in [1] + LEVELS:
        c[:, C_OFF[f"lv{s}"]:][:, :P] = (i // (2 * s) == j // (2 * s)) & (i // s % 2 == 1) & (j // s % 2 == 0)
    c[:, C_RESET:C_RESET + T] = np.arange(T) % P != 0
    c[:, C_EPS] = EPS
    c[:, C_J16:] = np.arange(256) % 16
    rows = 16
    sel = np.zeros((rows, rows, P), np.float32)
    sel[np.arange(rows), np.arange(rows)] = 1
    return c, sel.reshape(rows, rows * P)


def build(nc, a, out, debug=None):
    debug = debug or {}
    made, names, numbers = {}, [], []

    def S(name):
        if name not in made:
            made[name] = nc.alloc_semaphore(name, num=numbers.pop(0)) if numbers else nc.alloc_semaphore(name)
        return made[name]

    def clear_since(before):
        done = [n for n in made if n not in before]
        nums = sorted(made[n].num for n in done)
        assert nums == list(range(nums[0], nums[0] + len(nums)))
        nc.all_engine_barrier(sems_to_clear=range(nums[0], nums[-1] + 1))
        for n in done:
            nc.release_semaphore(made.pop(n))
        numbers[:] = sorted(numbers + nums)

    def row(t, i):
        return t[:, bass.ds(i, 1), :].rearrange("p a n -> p (a n)")

    g_dram = nc.dram_tensor("routing", (P, KEYS, T), F32, kind="Internal").ap()

    ctx = ExitStack()
    with ctx:
        def sb(stack, name, shape, dt=F32):
            names.append(name)
            return stack.enter_context(nc.sbuf_tensor(f"{name}_{len(names)}", shape, dt))

        bank = [ctx.enter_context(nc.psum_tensor(f"bank{i}", [P, T], F32)) for i in range(8)]
        xT = sb(ctx, "xT", [P, KD, T])
        cst = sb(ctx, "cst", [P, NCONST])
        cact = sb(ctx, "cact", [P, KD])
        vec = sb(ctx, "vec", [P, NV])
        fnw = sb(ctx, "fnw", [P, KD])
        mod = sb(ctx, "mod", [P, 6 * KD])
        gain = sb(ctx, "gain", [P, 2 * KD])
        rinv = sb(ctx, "rinv", [P, T])

        def C(name, n=P):
            return cst[0:n, C_OFF[name]:C_OFF[name] + n]

        def v(name, i=0, n=None):
            lo, hi = V[name]
            return vec[:, lo + i:(lo + i + n) if n else hi]

        eps = cst[:, C_EPS:C_EPS + 1]
        zero = cst[:, C_EPS + 1:C_EPS + 2]

        with nc.Block() as block:
            @block.sync
            def _(sp):
                for dst, src in ((xT[:], a["x"]), (cst[:], a["consts"]), (cact[:], a["c"]), (fnw[:], a["fnw"])):
                    sp.dma_start(dst, src).then_inc(S("start_loaded"), 16)

            @block.scalar
            def _(act):
                act.wait_ge(S("start_loaded"), 64)
                nc.scalar.activation(cact[:], cact[:], ACT.Silu, bias=zero).then_inc(S("c_silu"), 1)
                act.wait_ge(S("c_silu"), 1)

        def norm(hT, tag, g=None, shift=None):
            sq, ss, mm, rt, rc, nm, dn = (S(f"{tag}_{x}") for x in ("sq", "ss", "mm", "root", "rinv", "scaled", "done"))
            with nc.Block() as block:
                @block.scalar
                def _(act):
                    for k in range(KD):
                        nc.scalar.activation(hT[:, k, :], xT[:, k, :], ACT.Square, bias=zero).then_inc(sq, 1)
                    act.wait_ge(mm, 1)
                    nc.scalar.activation(rinv[:], bank[0][:], ACT.Sqrt, bias=eps, scale=1.0 / D).then_inc(rt, 1)
                    for k in range(KD):
                        act.wait_ge(nm, k + 1)
                        if shift is None:
                            nc.scalar.activation(hT[:, k, :], hT[:, k, :], ACT.Identity, bias=zero,
                                                 scale=g[:, k:k + 1]).then_inc(dn, 1)
                        else:
                            nc.scalar.activation(hT[:, k, :], hT[:, k, :], ACT.Identity, bias=shift[:, k:k + 1],
                                                 scale=g[:, k:k + 1]).then_inc(dn, 1)
                    act.wait_ge(dn, KD)

                @block.tensor
                def _(pe):
                    for k in range(KD):
                        pe.wait_ge(sq, k + 1)
                        last = nc.tensor.matmul(bank[0][:], C("ones"), hT[:, k, :], start=k == 0, stop=k == KD - 1)
                    last.then_inc(mm, 1)

                @block.vector
                def _(dve):
                    dve.wait_ge(rt, 1)
                    nc.vector.reciprocal(rinv[:], rinv[:]).then_inc(rc, 1)
                    dve.wait_ge(rc, 1)
                    for k in range(KD):
                        nc.vector.tensor_tensor(hT[:, k, :], xT[:, k, :], rinv[:], ALU.mult).then_inc(nm, 1)

        with nc.Fori(0, DEPTH) as layer:
            outside = set(made)

            def lay(name):
                t = a[name]
                dims = " ".join(f"d{i}" for i in range(len(t.shape)))
                rest = dims[3:]
                return t[bass.ds(layer, 1)].rearrange(f"{dims} -> (d0 {rest.split(' ')[0]}) {' '.join(rest.split(' ')[1:])}")

            with ExitStack() as ph, nc.Block() as block:
                wa = [sb(ph, f"wa{u}", [P, 4, KD, P]) for u in range(2)]
                ada = lay("w_ada")

                @block.sync
                def _(sp):
                    sp.sem_inc(S("ada_free"), 2)
                    sp.dma_start(vec[:], lay("vecs")).then_inc(S("vec_loaded"), 16)
                    with sp.Fori(0, 6) as i:
                        for u in range(2):
                            sp.wait_ge(S("ada_free"), 2 * i + u + 1)
                            sp.dma_start(wa[u][:].rearrange("p a k n -> p (a k n)"),
                                         ada[bass.ds(2 * i + u, 1)].rearrange("g p n -> (g p) n")
                                         ).then_inc(S(f"ada_loaded{u}"), 16)

                @block.tensor
                def _(pe):
                    pe.sem_inc(S("ada_bank_free"), 2)
                    with pe.Fori(0, 6) as i:
                        for u in range(2):
                            pe.wait_ge(S(f"ada_loaded{u}"), 16 * i + 16)
                            pe.wait_ge(S("ada_bank_free"), 2 * i + u + 1)
                            for m in range(4):
                                for k in range(KD):
                                    last = nc.tensor.matmul(bank[u][:, m:m + 1], wa[u][:, m, k, :], cact[:, k:k + 1],
                                                            start=k == 0, stop=k == KD - 1)
                            last.then_inc(S("ada_mm"), 1)

                @block.vector
                def _(dve):
                    dve.wait_ge(S("vec_loaded"), 16)
                    with dve.Fori(0, 6) as i:
                        for u in range(2):
                            dve.wait_ge(S("ada_mm"), 2 * i + u + 1)
                            nc.vector.tensor_tensor(mod[:, bass.ds(8 * i + 4 * u, 4)], bank[u][:, 0:4],
                                                    vec[:, bass.ds(8 * i + 4 * u, 4)], ALU.add).then_inc(S("ada_bank_free"), 1)
                            dve.wait_ge(S("ada_bank_free"), 2 * i + u + 3)
                            dve.sem_inc(S("ada_free"), 1)
                    for n, (sc, w) in enumerate(((1, "nmix"), (4, "nffn"))):
                        nc.vector.scalar_tensor_tensor(gain[:, n * KD:(n + 1) * KD], mod[:, sc * KD:(sc + 1) * KD], 1.0,
                                                       v(w), ALU.add, ALU.mult).then_inc(S("gain_done"), 1)
                    dve.wait_ge(S("gain_done"), 2)

            mix = ExitStack()
            hT = sb(mix, "hT", [P, KD, T])
            norm(hT, "nmix", gain[:, 0:KD], mod[:, 0:KD])
            ch = sb(mix, "ch", [P, N_CH, T])
            zt = sb(mix, "zt", [P, 4, NC, WIDTH])
            wsm = sb(mix, "wsm", [P, KD, SMALL])
            small = sb(mix, "small", [P, NC, 16])
            low = sb(mix, "low", [RANK, T])

            with ExitStack() as ph, nc.Block() as block:
                wc = [sb(ph, f"wc{u}", [P, KD, P]) for u in range(2)]
                wz = sb(ph, "wz", [P, 4, KD, P])
                raw = [sb(ph, f"raw{u}", [P, T + 3]) for u in range(2)]
                y = [sb(ph, f"y{u}", [P, T]) for u in range(2)]
                w_ch, w_zt = lay("w_ch"), lay("w_zt")

                @block.sync
                def _(sp):
                    sp.sem_inc(S("wc_free"), 2)
                    sp.sem_inc(S("wz_free"), 1)
                    sp.dma_start(wsm[:], lay("w_small")).then_inc(S("wsm_loaded"), 16)
                    with sp.Fori(0, N_CH // 2) as i:
                        for u in range(2):
                            sp.wait_ge(S("wc_free"), 2 * i + u + 1)
                            sp.dma_start(wc[u][:].rearrange("p k n -> p (k n)"),
                                         w_ch[bass.ds(2 * i + u, 1)].rearrange("g p n -> (g p) n")
                                         ).then_inc(S(f"wc_loaded{u}"), 16)
                    with sp.Fori(0, 4) as i:
                        sp.wait_ge(S("wz_free"), i + 1)
                        sp.dma_start(wz[:].rearrange("p a k n -> p (a k n)"),
                                     w_zt[bass.ds(i, 1)].rearrange("g p n -> (g p) n")).then_inc(S("wz_loaded"), 16)

                @block.tensor
                def _(pe):
                    pe.sem_inc(S("ch_bank_free"), 2)
                    with pe.Fori(0, N_CH // 2) as i:
                        for u in range(2):
                            pe.wait_ge(S(f"wc_loaded{u}"), 16 * i + 16)
                            pe.wait_ge(S("ch_bank_free"), 2 * i + u + 1)
                            for k in range(KD):
                                last = nc.tensor.matmul(bank[u][:], wc[u][:, k, :], hT[:, k, :], start=k == 0, stop=k == KD - 1)
                            last.then_inc(S("ch_mm"), 1)
                    pe.wait_ge(S("wsm_loaded"), 16)
                    for t in range(NC):
                        for k in range(KD):
                            last = nc.tensor.matmul(bank[6][:, t * 16:t * 16 + 16], hT[:, k, t * P:(t + 1) * P],
                                                    wsm[:, k, 0:16], start=k == 0, stop=k == KD - 1)
                    last.then_inc(S("small_mm"), 1)
                    for k in range(KD):
                        last = nc.tensor.matmul(bank[7][0:RANK, :], wsm[:, k, 16:32], hT[:, k, :], start=k == 0, stop=k == KD - 1)
                    last.then_inc(S("low_mm"), 1)
                    pe.sem_inc(S("zt_bank_free"), 4)
                    with pe.Fori(0, 4) as i:
                        pe.wait_ge(S("wz_loaded"), 16 * i + 16)
                        for t in range(NC):
                            pe.wait_ge(S("zt_bank_free"), 4 * i + t + 1)
                            for k in range(KD):
                                last = nc.tensor.matmul(bank[2 + t][:], hT[:, k, t * P:(t + 1) * P], wz[:, :, k, :],
                                                        start=k == 0, stop=k == KD - 1)
                            last.then_inc(S("zt_mm"), 1)

                @block.scalar
                def _(act):
                    act.sem_inc(S("raw_free"), 2)

                    def evacuate(n, u):
                        act.wait_ge(S("ch_mm"), n + 1)
                        act.wait_ge(S("raw_free"), n + 1)
                        nc.scalar.activation(raw[u][:, 3:], bank[u][:], ACT.Copy).then_inc(S("ch_bank_free"), 1)
                        act.wait_ge(S("ch_bank_free"), n + 3)
                        act.sem_inc(S("wc_free"), 1)
                        act.sem_inc(S("raw_ready"), 1)

                    with act.Fori(0, N_SILU // 2) as i:
                        for u in range(2):
                            evacuate(2 * i + u, u)
                        for u in range(2):
                            act.wait_ge(S("conv_done"), 2 * i + u + 1)
                            nc.scalar.activation(row(ch, 2 * i + u), y[u][:], ACT.Silu, bias=zero).then_inc(S("y_free"), 1)
                    with act.Fori(N_SILU // 2, N_CONV // 2) as i:
                        for u in range(2):
                            evacuate(2 * i + u, u)
                    with act.Fori(N_CONV // 2, N_CH // 2) as i:
                        for u in range(2):
                            act.wait_ge(S("ch_mm"), 2 * i + u + 1)
                            nc.scalar.activation(row(ch, 2 * i + u), bank[u][:], ACT.Copy).then_inc(S("ch_bank_free"), 1)
                            act.wait_ge(S("ch_bank_free"), 2 * i + u + 3)
                            act.sem_inc(S("wc_free"), 1)
                    act.wait_ge(S("low_mm"), 1)
                    nc.scalar.activation(low[:], bank[7][0:RANK, :], ACT.Copy).then_inc(S("low_done"), 1)
                    with act.Fori(0, 4) as i:
                        for t in range(NC):
                            act.wait_ge(S("zt_mm"), 4 * i + t + 1)
                            nc.scalar.activation(zt[:, bass.ds(i, 1), t, :].rearrange("p a n -> p (a n)"), bank[2 + t][:], ACT.Copy
                                                 ).then_inc(S("zt_bank_free"), 1)
                        act.wait_ge(S("zt_bank_free"), 4 * i + 8)
                        act.sem_inc(S("wz_free"), 1)

                @block.vector
                def _(dve):
                    for u in range(2):
                        nc.vector.memset(raw[u][:, 0:3], 0.0).then_inc(S("pad_zero"), 1)
                    dve.wait_ge(S("pad_zero"), 2)
                    dve.sem_inc(S("y_free"), 2)
                    first, bias = V["taps"][0], V["cbias"][0]

                    def conv(n, u, dst, reuse):
                        dve.wait_ge(S("raw_ready"), n + 1)
                        if reuse:
                            dve.wait_ge(S("y_free"), n + 1)
                        nc.vector.tensor_scalar(dst, raw[u][:, 3:], vec[:, bass.ds(first + 4 * n + 3, 1)],
                                                vec[:, bass.ds(bias + n, 1)], ALU.mult, ALU.add).then_inc(S("tap_done"), 1)
                        for j in range(3):
                            dve.wait_ge(S("tap_done"), 3 * n + j + 1)
                            ins = nc.vector.scalar_tensor_tensor(dst, raw[u][:, j:j + T], vec[:, bass.ds(first + 4 * n + j, 1)],
                                                                 dst, ALU.mult, ALU.add)
                            ins.then_inc(S("tap_done") if j < 2 else S("conv_done"), 1)
                        dve.wait_ge(S("conv_done"), n + 1)
                        dve.sem_inc(S("raw_free"), 1)

                    with dve.Fori(0, N_SILU // 2) as i:
                        for u in range(2):
                            conv(2 * i + u, u, y[u][:], True)
                    with dve.Fori(N_SILU // 2, N_CONV // 2) as i:
                        for u in range(2):
                            conv(2 * i + u, u, row(ch, 2 * i + u), False)
                    dve.wait_ge(S("small_mm"), 1)
                    nc.vector.tensor_copy(small[:].rearrange("p t n -> p (t n)"), bank[6][:, 0:NC * 16]).then_inc(S("small_done"), 1)

            clear_since(outside)

            sm = ExitStack()
            dec = sb(sm, "dec", [P, NC, 16])
            dts = sb(sm, "dts", [P, NC * NHEAD + 4])
            ecol = sb(sm, "ecol", [P, NC * NHEAD])
            etot = sb(sm, "etot", [P, NC * NHEAD])
            rows = sb(sm, "rows", [16, T])
            sel = sb(sm, "sel", [16, 16 * P])
            NS = NC * NHEAD
            with ExitStack() as ph, nc.Block() as block:
                t = [sb(ph, f"sp{i}", [P, NS + 4]) for i in range(7)]
                x, nab, z, w, ln, one, den = (q[:] for q in t)
                ea = sb(ph, "ea", [P, NHEAD])
                da = sb(ph, "da", [P, NS])
                per_head = [P, NC, NHEAD]

                @block.sync
                def _(sp):
                    sp.dma_start(sel[:], a["sel"]).then_inc(S("sel_loaded"), 16)
                    sp.wait_ge(S("sel_loaded"), 16)

                @block.vector
                def _(dve):
                    nc.vector.tensor_tensor(x[:, 0:NS].rearrange("p (t h) -> p t h", t=NC), small[:, :, 0:NHEAD],
                                            v("dt_bias").unsqueeze(1).to_broadcast(per_head), ALU.add).then_inc(S("sp_x"), 1)
                    nc.vector.tensor_scalar(x[:, NS:], v("lru_lam"), -1.0, None, ALU.mult).then_inc(S("sp_x"), 1)
                    dve.wait_ge(S("sp_x"), 2)
                    nc.vector.scalar_tensor_tensor(nab, x, -1.0, x, ALU.mult, ALU.min).then_inc(S("sp_nab"), 1)
                    dve.wait_ge(S("sp_z"), 1)
                    nc.vector.tensor_scalar(w, z, 1.0, None, ALU.add).then_inc(S("sp_w"), 1)
                    dve.wait_ge(S("sp_w"), 1)
                    nc.vector.tensor_scalar(one, w, 1.0, None, ALU.is_equal).then_inc(S("sp_d"), 1)
                    dve.wait_ge(S("sp_d"), 1)
                    nc.vector.scalar_tensor_tensor(den, w, -1.0, one, ALU.add, ALU.add).then_inc(S("sp_d"), 1)
                    dve.wait_ge(S("sp_d"), 2)
                    nc.vector.reciprocal(den, den).then_inc(S("sp_d"), 1)
                    dve.wait_ge(S("sp_ln"), 1)
                    nc.vector.tensor_tensor(ln, ln, one, ALU.add).then_inc(S("sp_d"), 1)
                    dve.wait_ge(S("sp_d"), 4)
                    nc.vector.tensor_tensor(ln, ln, den, ALU.mult).then_inc(S("sp_d"), 1)
                    dve.wait_ge(S("sp_d"), 5)
                    nc.vector.tensor_tensor(ln, ln, z, ALU.mult).then_inc(S("sp_d"), 1)
                    dve.wait_ge(S("sp_d"), 6)
                    nc.vector.scalar_tensor_tensor(dts[:], x, 0.0, ln, ALU.max, ALU.add).then_inc(S("sp_d"), 1)
                    dve.wait_ge(S("sp_d"), 7)
                    dve.wait_ge(S("ea_done"), 1)
                    nc.vector.scalar_tensor_tensor(da[:].rearrange("p (t h) -> p t h", t=NC),
                                                   dts[:, 0:NS].rearrange("p (t h) -> p t h", t=NC), -1.0,
                                                   ea[:].unsqueeze(1).to_broadcast(per_head), ALU.mult, ALU.mult
                                                   ).then_inc(S("da_done"), 1)
                    dve.wait_ge(S("decay_mm"), 2)
                    nc.vector.tensor_copy(dec[:, :, 0:NHEAD], bank[0][:, 0:NS].rearrange("p (t h) -> p t h", t=NC)
                                          ).then_inc(S("dec_done"), 1)
                    dve.wait_ge(S("decay_mm"), 3)
                    nc.vector.tensor_copy(rows[:], bank[2][0:16, :]).then_inc(S("rows_done"), 1)
                    dve.wait_ge(S("rows_done"), 1)

                @block.scalar
                def _(act):
                    nc.scalar.activation(ea[:], v("a_log"), ACT.Exp, bias=zero).then_inc(S("ea_done"), 1)
                    act.wait_ge(S("sp_nab"), 1)
                    nc.scalar.activation(z, nab, ACT.Exp, bias=zero).then_inc(S("sp_z"), 1)
                    act.wait_ge(S("sp_w"), 1)
                    nc.scalar.activation(ln, w, ACT.Ln, bias=zero).then_inc(S("sp_ln"), 1)
                    act.wait_ge(S("decay_mm"), 2)
                    act.wait_ge(S("dec_done"), 1)
                    nc.scalar.activation(ecol[:], dec[:, :, 0:NHEAD], ACT.Exp, bias=zero).then_inc(S("ecol_done"), 1)
                    nc.scalar.activation(etot[:], bank[1][:, 0:NS], ACT.Exp, bias=zero).then_inc(S("ecol_done"), 1)
                    nc.scalar.activation(dec[:, :, NHEAD:16], small[:, :, NHEAD:16], ACT.Sigmoid, bias=zero).then_inc(S("beta_done"), 1)

                @block.tensor
                def _(pe):
                    pe.wait_ge(S("da_done"), 1)
                    nc.tensor.matmul(bank[0][:, 0:NS], C("tri"), da[:], start=True, stop=True).then_inc(S("decay_mm"), 1)
                    nc.tensor.matmul(bank[1][:, 0:NS], C("ones"), da[:], start=True, stop=True).then_inc(S("decay_mm"), 1)
                    pe.wait_ge(S("dec_done"), 1)
                    pe.wait_ge(S("beta_done"), 1)
                    for c in range(NC):
                        last = nc.tensor.transpose(bank[2][0:16, c * P:(c + 1) * P], dec[:, c, :], C("ident"))
                    last.then_inc(S("decay_mm"), 1)

            def decays(tmp, DT, first, n, tag, EG=None):
                def pe_part(pe):
                    for h in range(n):
                        if h >= 4:
                            pe.wait_ge(S(f"{tag}_bc_free"), h - 3)
                        nc.tensor.matmul(bank[4 + h % 4][:], sel[:, (first + h) * P:(first + h + 1) * P], rows[:],
                                         start=True, stop=True).then_inc(S(f"{tag}_bc"), 1)

                def dve_part(dve):
                    for h in range(n):
                        dve.wait_ge(S(f"{tag}_bc"), h + 1)
                        if EG is not None:
                            dve.wait_ge(S(f"{tag}_eg"), h + 1)
                        if h >= 2:
                            dve.wait_ge(S(f"{tag}_dt"), h - 1)
                        for c in range(NC):
                            last = nc.vector.scalar_tensor_tensor(tmp[h % 2][:, c * P:(c + 1) * P], bank[4 + h % 4][:, c * P:(c + 1) * P],
                                                                  dec[:, c, first + h:first + h + 1], C("neg"),
                                                                  ALU.subtract, ALU.add)
                        last.then_inc(S(f"{tag}_bc_free"), 1)

                def act_part(act):
                    for h in range(n):
                        if EG is not None:
                            act.wait_ge(S(f"{tag}_bc"), h + 1)
                            nc.scalar.activation(EG[:, h, :], bank[4 + h % 4][:], ACT.Exp, bias=zero).then_inc(S(f"{tag}_eg"), 1)
                        act.wait_ge(S(f"{tag}_bc_free"), h + 1)
                        nc.scalar.activation(DT[:, h, :], tmp[h % 2], ACT.Exp, bias=zero).then_inc(S(f"{tag}_dt"), 1)
                return pe_part, dve_part, act_part

            def finish(o, zi, groups, after_gate, nw, dst, tag):
                n = WIDTH // groups
                with ExitStack() as ph, nc.Block() as block:
                    sq = [sb(ph, f"sq{u}", [P, WIDTH]) for u in range(2)]
                    ms = sb(ph, "ms", [P, NC * groups])

                    @block.scalar
                    def _(act):
                        for c in range(NC):
                            nc.scalar.activation(zt[:, zi, c, :], zt[:, zi, c, :], ACT.Silu, bias=zero).then_inc(S(f"{tag}_sz"), 1)
                        act.wait_ge(S(f"{tag}_ms"), NC)
                        nc.scalar.activation(ms[:], ms[:], ACT.Sqrt, bias=eps, scale=1.0 / n).then_inc(S(f"{tag}_rms"), 1)
                        for m in range(NW):
                            act.wait_ge(S(f"{tag}_yt"), m + 1)
                            nc.scalar.activation(ch[:, dst + m, :], bank[m][:], ACT.Identity, bias=zero,
                                                 scale=nw[:, m:m + 1] if groups == 1 else nw[:, 0:1]).then_inc(S(f"{tag}_y"), 1)
                        act.wait_ge(S(f"{tag}_y"), NW)

                    @block.vector
                    def _(dve):
                        def gate(c):
                            dve.wait_ge(S(f"{tag}_sz"), c + 1)
                            nc.vector.tensor_tensor(o[:, c, :], o[:, c, :], zt[:, zi, c, :], ALU.mult).then_inc(S(f"{tag}_gated"), 1)

                        for c in range(NC):
                            if after_gate:
                                gate(c)
                                dve.wait_ge(S(f"{tag}_gated"), c + 1)
                            if c >= 2:
                                dve.wait_ge(S(f"{tag}_ms"), c - 1)
                            nc.vector.tensor_tensor(sq[c % 2][:], o[:, c, :], o[:, c, :], ALU.mult).then_inc(S(f"{tag}_sq"), 1)
                            if not after_gate:
                                dve.wait_ge(S(f"{tag}_sq"), c + 1)
                                gate(c)
                            dve.wait_ge(S(f"{tag}_sq"), c + 1)
                            nc.vector.tensor_reduce(ms[:, c * groups:(c + 1) * groups],
                                                    sq[c % 2][:].rearrange("p (g n) -> p g n", g=groups), AX.X, ALU.add
                                                    ).then_inc(S(f"{tag}_ms"), 1)
                        dve.wait_ge(S(f"{tag}_rms"), 1)
                        nc.vector.reciprocal(ms[:], ms[:]).then_inc(S(f"{tag}_rinv"), 1)
                        dve.wait_ge(S(f"{tag}_rinv"), 1)
                        dve.wait_ge(S(f"{tag}_gated"), NC)
                        for c in range(NC):
                            if groups == 1:
                                ins = nc.vector.tensor_scalar(o[:, c, :], o[:, c, :], ms[:, c:c + 1], None, ALU.mult)
                            else:
                                r = ms[:, c * groups:(c + 1) * groups].unsqueeze(2).to_broadcast([P, groups, n])
                                og = o[:, c, :].rearrange("p (g n) -> p g n", g=groups)
                                ins = nc.vector.tensor_tensor(og, og, r, ALU.mult)
                            ins.then_inc(S(f"{tag}_normed"), 1)

                    @block.tensor
                    def _(pe):
                        pe.wait_ge(S(f"{tag}_normed"), NC)
                        for m in range(NW):
                            for c in range(NC):
                                last = nc.tensor.transpose(bank[m][:, c * P:(c + 1) * P], o[:, c, m * P:(m + 1) * P], C("ident"))
                            last.then_inc(S(f"{tag}_yt"), 1)

            clear_since(outside)

            with ExitStack() as ssd:
                DT = sb(ssd, "ssd_DT", [P, SSM_H, T])
                xw = sb(ssd, "xw", [P, NC, WIDTH])
                o = xw
                G4 = SSM_H // SSM_G
                with ExitStack() as ph, nc.Block() as block:
                    xdt = sb(ph, "xdt", [P, NC, WIDTH])
                    btok = sb(ph, "btok", [P, NC, P])
                    cb = sb(ph, "cb", [P, NC * SSM_G, P])
                    dskip = sb(ph, "dskip", [P, NW, P])
                    st = sb(ph, "st", [P, NC - 1, SSM_G, G4 * SSM_P])
                    at = [sb(ph, f"at{u}", [P, SSM_H, P]) for u in range(2)]
                    tmp = [q[:, 0:4, :].rearrange("p h n -> p (h n)") for q in at]
                    pe_dt, dve_dt, act_dt = decays(tmp, DT, 0, SSM_H, "ssd")
                    chunk = [slice(c * P, (c + 1) * P) for c in range(NC)]
                    half = [slice(g * SSM_P, (g + 1) * SSM_P) for g in range(SSM_G)]
                    GW = G4 * SSM_P

                    @block.tensor
                    def _(pe):
                        for c in range(NC):
                            for m in range(NW):
                                last = nc.tensor.transpose(bank[c][:, m * P:(m + 1) * P], ch[:, m, chunk[c]], C("ident"))
                            last.then_inc(S("ssd_xt"), 1)
                        pe_dt(pe)
                        pe.wait_ge(S("ssd_bc_free"), SSM_H)
                        for c in range(NC):
                            last = nc.tensor.transpose(bank[4][:, chunk[c]], ch[:, 4, chunk[c]], C("ident"))
                        last.then_inc(S("ssd_bt"), 1)
                        for c in range(NC):
                            for g in range(SSM_G):
                                last = nc.tensor.matmul(bank[5 + g][:, chunk[c]], ch[half[g], 4, chunk[c]],
                                                        ch[half[g], 5, chunk[c]], start=True, stop=True)
                        last.then_inc(S("ssd_cb"), 1)
                        pe.wait_ge(S("ssd_btok"), 1)
                        pe.wait_ge(S("ssd_xdt"), NC)
                        for c in range(NC - 1):
                            pe.wait_ge(S("ssd_xw"), c + 1)
                            for g in range(SSM_G):
                                last = nc.tensor.matmul(bank[c // 2][half[g], (c % 2) * GW:(c % 2 + 1) * GW], btok[:, c, half[g]],
                                                        xw[:, c, g * GW:(g + 1) * GW], start=True, stop=True)
                        last.then_inc(S("ssd_st_mm"), 1)
                        pe.wait_ge(S("ssd_skip"), NW)
                        pe.wait_ge(S("ssd_cbs"), 2)
                        for c in range(NC):
                            if c >= 2:
                                pe.wait_ge(S("ssd_o"), c - 1)
                            if c >= 1:
                                pe.wait_ge(S("ssd_state"), 2 * c)
                                nc.tensor.matmul(bank[5 + c % 2][:], ch[:, 5, chunk[c]], st[:, c - 1].rearrange("p g n -> p (g n)"),
                                                 start=True, stop=True).then_inc(S("ssd_yoff"), 1)
                            for m in range(NW):
                                nc.tensor.matmul(bank[2 + c % 2][:, m * P:(m + 1) * P], ch[:, m, chunk[c]], dskip[:, m, :],
                                                 start=m == 0, stop=False, skip_group_check=True)
                            pe.wait_ge(S("ssd_at"), 2 * c + 2)
                            for h in range(SSM_H):
                                last = nc.tensor.matmul(bank[2 + c % 2][:, h * SSM_P:(h + 1) * SSM_P], at[c % 2][:, h, :],
                                                        xdt[:, c, h * SSM_P:(h + 1) * SSM_P], start=False, stop=h == SSM_H - 1,
                                                        skip_group_check=True)
                            last.then_inc(S("ssd_ydiag"), 1)

                    @block.scalar
                    def _(act):
                        act_dt(act)
                        act.wait_ge(S("ssd_bt"), 1)
                        nc.scalar.activation(btok[:].rearrange("p c n -> p (c n)"), bank[4][:], ACT.Copy).then_inc(S("ssd_btok"), 1)
                        act.wait_ge(S("ssd_cb"), 1)
                        for b in range(2):
                            nc.scalar.activation(cb[:, 4 * b:4 * b + 4, :].rearrange("p c n -> p (c n)"), bank[5 + b][:], ACT.Copy
                                                 ).then_inc(S("ssd_cbs"), 1)

                    @block.vector
                    def _(dve):
                        for m in range(NW):
                            nc.vector.tensor_scalar(dskip[:, m, :], C("ident"), v("ssm_d", m, 1), None, ALU.mult).then_inc(S("ssd_skip"), 1)
                        per = [P, SSM_H, SSM_P]
                        for c in range(NC):
                            dve.wait_ge(S("ssd_xt"), c + 1)
                            nc.vector.tensor_tensor(xdt[:, c, :].rearrange("p (h n) -> p h n", h=SSM_H),
                                                    bank[c][:].rearrange("p (h n) -> p h n", h=SSM_H),
                                                    dts[:, c * NHEAD:c * NHEAD + SSM_H].unsqueeze(2).to_broadcast(per), ALU.mult
                                                    ).then_inc(S("ssd_xdt"), 1)
                        dve_dt(dve)
                        dve.wait_ge(S("ssd_dt"), SSM_H)
                        dve.wait_ge(S("ssd_xdt"), NC)
                        for c in range(NC - 1):
                            nc.vector.tensor_tensor(xw[:, c, :].rearrange("p (h n) -> p h n", h=SSM_H),
                                                    xdt[:, c, :].rearrange("p (h n) -> p h n", h=SSM_H),
                                                    DT[:, :, c * P + P - 1:c * P + P].to_broadcast(per), ALU.mult
                                                    ).then_inc(S("ssd_xw"), 1)
                        nc.vector.memset(st[:], 0.0).then_inc(S("ssd_zero"), 1)
                        dve.wait_ge(S("ssd_zero"), 1)
                        dve.wait_ge(S("ssd_st_mm"), 1)
                        for g in range(SSM_G):
                            nc.vector.tensor_copy(st[half[g], 0, g, :], bank[0][half[g], 0:GW]).then_inc(S("ssd_state"), 1)
                        n = 0
                        for c in range(1, NC - 1):
                            dve.wait_ge(S("ssd_state"), 2 * c)
                            for g in range(SSM_G):
                                e = etot[half[g], c * NHEAD + g * G4:c * NHEAD + (g + 1) * G4].unsqueeze(2).to_broadcast([SSM_P, G4, SSM_P])
                                nc.vector.tensor_tensor(st[half[g], c, g, :].rearrange("p (h n) -> p h n", h=G4),
                                                        st[half[g], c - 1, g, :].rearrange("p (h n) -> p h n", h=G4), e, ALU.mult
                                                        ).then_inc(S("ssd_decayed"), 1)
                            n += 2
                            dve.wait_ge(S("ssd_decayed"), n)
                            for g in range(SSM_G):
                                nc.vector.tensor_tensor(st[half[g], c, g, :], st[half[g], c, g, :],
                                                        bank[c // 2][half[g], (c % 2) * GW:(c % 2 + 1) * GW], ALU.add
                                                        ).then_inc(S("ssd_state"), 1)
                        dve.wait_ge(S("ssd_cbs"), 2)
                        for c in range(NC):
                            if c >= 2:
                                dve.wait_ge(S("ssd_ydiag"), c - 1)
                            for g in range(SSM_G):
                                nc.vector.tensor_tensor(at[c % 2][:, g * G4:(g + 1) * G4, :], DT[:, g * G4:(g + 1) * G4, chunk[c]],
                                                        cb[:, NC * g + c, :].unsqueeze(1).to_broadcast([P, G4, P]), ALU.mult
                                                        ).then_inc(S("ssd_at"), 1)
                            if c >= 1:
                                dve.wait_ge(S("ssd_yoff"), c)
                                nc.vector.tensor_tensor(o[:, c, :].rearrange("p (h n) -> p h n", h=SSM_H),
                                                        bank[5 + c % 2][:].rearrange("p (h n) -> p h n", h=SSM_H),
                                                        ecol[:, c * NHEAD:c * NHEAD + SSM_H].unsqueeze(2).to_broadcast(per), ALU.mult
                                                        ).then_inc(S("ssd_yo"), 1)
                                dve.wait_ge(S("ssd_yo"), c)
                            dve.wait_ge(S("ssd_ydiag"), c + 1)
                            if c == 0:
                                nc.vector.tensor_copy(o[:, c, :], bank[2][:]).then_inc(S("ssd_o"), 1)
                            else:
                                nc.vector.tensor_tensor(o[:, c, :], o[:, c, :], bank[2 + c % 2][:], ALU.add).then_inc(S("ssd_o"), 1)
                finish(o, 0, 1, True, v("ssm_nw"), T_SSM, "ssdf")

            clear_since(outside)

            with ExitStack() as gdn:
                DT = sb(gdn, "gdn_DT", [P, GDN_H, T])
                qg = sb(gdn, "qg", [P, GDN_H, T])
                MT = sb(gdn, "MT", [P, GDN_H, T])
                XT = sb(gdn, "XT", [P, GDN_H, T])
                X = zt[:, 0]
                MS = sb(gdn, "MS", [P, GDN_H, T])
                Y = sb(gdn, "Y", [P, GDN_H, T])
                q_t, k_t, v_t = T_GDN, T_GDN + 4, T_GDN + 8
                with ExitStack() as ph, nc.Block() as block:
                    sq = [sb(ph, f"sq{u}", [P, T]) for u in range(2)]
                    rn = [sb(ph, f"rn{u}", [P, T]) for u in range(2)]

                    @block.scalar
                    def _(act):
                        for n in range(8):
                            if n >= 2:
                                act.wait_ge(S("qk_ss"), n - 1)
                            nc.scalar.activation(sq[n % 2][:], ch[:, T_GDN + n, :], ACT.Square, bias=zero).then_inc(S("qk_sq"), 1)
                            if n >= 1:
                                act.wait_ge(S("qk_ss"), n)
                                if n >= 3:
                                    act.wait_ge(S("qk_done"), n - 2)
                                nc.scalar.activation(rn[(n - 1) % 2][:], bank[(n - 1) % 2][:], ACT.Sqrt, bias=eps).then_inc(S("qk_root"), 1)
                        act.wait_ge(S("qk_ss"), 8)
                        act.wait_ge(S("qk_done"), 6)
                        nc.scalar.activation(rn[1][:], bank[1][:], ACT.Sqrt, bias=eps).then_inc(S("qk_root"), 1)

                    @block.tensor
                    def _(pe):
                        for n in range(8):
                            pe.wait_ge(S("qk_sq"), n + 1)
                            if n >= 2:
                                pe.wait_ge(S("qk_root"), n - 1)
                            nc.tensor.matmul(bank[n % 2][:], C("ones"), sq[n % 2][:], start=True, stop=True).then_inc(S("qk_ss"), 1)

                    @block.vector
                    def _(dve):
                        for n in range(8):
                            dve.wait_ge(S("qk_root"), n + 1)
                            nc.vector.reciprocal(rn[n % 2][:], rn[n % 2][:]).then_inc(S("qk_rinv"), 1)
                            dve.wait_ge(S("qk_rinv"), n + 1)
                            nc.vector.scalar_tensor_tensor(ch[:, T_GDN + n, :], ch[:, T_GDN + n, :], float(P) ** -0.5 if n < 4 else 1.0,
                                                           rn[n % 2][:], ALU.mult, ALU.mult).then_inc(S("qk_done"), 1)
                        dve.wait_ge(S("qk_done"), 8)

                with ExitStack() as ph, nc.Block() as block:
                    tmp = [sb(ph, f"dtmp{u}", [P, T])[:] for u in range(2)]
                    pe_dt, dve_dt, act_dt = decays(tmp, DT, SSM_H, GDN_H, "gdn", EG=qg)

                    @block.tensor
                    def _(pe):
                        pe_dt(pe)
                        for h in range(GDN_H):
                            for c in range(NC):
                                last = nc.tensor.matmul(bank[h][:, c * P:(c + 1) * P], ch[:, k_t + h, c * P:(c + 1) * P],
                                                        ch[:, k_t + h, c * P:(c + 1) * P], start=True, stop=True)
                            last.then_inc(S("gdn_kk"), 1)
                        for h in range(GDN_H):
                            pe.wait_ge(S("gdn_bc_free"), h + 1)
                            nc.tensor.matmul(bank[4 + h][:], sel[:, (NHEAD + h) * P:(NHEAD + h + 1) * P], rows[:],
                                             start=True, stop=True).then_inc(S("gdn_beta"), 1)
                        for h in range(GDN_H):
                            pe.wait_ge(S("gdn_x1"), h + 1)
                            for c in range(NC):
                                last = nc.tensor.transpose(bank[h][:, c * P:(c + 1) * P], XT[:, h, c * P:(c + 1) * P], C("ident"))
                            last.then_inc(S("gdn_x1t"), 1)

                    @block.scalar
                    def _(act):
                        act_dt(act)
                        for h in range(GDN_H):
                            act.wait_ge(S("gdn_x1t"), h + 1)
                            nc.scalar.activation(X[:, h, :], bank[h][:], ACT.Copy).then_inc(S("gdn_x"), 1)
                        act.wait_ge(S("gdn_x"), GDN_H)

                    @block.vector
                    def _(dve):
                        dve_dt(dve)
                        for h in range(GDN_H):
                            nc.vector.tensor_tensor(qg[:, h, :], qg[:, h, :], ch[:, q_t + h, :], ALU.mult).then_inc(S("gdn_qg"), 1)
                        for h in range(GDN_H):
                            dve.wait_ge(S("gdn_kk"), h + 1)
                            dve.wait_ge(S("gdn_dt"), h + 1)
                            nc.vector.tensor_tensor(MT[:, h, :], DT[:, h, :], bank[h][:], ALU.mult).then_inc(S("gdn_m"), 1)
                            dve.wait_ge(S("gdn_m"), 2 * h + 1)
                            dve.wait_ge(S("gdn_beta"), h + 1)
                            nc.vector.tensor_tensor(MT[:, h, :], MT[:, h, :], bank[4 + h][:], ALU.mult).then_inc(S("gdn_m"), 1)
                            dve.wait_ge(S("gdn_m"), 2 * h + 2)
                            per = [P, NC, P]
                            m4 = MT[:, h, :].rearrange("p (c n) -> p c n", c=NC)
                            x4 = XT[:, h, :].rearrange("p (c n) -> p c n", c=NC)
                            nc.vector.tensor_tensor(x4, m4, C("lv1").unsqueeze(1).to_broadcast(per), ALU.mult).then_inc(S("gdn_lv1"), 1)
                            dve.wait_ge(S("gdn_lv1"), h + 1)
                            nc.vector.tensor_tensor(x4, C("ident").unsqueeze(1).to_broadcast(per), x4, ALU.subtract).then_inc(S("gdn_x1"), 1)
                        dve.wait_ge(S("gdn_x1"), GDN_H)

                with nc.Block() as block:
                    N_LV = len(LEVELS)

                    @block.tensor
                    def _(pe):
                        for n, s in enumerate(LEVELS):
                            for h in range(GDN_H):
                                pe.wait_ge(S("inv_ms"), GDN_H * n + h + 1)
                                if n:
                                    pe.wait_ge(S("inv_x"), GDN_H * (n - 1) + h + 1)
                                for c in range(NC):
                                    cc = slice(c * P, (c + 1) * P)
                                    last = nc.tensor.matmul(bank[h][:, cc], MS[:, h, cc], X[:, h, cc], start=True, stop=True)
                                last.then_inc(S("inv_y_mm"), 1)
                            for h in range(GDN_H):
                                pe.wait_ge(S("inv_y"), GDN_H * n + h + 1)
                                if n:
                                    pe.wait_ge(S("inv_xt"), GDN_H * (n - 1) + h + 1)
                                for c in range(NC):
                                    cc = slice(c * P, (c + 1) * P)
                                    last = nc.tensor.matmul(bank[4 + h][:, cc], Y[:, h, cc], XT[:, h, cc], start=True, stop=True)
                                last.then_inc(S("inv_xt_mm"), 1)
                                if n < N_LV - 1:
                                    for c in range(NC):
                                        cc = slice(c * P, (c + 1) * P)
                                        last = nc.tensor.matmul(bank[h][:, cc], XT[:, h, cc], Y[:, h, cc], start=True, stop=True)
                                    last.then_inc(S("inv_x_mm"), 1)

                    @block.scalar
                    def _(act):
                        for n in range(N_LV):
                            for h in range(GDN_H):
                                act.wait_ge(S("inv_y_mm"), GDN_H * n + h + 1)
                                if n:
                                    act.wait_ge(S("inv_x_mm"), GDN_H * (n - 1) + h + 1)
                                nc.scalar.activation(Y[:, h, :], bank[h][:], ACT.Copy).then_inc(S("inv_y"), 1)

                    @block.vector
                    def _(dve):
                        for n, s in enumerate(LEVELS):
                            for h in range(GDN_H):
                                if n:
                                    dve.wait_ge(S("inv_y_mm"), GDN_H * (n - 1) + h + 1)
                                nc.vector.tensor_tensor(MS[:, h, :].rearrange("p (c n) -> p c n", c=NC),
                                                        MT[:, h, :].rearrange("p (c n) -> p c n", c=NC),
                                                        C(f"lv{s}").unsqueeze(1).to_broadcast([P, NC, P]), ALU.mult).then_inc(S("inv_ms"), 1)
                            for h in range(GDN_H):
                                if n < N_LV - 1:
                                    dve.wait_ge(S("inv_x_mm"), GDN_H * n + h + 1)
                                    nc.vector.tensor_tensor(X[:, h, :], X[:, h, :], bank[h][:], ALU.subtract).then_inc(S("inv_x"), 1)
                                dve.wait_ge(S("inv_xt_mm"), GDN_H * n + h + 1)
                                if n < N_LV - 1:
                                    dve.wait_ge(S("inv_x_mm"), GDN_H * n + h + 1)
                                nc.vector.tensor_tensor(XT[:, h, :], XT[:, h, :], bank[4 + h][:], ALU.subtract).then_inc(S("inv_xt"), 1)
                        dve.wait_ge(S("inv_xt"), GDN_H * N_LV)

                AT, KB, WT, o = MS, MT, X, Y
                KD_, VB = ch[:, k_t:k_t + GDN_H, :], ch[:, v_t:v_t + GDN_H, :]
                with ExitStack() as ph, nc.Block() as block:
                    vn = sb(ph, "vn", [P, T])
                    sg = sb(ph, "sg", [P, T])
                    eb = sb(ph, "eb", [P, NC, GDN_H])
                    per = [P, NC, P]

                    def byc(t):
                        return t.rearrange("p (c n) -> p c n", c=NC)

                    @block.tensor
                    def _(pe):
                        def grid(b, left, right, sem):
                            for c in range(NC):
                                cc = slice(c * P, (c + 1) * P)
                                last = nc.tensor.matmul(bank[b][:, cc], left[:, cc], right[:, cc], start=True, stop=True)
                            last.then_inc(S(sem), 1)

                        for h in range(GDN_H):
                            if h:
                                pe.wait_ge(S("gdn_at"), h)
                            grid(0, ch[:, k_t + h, :], ch[:, q_t + h, :], "gdn_kq")
                            if h:
                                pe.wait_ge(S("gdn_kd"), h)
                                pe.wait_ge(S("gdn_vb"), h)
                            for b, t in ((1, k_t), (2, v_t)):
                                for c in range(NC):
                                    cc = slice(c * P, (c + 1) * P)
                                    last = nc.tensor.transpose(bank[b][:, cc], ch[:, t + h, cc], C("ident"))
                                last.then_inc(S("gdn_kvt"), 1)
                            pe.wait_ge(S("gdn_kb"), h + 1)
                            if h:
                                pe.wait_ge(S("gdn_wt"), h)
                            grid(3, KB[:, h, :], XT[:, h, :], "gdn_w_mm")
                        for c in range(NC):
                            cc = slice(c * P, (c + 1) * P)
                            if c:
                                pe.wait_ge(S("gdn_state"), c)
                            else:
                                pe.wait_ge(S("gdn_wt"), GDN_H)
                                pe.wait_ge(S("gdn_vb"), GDN_H)
                            for h in range(GDN_H):
                                hh = slice(h * P, (h + 1) * P)
                                last = nc.tensor.matmul(bank[4][:, hh], XT[:, h, cc], VB[:, h, cc], start=True, stop=c == 0)
                                if c:
                                    last = nc.tensor.matmul(bank[4][:, hh], WT[:, h, cc], sg[:, hh], start=False, stop=True)
                            last.then_inc(S("gdn_vn_mm"), 1)
                            pe.wait_ge(S("gdn_vn"), c + 1)
                            if c:
                                pe.wait_ge(S("gdn_o"), c)
                            for h in range(GDN_H):
                                hh = slice(h * P, (h + 1) * P)
                                last = nc.tensor.matmul(bank[6][:, hh], KD_[:, h, cc], vn[:, hh], start=True, stop=True)
                            last.then_inc(S("gdn_s_mm"), 1)
                            for h in range(GDN_H):
                                hh = slice(h * P, (h + 1) * P)
                                last = nc.tensor.matmul(bank[5][:, hh], AT[:, h, cc], vn[:, hh], start=True, stop=c == 0)
                                if c:
                                    last = nc.tensor.matmul(bank[5][:, hh], qg[:, h, cc], sg[:, hh], start=False, stop=True)
                            last.then_inc(S("gdn_o_mm"), 1)

                    @block.scalar
                    def _(act):
                        for h in range(GDN_H):
                            act.wait_ge(S("gdn_w_mm"), h + 1)
                            nc.scalar.activation(WT[:, h, :], bank[3][:], ACT.Copy, scale=-1.0).then_inc(S("gdn_wt"), 1)
                        for c in range(NC):
                            act.wait_ge(S("gdn_vn_mm"), c + 1)
                            if c:
                                act.wait_ge(S("gdn_o_mm"), c)
                            nc.scalar.activation(vn[:], bank[4][:], ACT.Copy).then_inc(S("gdn_vn"), 1)
                            act.wait_ge(S("gdn_o_mm"), c + 1)
                            nc.scalar.activation(o[:, c, :], bank[5][:], ACT.Copy).then_inc(S("gdn_o"), 1)
                        act.wait_ge(S("gdn_o"), NC)

                    @block.vector
                    def _(dve):
                        nc.vector.tensor_tensor(eb[:], dec[:, :, NHEAD:16],
                                                ecol[:].rearrange("p (c h) -> p c h", c=NC)[:, :, SSM_H:NHEAD], ALU.mult).then_inc(S("gdn_eb"), 1)
                        dve.wait_ge(S("gdn_eb"), 1)
                        for h in range(GDN_H):
                            dve.wait_ge(S("gdn_kq"), h + 1)
                            nc.vector.tensor_tensor(AT[:, h, :], DT[:, h, :], bank[0][:], ALU.mult).then_inc(S("gdn_at"), 1)
                            dve.wait_ge(S("gdn_kvt"), 2 * h + 2)
                            nc.vector.tensor_tensor(byc(KB[:, h, :]), byc(bank[1][:]), eb[:, :, h:h + 1].to_broadcast(per), ALU.mult
                                                    ).then_inc(S("gdn_kb"), 1)
                            nc.vector.tensor_tensor(byc(KD_[:, h, :]), byc(bank[1][:]), DT[:, h, P - 1:T:P].unsqueeze(2).to_broadcast(per),
                                                    ALU.mult).then_inc(S("gdn_kd"), 1)
                            nc.vector.tensor_tensor(byc(VB[:, h, :]), byc(bank[2][:]), dec[:, :, NHEAD + h:NHEAD + h + 1].to_broadcast(per),
                                                    ALU.mult).then_inc(S("gdn_vb"), 1)
                        for c in range(NC - 1):
                            dve.wait_ge(S("gdn_s_mm"), c + 1)
                            if c == 0:
                                nc.vector.tensor_copy(sg[:], bank[6][:]).then_inc(S("gdn_state"), 1)
                            else:
                                dve.wait_ge(S("gdn_o_mm"), c + 1)
                                dve.wait_ge(S("gdn_state"), c)
                                for h in range(GDN_H):
                                    hh = slice(h * P, (h + 1) * P)
                                    e = c * NHEAD + SSM_H + h
                                    last = nc.vector.scalar_tensor_tensor(sg[:, hh], sg[:, hh], etot[:, e:e + 1], bank[6][:, hh],
                                                                          ALU.mult, ALU.add)
                                last.then_inc(S("gdn_state"), 1)
                finish(o, 1, GDN_H, False, v("gdn_nw"), T_GDN, "gdnf")

            clear_since(outside)

            with ExitStack() as gla:
                o = sb(gla, "gla_o", [P, NC, WIDTH])
                G2 = [P, 2 * NC, P]
                with ExitStack() as ph, nc.Block() as block:
                    wg = sb(ph, "wg", [RANK, 2 * P])
                    G = sb(ph, "G", [P, 2, T])
                    nab = sb(ph, "nab", [P, 2, T])
                    e1 = sb(ph, "e1", [P, 2, T])
                    e2 = sb(ph, "e2", [P, 2, T])
                    qe = sb(ph, "qe", [P, 2, T])
                    ke = sb(ph, "ke", [P, 2, T])
                    qs = sb(ph, "qs", [P, 2, T])
                    kd = sb(ph, "kd", [P, 2, T])
                    kt = sb(ph, "kt", [P, NC, 2 * P])
                    at = zt[:, 0]
                    gs = sb(ph, "gs", [P, NC - 1, 2, 2, P])
                    ed = sb(ph, "ed", [P, 2 * NC])
                    q2, k2 = ch[:, T_GLAQ:T_GLAQ + 2, :], ch[:, T_GLAQ + 2:T_GLAQ + 4, :]

                    def by(t):
                        return t.rearrange("p m (c n) -> p (m c) n", c=NC)

                    def tok(m):
                        return by(G[:])[:, :, m:m + 1].to_broadcast(G2)

                    @block.gpsimd
                    def _(pool):
                        nc.gpsimd.memset(gs[:], 0.0).then_inc(S("gla_zero"), 1)

                    @block.sync
                    def _(sp):
                        sp.dma_start(wg[:], lay("w_gate")).then_inc(S("wg_loaded"), 16)

                    @block.tensor
                    def _(pe):
                        pe.wait_ge(S("wg_loaded"), 16)
                        for m in range(2):
                            nc.tensor.matmul(bank[m][:], wg[:, m * P:(m + 1) * P], low[:], start=True, stop=True).then_inc(S("gla_pre"), 1)
                        pe.wait_ge(S("gla_kd"), 1)
                        for c in range(NC):
                            for m in range(2):
                                last = nc.tensor.transpose(bank[2 + c // 2][:, (c % 2 * 2 + m) * P:(c % 2 * 2 + m + 1) * P],
                                                           kd[:, m, c * P:(c + 1) * P], C("ident"))
                        last.then_inc(S("gla_kdt"), 1)
                        pe.wait_ge(S("gla_ke"), 2)
                        for h in range(GLA_H):
                            r = slice(h % 2 * GLA_K, (h % 2 + 1) * GLA_K)
                            for c in range(NC):
                                cc = slice(c * P, (c + 1) * P)
                                last = nc.tensor.matmul(bank[4 + h][:, cc], ke[r, h // 2, cc], qe[r, h // 2, cc], start=True, stop=True)
                            last.then_inc(S("gla_qk"), 1)
                        pe.wait_ge(S("gla_kt"), 2)
                        for c in range(NC - 1):
                            for h in range(GLA_H):
                                r = slice(h % 2 * GLA_K, (h % 2 + 1) * GLA_K)
                                m = (c % 2) * 2 + h // 2
                                last = nc.tensor.matmul(bank[c // 2][r, m * P:(m + 1) * P], kt[:, c, h * GLA_K:(h + 1) * GLA_K],
                                                        zt[:, 3, c, h * P:(h + 1) * P], start=True, stop=True)
                        last.then_inc(S("gla_s_mm"), 1)
                        for c in range(NC):
                            cc = slice(c * P, (c + 1) * P)
                            if c:
                                pe.wait_ge(S("gla_state"), c)
                            else:
                                pe.wait_ge(S("gla_at"), GLA_H)
                            if c >= 2:
                                pe.wait_ge(S("gla_o"), c - 1)
                            for m in range(2) if c else ():
                                nc.tensor.matmul(bank[2 + c % 2][:, 2 * m * P:2 * (m + 1) * P], qs[:, m, cc],
                                                 gs[:, c - 1, m].rearrange("p h n -> p (h n)"), start=m == 0, stop=False,
                                                 skip_group_check=True)
                            for h in range(GLA_H):
                                hh = slice(h * P, (h + 1) * P)
                                last = nc.tensor.matmul(bank[2 + c % 2][:, hh], at[:, h, cc], zt[:, 3, c, hh], start=c == 0 and h == 0,
                                                        stop=h == GLA_H - 1, skip_group_check=True)
                            last.then_inc(S("gla_o_mm"), 1)

                    @block.scalar
                    def _(act):
                        act.wait_ge(S("gla_nab"), 2)
                        nc.scalar.activation(e1[:], nab[:], ACT.Exp, bias=zero).then_inc(S("gla_z"), 1)
                        act.wait_ge(S("gla_z"), 1)
                        nc.scalar.activation(e1[:], e1[:], ACT.Ln, bias=cst[:, C_OFF["ones"]:C_OFF["ones"] + 1]).then_inc(S("gla_ln"), 1)
                        act.wait_ge(S("gla_mid"), 1)
                        nc.scalar.activation(e1[:], nab[:], ACT.Exp, bias=zero).then_inc(S("gla_e"), 1)
                        nc.scalar.activation(e2[:], nab[:], ACT.Exp, bias=zero, scale=-1.0).then_inc(S("gla_e"), 1)
                        nc.scalar.activation(qs[:], G[:], ACT.Exp, bias=zero).then_inc(S("gla_eg"), 1)
                        nc.scalar.activation(ed[:], by(G[:])[:, :, P - 1], ACT.Exp, bias=zero).then_inc(S("gla_ed"), 1)
                        act.wait_ge(S("gla_end"), 1)
                        nc.scalar.activation(kd[:], kd[:], ACT.Exp, bias=zero, scale=-1.0).then_inc(S("gla_ekd"), 1)
                        act.wait_ge(S("gla_kdt"), 1)
                        for b in range(2):
                            nc.scalar.activation(kt[:, 2 * b:2 * b + 2, :].rearrange("p c n -> p (c n)"), bank[2 + b][:], ACT.Copy
                                                 ).then_inc(S("gla_kt"), 1)
                        for c in range(NC):
                            act.wait_ge(S("gla_o_mm"), c + 1)
                            nc.scalar.activation(o[:, c, :], bank[2 + c % 2][:], ACT.Copy).then_inc(S("gla_o"), 1)
                        act.wait_ge(S("gla_o"), NC)

                    @block.vector
                    def _(dve):
                        for m in range(2):
                            dve.wait_ge(S("gla_pre"), m + 1)
                            nc.vector.tensor_scalar(G[:, m, :], bank[m][:], v("gla_b", m, 1), None, ALU.add).then_inc(S("gla_x"), 1)
                        dve.wait_ge(S("gla_x"), 2)
                        for m in range(2):
                            nc.vector.scalar_tensor_tensor(nab[:, m, :], G[:, m, :], -1.0, G[:, m, :], ALU.mult, ALU.min).then_inc(S("gla_nab"), 1)
                        dve.wait_ge(S("gla_ln"), 1)
                        nc.vector.scalar_tensor_tensor(e1[:], G[:], 0.0, e1[:], ALU.min, ALU.subtract).then_inc(S("gla_ls"), 1)
                        dve.wait_ge(S("gla_ls"), 1)
                        nc.vector.tensor_scalar(e1[:], e1[:], 1.0 / GLA_TAU, None, ALU.mult).then_inc(S("gla_ls"), 1)
                        dve.wait_ge(S("gla_ls"), 2)
                        for m in range(2):
                            nc.vector.tensor_tensor_scan(G[:, m, :], cst[:, C_RESET:C_RESET + T], e1[:, m, :], 0.0, ALU.mult, ALU.add
                                                         ).then_inc(S("gla_G"), 1)
                        dve.wait_ge(S("gla_G"), 2)
                        nc.vector.tensor_tensor(by(nab[:]), by(G[:]), tok(P // 2 - 1), ALU.subtract).then_inc(S("gla_mid"), 1)
                        nc.vector.tensor_tensor(by(kd[:]), by(G[:]), tok(P - 1), ALU.subtract).then_inc(S("gla_end"), 1)
                        s = float(GLA_K) ** -0.5
                        dve.wait_ge(S("gla_ekd"), 1)
                        nc.vector.tensor_tensor(kd[:], kd[:], k2, ALU.mult).then_inc(S("gla_kd"), 1)
                        dve.wait_ge(S("gla_e"), 2)
                        nc.vector.scalar_tensor_tensor(qe[:], q2, s, e1[:], ALU.mult, ALU.mult).then_inc(S("gla_ke"), 1)
                        nc.vector.tensor_tensor(ke[:], k2, e2[:], ALU.mult).then_inc(S("gla_ke"), 1)
                        dve.wait_ge(S("gla_eg"), 1)
                        nc.vector.scalar_tensor_tensor(qs[:], q2, s, qs[:], ALU.mult, ALU.mult).then_inc(S("gla_qs"), 1)
                        for h in range(GLA_H):
                            dve.wait_ge(S("gla_qk"), h + 1)
                            nc.vector.tensor_tensor(at[:, h, :].rearrange("p (c n) -> p c n", c=NC), bank[4 + h][:].rearrange("p (c n) -> p c n", c=NC),
                                                    C("tri").unsqueeze(1).to_broadcast([P, NC, P]), ALU.mult).then_inc(S("gla_at"), 1)
                        dve.wait_ge(S("gla_s_mm"), 1)
                        dve.wait_ge(S("gla_ed"), 1)
                        dve.wait_ge(S("gla_qs"), 1)
                        dve.wait_ge(S("gla_zero"), 1)
                        for c in range(NC - 1):
                            if c:
                                dve.wait_ge(S("gla_state"), c)
                            for m in range(2):
                                b = (c % 2) * 2 + m
                                for h in range(2):
                                    r = slice(h * GLA_K, (h + 1) * GLA_K)
                                    if c == 0:
                                        last = nc.vector.tensor_copy(gs[r, c, m, h], bank[0][r, m * P:(m + 1) * P])
                                    else:
                                        last = nc.vector.scalar_tensor_tensor(gs[r, c, m, h], gs[r, c - 1, m, h],
                                                                              ed[r, m * NC + c:m * NC + c + 1],
                                                                              bank[c // 2][r, b * P:(b + 1) * P], ALU.mult, ALU.add)
                            last.then_inc(S("gla_state"), 1)
                finish(o, 2, GLA_H, False, v("gla_nw"), T_GLAQ, "glaf")

            clear_since(outside)

            with ExitStack() as ph, nc.Block() as block:
                wl = sb(ph, "wl", [P, 2, NW, P])
                aa = sb(ph, "aa", [P, NW, T])
                gi = sb(ph, "gi", [P, NW, T])
                th = sb(ph, "th", [P, NW, T])
                lam = sb(ph, "lam", [P, NW])
                x4, g4 = ch[:, T_LRUX:T_LRUX + NW, :], ch[:, T_LRUG:T_LRUG + NW, :]

                @block.gpsimd
                def _(pool):
                    nc.gpsimd.memset(wl[:], 0.0).then_inc(S("wl_zero"), 1)

                @block.sync
                def _(sp):
                    sp.wait_ge(S("wl_zero"), 1)
                    w = lay("w_lru")
                    for g in range(2):
                        for half in range(2):
                            r = slice(64 * half, 64 * half + 64)
                            sp.dma_start(wl[r, g, :, r], w[half, :, g]).then_inc(S("wl_loaded"), 16)

                @block.tensor
                def _(pe):
                    pe.wait_ge(S("wl_loaded"), 64)
                    for g in range(2):
                        for m in range(NW):
                            nc.tensor.matmul(bank[4 * g + m][:], wl[:, g, m, :], x4[:, m, :], start=True, stop=True).then_inc(S("lru_mm"), 1)

                @block.scalar
                def _(act):
                    for g, (dst, b) in enumerate(((aa, "lru_ba"), (gi, "lru_bx"))):
                        for m in range(NW):
                            act.wait_ge(S("lru_mm"), 4 * g + m + 1)
                            nc.scalar.activation(dst[:, m, :], bank[4 * g + m][:], ACT.Sigmoid, bias=v(b, m, 1)).then_inc(S("lru_gate"), 1)
                    for m in range(NW):
                        act.wait_ge(S("lru_loga"), m + 1)
                        nc.scalar.activation(th[:, m, :], aa[:, m, :], ACT.Tanh, bias=zero, scale=-1.0).then_inc(S("lru_th"), 1)
                    act.wait_ge(S("lru_th"), NW)
                    for m in range(NW):
                        nc.scalar.activation(aa[:, m, :], aa[:, m, :], ACT.Exp, bias=zero).then_inc(S("lru_a"), 1)
                    for m in range(NW):
                        act.wait_ge(S("lru_u2"), 2 * m + 2)
                        nc.scalar.activation(th[:, m, :], th[:, m, :], ACT.Sqrt, bias=zero).then_inc(S("lru_root"), 1)
                    for m in range(NW):
                        nc.scalar.activation(g4[:, m, :], g4[:, m, :], ACT.Gelu_apprx_tanh, bias=zero).then_inc(S("lru_gelu"), 1)

                @block.vector
                def _(dve):
                    nc.vector.tensor_scalar(lam[:], dts[:, NS:], -LRU_C, None, ALU.mult).then_inc(S("lru_lam"), 1)
                    dve.wait_ge(S("lru_lam"), 1)
                    for m in range(NW):
                        dve.wait_ge(S("lru_gate"), m + 1)
                        nc.vector.tensor_scalar(aa[:, m, :], aa[:, m, :], lam[:, m:m + 1], None, ALU.mult).then_inc(S("lru_loga"), 1)
                    for m in range(NW):
                        dve.wait_ge(S("lru_gate"), NW + m + 1)
                        nc.vector.tensor_tensor(gi[:, m, :], gi[:, m, :], x4[:, m, :], ALU.mult).then_inc(S("lru_gx"), 1)
                    for m in range(NW):
                        dve.wait_ge(S("lru_a"), m + 1)
                        dve.wait_ge(S("lru_gx"), m + 1)
                        nc.vector.tensor_tensor(x4[:, m, :], aa[:, m, :], aa[:, m, :], ALU.mult).then_inc(S("lru_u2"), 1)
                        dve.wait_ge(S("lru_u2"), 2 * m + 1)
                        nc.vector.scalar_tensor_tensor(th[:, m, :], x4[:, m, :], 1.0, th[:, m, :], ALU.add, ALU.mult).then_inc(S("lru_u2"), 1)
                    for m in range(NW):
                        dve.wait_ge(S("lru_root"), m + 1)
                        nc.vector.tensor_tensor(gi[:, m, :], gi[:, m, :], th[:, m, :], ALU.mult).then_inc(S("lru_u"), 1)
                        dve.wait_ge(S("lru_u"), m + 1)
                        dve.wait_ge(S("lru_u2"), 2 * m + 2)
                        nc.vector.tensor_tensor_scan(x4[:, m, :], aa[:, m, :], gi[:, m, :], 0.0, ALU.mult, ALU.add).then_inc(S("lru_h"), 1)
                    for m in range(NW):
                        dve.wait_ge(S("lru_h"), m + 1)
                        dve.wait_ge(S("lru_gelu"), m + 1)
                        nc.vector.tensor_tensor(x4[:, m, :], x4[:, m, :], g4[:, m, :], ALU.mult).then_inc(S("lru_y"), 1)
                    dve.wait_ge(S("lru_y"), NW)
            sm.close()
            clear_since(outside)

            branch = (T_SSM, T_GDN, T_GLAQ, T_LRUX)
            with ExitStack() as ph, nc.Block() as block:
                wm = [sb(ph, f"wm{u}", [P, KD, P]) for u in range(2)]
                wb = [sb(ph, f"wb{u}", [P, NW, P]) for u in range(2)]
                sg = [sb(ph, f"sig{u}", [P, T]) for u in range(2)]
                mg = [sb(ph, f"mg{u}", [P, T]) for u in range(2)]
                acc = sb(ph, "acc", [P, T])
                merged = sb(ph, "merged", [P, KD, T])
                w_m, w_b, w_o = lay("w_merge"), lay("w_branch"), lay("w_out")

                @block.sync
                def _(sp):
                    sp.sem_inc(S("wm_free"), 2)
                    with sp.Fori(0, N_MERGE // 2) as i:
                        for u in range(2):
                            sp.wait_ge(S("wm_free"), 2 * i + u + 1)
                            sp.dma_start(wm[u][:].rearrange("p k n -> p (k n)"),
                                         w_m[bass.ds(2 * i + u, 1)].rearrange("g p n -> (g p) n")).then_inc(S(f"wm_loaded{u}"), 16)
                            sp.dma_start(wb[u][:].rearrange("p k n -> p (k n)"),
                                         w_b[bass.ds(2 * i + u, 1)].rearrange("g p n -> (g p) n")).then_inc(S(f"wm_loaded{u}"), 16)
                    with sp.Fori(0, KD // 2) as i:
                        for u in range(2):
                            sp.wait_ge(S("wm_free"), 2 * i + u + N_MERGE + 1)
                            sp.dma_start(wm[u][:].rearrange("p k n -> p (k n)"),
                                         w_o[bass.ds(2 * i + u, 1)].rearrange("g p n -> (g p) n")).then_inc(S(f"wo_loaded{u}"), 16)

                @block.tensor
                def _(pe):
                    pe.sem_inc(S("mg_bank_free"), 2)
                    with pe.Fori(0, KD) as i:
                        for b in range(4):
                            u = b % 2
                            pe.wait_ge(S(f"wm_loaded{u}"), 64 * i + 32 * (b // 2) + 32)
                            pe.wait_ge(S("mg_bank_free"), 4 * i + b + 1)
                            for k in range(KD):
                                last = nc.tensor.matmul(bank[u][:], wm[u][:, k, :], hT[:, k, :], start=k == 0, stop=k == KD - 1)
                            last.then_inc(S("mg_mm"), 1)
                            for k in range(NW):
                                last = nc.tensor.matmul(bank[2 + u][:], wb[u][:, k, :], ch[:, branch[b] + k, :], start=k == 0, stop=k == NW - 1)
                            last.then_inc(S("mg_mm"), 1)
                    pe.wait_ge(S("merged"), KD)
                    pe.sem_inc(S("out_bank_free"), 2)
                    with pe.Fori(0, KD // 2) as i:
                        for u in range(2):
                            pe.wait_ge(S(f"wo_loaded{u}"), 16 * i + 16)
                            pe.wait_ge(S("out_bank_free"), 2 * i + u + 1)
                            for k in range(KD):
                                last = nc.tensor.matmul(bank[4 + u][:], wm[u][:, k, :], merged[:, k, :], start=k == 0, stop=k == KD - 1)
                            last.then_inc(S("out_mm"), 1)

                @block.scalar
                def _(act):
                    act.sem_inc(S("sig_free"), 2)
                    with act.Fori(0, KD) as i:
                        for b in range(4):
                            u = b % 2
                            act.wait_ge(S("mg_mm"), 8 * i + 2 * b + 1)
                            act.wait_ge(S("sig_free"), 4 * i + b + 1)
                            nc.scalar.activation(sg[u][:], bank[u][:], ACT.Sigmoid, bias=zero).then_inc(S("sig_done"), 1)

                @block.vector
                def _(dve):
                    with dve.Fori(0, KD) as i:
                        for b in range(4):
                            u = b % 2
                            dve.wait_ge(S("mg_mm"), 8 * i + 2 * b + 2)
                            dve.wait_ge(S("sig_done"), 4 * i + b + 1)
                            dst = acc[:] if b == 0 else mg[u][:]
                            nc.vector.tensor_tensor(dst, sg[u][:], bank[2 + u][:], ALU.mult).then_inc(S("mg_prod"), 1)
                            dve.wait_ge(S("mg_prod"), 4 * i + b + 1)
                            dve.sem_inc(S("mg_bank_free"), 1)
                            dve.sem_inc(S("sig_free"), 1)
                            dve.sem_inc(S("wm_free"), 1)
                            if b in (1, 2):
                                if b == 2:
                                    dve.wait_ge(S("mg_sum"), 2 * i + 1)
                                nc.vector.tensor_tensor(acc[:], acc[:], mg[u][:], ALU.add).then_inc(S("mg_sum"), 1)
                            if b == 3:
                                dve.wait_ge(S("mg_sum"), 2 * i + 2)
                                nc.vector.tensor_tensor(row(merged, i), acc[:], mg[u][:], ALU.add).then_inc(S("merged"), 1)
                                dve.wait_ge(S("merged"), i + 1)
                    with dve.Fori(0, KD // 2) as i:
                        for u in range(2):
                            dve.wait_ge(S("out_mm"), 2 * i + u + 1)
                            xt = row(xT, 2 * i + u)
                            nc.vector.scalar_tensor_tensor(xt, bank[4 + u][:], mod[:, bass.ds(2 * KD + 2 * i + u, 1)], xt, ALU.mult, ALU.add
                                                           ).then_inc(S("x_mixed"), 1)
                            dve.wait_ge(S("x_mixed"), 2 * i + u + 1)
                            dve.sem_inc(S("out_bank_free"), 1)
                            dve.sem_inc(S("wm_free"), 1)
            mix.close()

            clear_since(outside)

            peer = ExitStack()
            hT = sb(peer, "h2T", [P, KD, T])
            norm(hT, "nffn", gain[:, KD:2 * KD], mod[:, 3 * KD:4 * KD])
            route = ExitStack()
            qT = sb(route, "qT", [P, QT, T])
            keys = sb(route, "keys", [P, QT, KEYS])
            stage = sb(route, "stage", [P, KEYS, P])
            with ExitStack() as ph, nc.Block() as block:
                wq = [sb(ph, f"wq{u}", [P, KD, P]) for u in range(2)]
                w_q = lay("w_q")

                @block.sync
                def _(sp):
                    sp.sem_inc(S("wq_free"), 2)
                    sp.dma_start(keys[:], lay("keys")).then_inc(S("keys_loaded"), 16)
                    with sp.Fori(0, QT // 2) as i:
                        for u in range(2):
                            sp.wait_ge(S("wq_free"), 2 * i + u + 1)
                            sp.dma_start(wq[u][:].rearrange("p k n -> p (k n)"),
                                         w_q[bass.ds(2 * i + u, 1)].rearrange("g p n -> (g p) n")).then_inc(S(f"wq_loaded{u}"), 16)
                    sp.wait_ge(S("keys_loaded"), 16)
                    sp.sem_inc(S("stage_free"), 16)

                @block.tensor
                def _(pe):
                    pe.sem_inc(S("q_bank_free"), 2)
                    with pe.Fori(0, QT // 2) as i:
                        for u in range(2):
                            pe.wait_ge(S(f"wq_loaded{u}"), 16 * i + 16)
                            pe.wait_ge(S("q_bank_free"), 2 * i + u + 1)
                            for k in range(KD):
                                last = nc.tensor.matmul(bank[u][:], wq[u][:, k, :], hT[:, k, :], start=k == 0, stop=k == KD - 1)
                            last.then_inc(S("q_mm"), 1)

                @block.scalar
                def _(act):
                    with act.Fori(0, QT // 2) as i:
                        for u in range(2):
                            act.wait_ge(S("q_mm"), 2 * i + u + 1)
                            nc.scalar.activation(row(qT, 2 * i + u), bank[u][:], ACT.Copy).then_inc(S("q_bank_free"), 1)
                            act.wait_ge(S("q_bank_free"), 2 * i + u + 3)
                            act.sem_inc(S("wq_free"), 1)

            with nc.Fori(0, NC) as tt:
                before = set(made)
                with ExitStack() as ph, nc.Block() as block:
                    qs = sb(ph, "qs", [P, QT, P])
                    s = sb(ph, "s", [P, QT, KEYS])
                    top = sb(ph, "top", [P, QT, TOPK])
                    idx = sb(ph, "idx", [P, QT, TOPK], U32)
                    idf = sb(ph, "idf", [P, QT, TOPK])
                    cand = sb(ph, "cand", [P, PEER_H, TOPK * TOPK])
                    best = sb(ph, "best", [P, PEER_H, TOPK])
                    pos = sb(ph, "pos", [P, PEER_H, TOPK], U32)
                    pu = sb(ph, "pu", [P, 2, PEER_H, TOPK], U32)
                    pf = sb(ph, "pf", [P, 2, PEER_H, TOPK])
                    chosen = sb(ph, "chosen", [P, 3, NHK])
                    ssum = sb(ph, "ssum", [P, PEER_H])
                    slots = sb(ph, "slots", [P, 3, P])
                    hot = sb(ph, "hot", [P, 8, 2, P])
                    eq = s[:].rearrange("p a n -> p (a n)").rearrange("p (h k j) -> p h k j", h=PEER_H, k=TOPK)
                    four = [P, PEER_H, TOPK, TOPK]
                    NEG = -3.0e38

                    @block.tensor
                    def _(pe):
                        pe.wait_ge(S("qs_done"), 1)
                        for n in range(QT):
                            last = nc.tensor.matmul(bank[n // 4][:, n % 4 * P:(n % 4 + 1) * P], qs[:, n, :], keys[:, n, :],
                                                    start=True, stop=True)
                            if n % 4 == 3:
                                last.then_inc(S("s_mm"), 1)
                        for n in range(3):
                            pe.wait_ge(S("chosen_done"), n + 1)
                            last = nc.tensor.transpose(bank[4][:, n * P:(n + 1) * P], chosen[:, n, :], C("ident"))
                        last.then_inc(S("slots_t"), 1)
                        pe.sem_inc(S("g_bank_free"), 2)
                        with pe.Fori(0, P // 8) as i:
                            for w in range(2):
                                pe.wait_ge(S("hot_ready"), 2 * i + w + 1)
                                pe.wait_ge(S("g_bank_free"), 2 * i + w + 1)
                                for q in range(4):
                                    last = nc.tensor.matmul(bank[6 + w][:, q * P:(q + 1) * P], hot[:, 4 * w + q, 0, :], hot[:, 4 * w + q, 1, :],
                                                            start=True, stop=True)
                                last.then_inc(S("g_mm"), 1)

                    @block.scalar
                    def _(act):
                        nc.scalar.activation(qs[:], qT[:, :, bass.ds(tt * P, P)], ACT.Copy).then_inc(S("qs_done"), 1)
                        for b in range(4):
                            act.wait_ge(S("s_mm"), b + 1)
                            nc.scalar.activation(s[:, 4 * b:4 * b + 4, :].rearrange("p a n -> p (a n)"), bank[b][:], ACT.Copy
                                                 ).then_inc(S("s_done"), 1)
                        act.wait_ge(S("soft_x"), 1)
                        nc.scalar.activation(best[:], best[:], ACT.Exp, bias=zero).then_inc(S("soft_e"), 1)
                        act.wait_ge(S("slots_t"), 1)
                        nc.scalar.activation(slots[:].rearrange("p a n -> p (a n)"), bank[4][:, 0:3 * P], ACT.Copy).then_inc(S("slots_done"), 1)
                        act.wait_ge(S("stage_free"), 16 * tt + 16)
                        with act.Fori(0, P // 8) as i:
                            for w in range(2):
                                act.wait_ge(S("g_mm"), 2 * i + w + 1)
                                nc.scalar.activation(stage[:, :, bass.ds(8 * i + 4 * w, 4)],
                                                     bank[6 + w][:].rearrange("p (q n) -> p n q", q=4), ACT.Copy).then_inc(S("g_bank_free"), 1)

                    @block.sync
                    def _(sp):
                        sp.wait_ge(S("g_bank_free"), P // 4 + 2)
                        sp.dma_start(g_dram[:, :, bass.ds(tt * P, P)], stage[:]).then_inc(S("stage_free"), 16)

                    @block.vector
                    def _(dve):
                        def top16(src, n, vals, where, tag):
                            for m in range(n):
                                if tag == "key" and m % 4 == 0:
                                    dve.wait_ge(S("s_done"), m // 4 + 1)
                                nc.vector.max(vals[:, m, 0:8], src[:, m, :]).then_inc(S(f"{tag}_max"), 1)
                            for m in range(n):
                                dve.wait_ge(S(f"{tag}_max"), m + 1)
                                nc.vector.max_index(where[:, m, 0:8], vals[:, m, 0:8], src[:, m, :]).then_inc(S(f"{tag}_idx"), 1)
                                dve.wait_ge(S(f"{tag}_idx"), m + 1)
                                nc.vector.match_replace(src[:, m, :], vals[:, m, 0:8], src[:, m, :], NEG).then_inc(S(f"{tag}_rep"), 1)
                            for m in range(n):
                                dve.wait_ge(S(f"{tag}_rep"), m + 1)
                                nc.vector.max(vals[:, m, 8:16], src[:, m, :]).then_inc(S(f"{tag}_max"), 1)
                            for m in range(n):
                                dve.wait_ge(S(f"{tag}_max"), n + m + 1)
                                nc.vector.max_index(where[:, m, 8:16], vals[:, m, 8:16], src[:, m, :]).then_inc(S(f"{tag}_idx"), 1)
                            dve.wait_ge(S(f"{tag}_idx"), 2 * n)

                        top16(s, QT, top, idx, "key")
                        nc.vector.tensor_copy(idf[:], idx[:]).then_inc(S("idf_done"), 1)
                        nc.vector.tensor_tensor(cand[:].rearrange("p h (k j) -> p h k j", k=TOPK), top[:, 0:QT:2, :].unsqueeze(3).to_broadcast(four),
                                                top[:, 1:QT:2, :].unsqueeze(2).to_broadcast(four), ALU.add).then_inc(S("cand_done"), 1)
                        dve.wait_ge(S("cand_done"), 1)
                        top16(cand, PEER_H, best, pos, "cand")
                        nc.vector.tensor_scalar(pu[:, 0], pos[:], 4, None, ALU.logical_shift_right).then_inc(S("pu_done"), 1)
                        nc.vector.tensor_scalar(pu[:, 1], pos[:], 15, None, ALU.bitwise_and).then_inc(S("pu_done"), 1)
                        sh = [P, PEER_H, TOPK]
                        nc.vector.tensor_copy(ssum[:], best[:, :, 0]).then_inc(S("soft_m"), 1)
                        dve.wait_ge(S("soft_m"), 1)
                        nc.vector.tensor_tensor(best[:], best[:], ssum[:].unsqueeze(2).to_broadcast(sh), ALU.subtract).then_inc(S("soft_x"), 1)
                        dve.wait_ge(S("pu_done"), 2)
                        nc.vector.tensor_copy(pf[:], pu[:]).then_inc(S("pf_done"), 1)
                        dve.wait_ge(S("soft_e"), 1)
                        nc.vector.tensor_reduce(ssum[:], best[:], AX.X, ALU.add).then_inc(S("soft_m"), 1)
                        dve.wait_ge(S("soft_m"), 2)
                        nc.vector.reciprocal(ssum[:], ssum[:]).then_inc(S("soft_m"), 1)
                        dve.wait_ge(S("soft_m"), 3)
                        nc.vector.tensor_tensor(chosen[:, 0, :].rearrange("p (h k) -> p h k", h=PEER_H), best[:],
                                                ssum[:].unsqueeze(2).to_broadcast(sh), ALU.mult).then_inc(S("chosen_done"), 1)
                        dve.wait_ge(S("pf_done"), 1)
                        dve.wait_ge(S("idf_done"), 1)
                        for n in range(2):
                            dve.wait_ge(S("chosen_done"), n + 1)
                            nc.vector.tensor_tensor(eq, pf[:, n].unsqueeze(3).to_broadcast(four),
                                                    cst[:, C_OFF["iota"]:C_OFF["iota"] + TOPK].unsqueeze(1).unsqueeze(1).to_broadcast(four),
                                                    ALU.is_equal).then_inc(S("pick"), 1)
                            dve.wait_ge(S("pick"), 2 * n + 1)
                            nc.vector.tensor_tensor(eq, eq, idf[:, n:QT:2, :].unsqueeze(2).to_broadcast(four), ALU.mult).then_inc(S("pick"), 1)
                            dve.wait_ge(S("pick"), 2 * n + 2)
                            nc.vector.tensor_reduce(chosen[:, 1 + n, :].rearrange("p (h k) -> p h k", h=PEER_H), eq, AX.X, ALU.add
                                                    ).then_inc(S("chosen_done"), 1)
                        dve.wait_ge(S("slots_done"), 1)
                        dve.sem_inc(S("hot_free"), 2)
                        with dve.Fori(0, P // 8) as i:
                            for w in range(2):
                                dve.wait_ge(S("g_bank_free"), 2 * i + w + 1)
                                for q in range(4):
                                    t = bass.ds(8 * i + 4 * w + q, 1)
                                    nc.vector.tensor_scalar(hot[:, 4 * w + q, 0, :], C("iota"), slots[:, 1, t], slots[:, 0, t],
                                                            ALU.is_equal, ALU.mult)
                                    last = nc.vector.tensor_scalar(hot[:, 4 * w + q, 1, :], C("iota"), slots[:, 2, t], None, ALU.is_equal)
                                last.then_inc(S("hot_ready"), 1)
                clear_since(before)
            route.close()

            NT = 4
            with ExitStack() as ph, nc.Block() as block:
                ub = sb(ph, "ub", [P, NT, KD, P])
                vb = sb(ph, "vb", [P, NT, D])
                gb = sb(ph, "gb", [P, NT, T])
                act_w = sb(ph, "act_w", [P, NT, T])
                acc = sb(ph, "acc", [P, KD, T])
                u_d, v_d = lay("u"), a["v"][bass.ds(layer, 1)].rearrange("l i g n -> (l i) g n")
                turns = KEYS // NT

                @block.sync
                def _(sp):
                    for name in ("u_free", "v_free", "gb_free"):
                        sp.sem_inc(S(name), 1)
                    sp.wait_ge(S("stage_free"), 16 * (NC + 1))
                    with sp.Fori(0, turns) as i:
                        sp.wait_ge(S("u_free"), i + 1)
                        sp.dma_start(ub[:].rearrange("p a k n -> p (a k n)"), u_d[bass.ds(i, 1)].rearrange("g p n -> (g p) n")
                                     ).then_inc(S("u_loaded"), 16)
                        sp.wait_ge(S("gb_free"), i + 1)
                        sp.dma_start(gb[:], g_dram[:, bass.ds(NT * i, NT), :]).then_inc(S("gb_loaded"), 16)
                        sp.wait_ge(S("v_free"), i + 1)
                        sp.dma_start(vb[:].rearrange("p a n -> p (a n)"), v_d[:, bass.ds(i, 1), :].rearrange("p g n -> p (g n)")
                                     ).then_inc(S("v_loaded"), 16)

                @block.tensor
                def _(pe):
                    pe.sem_inc(S("hid_bank_free"), 2)
                    pe.sem_inc(S("acc_bank_free"), 4)
                    with pe.Fori(0, turns) as i:
                        pe.wait_ge(S("u_loaded"), 16 * i + 16)
                        for e in range(NT):
                            pe.wait_ge(S("hid_bank_free"), NT * i + e + 1)
                            for k in range(KD):
                                last = nc.tensor.matmul(bank[e % 2][:], ub[:, e, k, :], hT[:, k, :], start=k == 0, stop=k == KD - 1)
                            last.then_inc(S("hid_mm"), 1)
                        pe.wait_ge(S("v_loaded"), 16 * i + 16)
                        for half in range(2):
                            for e in range(NT):
                                if half == 0:
                                    pe.wait_ge(S("act_ready"), NT * i + e + 1)
                                for m in range(4):
                                    d = 4 * half + m
                                    if e == 0:
                                        pe.wait_ge(S("acc_bank_free"), KD * i + d + 1)
                                    last = nc.tensor.matmul(bank[2 + m][:], vb[:, e, d * P:(d + 1) * P], act_w[:, e, :],
                                                            start=e == 0, stop=e == NT - 1)
                                    if e == NT - 1:
                                        last.then_inc(S("out_tile"), 1)

                @block.scalar
                def _(act):
                    act.sem_inc(S("act_free"), 1)
                    with act.Fori(0, turns) as i:
                        act.wait_ge(S("act_free"), i + 1)
                        for e in range(NT):
                            act.wait_ge(S("hid_mm"), NT * i + e + 1)
                            nc.scalar.activation(act_w[:, e, :], bank[e % 2][:], ACT.Gelu_apprx_tanh, bias=zero).then_inc(S("hid_bank_free"), 1)
                        act.wait_ge(S("hid_bank_free"), NT * i + NT + 2)
                        act.sem_inc(S("u_free"), 1)

                @block.vector
                def _(dve):
                    dve.wait_ge(S("stage_free"), 16 * (NC + 1))
                    nc.vector.memset(acc[:], 0.0).then_inc(S("acc_zero"), 1)
                    dve.wait_ge(S("acc_zero"), 1)
                    with dve.Fori(0, turns) as i:
                        dve.wait_ge(S("gb_loaded"), 16 * i + 16)
                        for e in range(NT):
                            dve.wait_ge(S("hid_bank_free"), NT * i + e + 3)
                            nc.vector.tensor_tensor(act_w[:, e, :], act_w[:, e, :], gb[:, e, :], ALU.mult).then_inc(S("act_ready"), 1)
                        dve.wait_ge(S("act_ready"), NT * i + NT)
                        dve.sem_inc(S("gb_free"), 1)
                        for d in range(KD):
                            dve.wait_ge(S("out_tile"), KD * i + d + 1)
                            nc.vector.tensor_tensor(acc[:, d, :], acc[:, d, :], bank[2 + d % 4][:], ALU.add).then_inc(S("acc_bank_free"), 1)
                        dve.wait_ge(S("acc_bank_free"), KD * i + KD + 4)
                        dve.sem_inc(S("v_free"), 1)
                        dve.sem_inc(S("act_free"), 1)
                    for d in range(KD):
                        nc.vector.scalar_tensor_tensor(xT[:, d, :], acc[:, d, :], mod[:, 5 * KD + d:5 * KD + d + 1], xT[:, d, :],
                                                       ALU.mult, ALU.add).then_inc(S("x_ffn"), 1)
                    dve.wait_ge(S("x_ffn"), KD)
            peer.close()
            clear_since(outside)

        with ExitStack() as ph:
            hT = sb(ph, "yT", [P, KD, T])
            norm(hT, "nfin", fnw)
            with nc.Block() as block:
                @block.sync
                def _(sp):
                    sp.dma_start(out, hT[:]).then_inc(S("out_stored"), 16)
                    sp.wait_ge(S("out_stored"), 16)


def _tiles(w):
    L, d, n = w.shape
    return w.reshape(L, d // P, P, n // P, P).transpose(0, 3, 2, 1, 4)


def _col(w):
    return w.reshape(w.shape[0], -1, P).transpose(0, 2, 1)


def _over(w):
    return np.broadcast_to(w[:, None, :], (w.shape[0], P, w.shape[1]))


def layout(i):
    L, B = DEPTH, WIDTH
    w_in = i["w_in"]
    sizes = (B, 768, SSM_H, 3 * B, B, 4, 4, 256, 256, B, B, RANK, B, B, 4 * D)
    at = np.concatenate([[0], np.cumsum(sizes)])
    part = [w_in[:, :, at[n]:at[n + 1]] for n in range(len(sizes))]
    ssm_z, xbc, dt, qkv, gdn_z, beta, decay, gq, gk, gv, gr, glow, lx, lg, merge = part
    cat = np.concatenate
    taps = cat([i["ssm_conv_w"], i["gdn_conv_w"], i["lru_conv_w"]], 2)
    taps = taps.reshape(L, 4, N_CONV, P).transpose(0, 3, 2, 1).reshape(L, P, N_CONV * 4)
    cbias = cat([i["ssm_conv_b"], np.zeros((L, 3 * B), np.float32), i["lru_conv_b"]], 1)
    vecs = cat([_col(i["b_ada"]), _col(i["norm_mix_w"]), _col(i["norm_ffn_w"]), taps, _col(cbias), _col(i["gla_b_gate"]),
                _col(i["lru_b_a"]), _col(i["lru_b_x"]), _col(i["lru_lambda"]), _col(np.repeat(i["ssm_d"], SSM_P, 1)),
                _col(i["ssm_norm_w"]), _col(i["gdn_norm_w"]), _col(i["gla_norm_w"]),
                _over(cat([i["ssm_dt_bias"], i["gdn_dt_bias"]], 1)), _over(cat([i["ssm_a_log"], i["gdn_a_log"]], 1))], 2)
    consts, sel = constants()
    merge = merge.reshape(L, D, 4, KD, P).transpose(0, 1, 3, 2, 4).reshape(L, D, 4 * D)
    return {
        "x": i["x"][0].T.reshape(KD, P, T).transpose(1, 0, 2),
        "c": i["c"][0].reshape(KD, P).T,
        "fnw": i["final_norm_w"].reshape(KD, P).T,
        "consts": consts, "sel": sel, "vecs": vecs,
        "w_ada": _tiles(i["w_ada"]).reshape(L, 12, 4, P, KD * P).transpose(0, 1, 3, 2, 4).reshape(L, 12, P, 4 * KD * P),
        "w_ch": _tiles(cat([xbc, qkv, lx, gq, gk, lg], 2)).reshape(L, N_CH, P, KD * P),
        "w_zt": _tiles(cat([ssm_z, gdn_z, gr, gv], 2)).reshape(L, 4, 4, P, KD * P).transpose(0, 1, 3, 2, 4).reshape(L, 4, P, 4 * KD * P),
        "w_small": cat([dt, decay, beta, glow], 2).reshape(L, KD, P, SMALL).transpose(0, 2, 1, 3),
        "w_merge": _tiles(merge).reshape(L, N_MERGE, P, KD * P),
        "w_gate": i["gla_w_gate"],
        "w_lru": np.stack([i["lru_w_a"], i["lru_w_x"]], 1).reshape(L, 2, 4, 2, 64, 64).transpose(0, 3, 4, 1, 2, 5),
        "w_branch": i["w_branch"].reshape(L, 4, NW, P, KD, P).transpose(0, 4, 1, 3, 2, 5).reshape(L, N_MERGE, P, NW * P),
        "w_out": _tiles(i["w_out"]).reshape(L, KD, P, KD * P),
        "w_q": _tiles(i["peer_w_q"]).reshape(L, QT, P, KD * P),
        "keys": i["peer_sub_keys"].reshape(L, QT, KEYS, P).transpose(0, 3, 1, 2),
        "u": i["peer_u"].reshape(L, KEYS, KEYS // 4, 4, KD, P).transpose(0, 2, 5, 3, 4, 1).reshape(L, KEYS // 4, P, 4 * KD * P),
        "v": i["peer_v"].reshape(L, KEYS, KEYS // 4, 4 * D),
    }


def kernel(**inputs):
    import concourse.bacc as bacc
    from concourse.bass_utils import run_bass_kernel_spmd as run

    nc = bacc.Bacc("TRN2", target_bir_lowering=False, num_devices=1)
    arrays, dram = {}, {}
    for name, x in layout({k: np.asarray(x) for k, x in inputs.items()}).items():
        arrays[f"in_{name}"] = np.ascontiguousarray(x)
        dram[name] = nc.dram_tensor(f"in_{name}", x.shape, F32, kind="ExternalInput").ap()
    out = nc.dram_tensor("out", (P, KD, T), F32, kind="ExternalOutput").ap()
    build(nc, dram, out)
    got = run(nc, [arrays], core_ids=[0]).results[0]["out"]
    return np.ascontiguousarray(got.transpose(1, 0, 2).reshape(D, T).T)[None]
```

```python
from contextlib import ExitStack

import numpy as np
import concourse.bass as bass
from concourse import mybir

F32 = mybir.dt.float32
FR = mybir.dt.float32r
U32 = mybir.dt.uint32
ALU = mybir.AluOpType
ACT = mybir.ActivationFunctionType
AX = mybir.AxisListType

P = 128
DEPTH, D, T = 2, 1024, 512
KD = D // P
NC = T // P
WIDTH = D // 2
NW = WIDTH // P
EPS = 1e-6
SSM_H, SSM_P, SSM_G = 8, 64, 2
GDN_H, GLA_H, GLA_K = 4, 4, 64
NHEAD = SSM_H + GDN_H
GLA_TAU, LRU_C = 16.0, 8.0
RANK = 16
PEER_H, KEYS, TOPK = 8, 128, 16
NHK = PEER_H * TOPK
QT = PEER_H * 2
GT = 32
NT = 4
HEAD = KEYS // 2
HT = HEAD // NC
HPRE = HT // 2

XBC, QKV, LRUX, GQK, LRUG = 6, 12, 4, 4, 4
T_SSM, T_GDN, T_LRUX, T_GLAQ, T_LRUG = 0, 6, 18, 22, 26
N_SILU, N_CONV, N_CH = 18, 22, 30
N_ZT, N_MERGE = 16, 32
SMALL = 32

_V = [("b_ada", 48), ("nmix", 8), ("nffn", 8), ("taps", N_CONV * 4), ("cbias", N_CONV), ("gla_b", 2),
      ("lru_ba", 4), ("lru_bx", 4), ("lru_lam", 4), ("ssm_d", 4), ("ssm_nw", 4), ("gdn_nw", 1),
      ("gla_nw", 1), ("dt_bias", NHEAD), ("a_log", NHEAD)]
V, NV = {}, 0
for _n, _w in _V:
    V[_n] = (NV, NV + _w)
    NV += _w

LEVELS = [2, 4, 8, 16, 32, 64]
CONSTS = ["ident", "ones", "tri", "neg", "iota", "lv1"] + [f"lv{s}" for s in LEVELS]
C_OFF = {n: i * P for i, n in enumerate(CONSTS)}
C_RESET = len(CONSTS) * P
C_EPS = C_RESET + T
NCONST = C_EPS + 2


def constants():
    j, i = np.arange(P)[:, None], np.arange(P)[None, :]
    c = np.zeros((P, NCONST), np.float32)
    c[:, 0:P] = np.eye(P)
    c[:, C_OFF["ones"]:][:, :P] = 1
    c[:, C_OFF["tri"]:][:, :P] = j <= i
    c[:, C_OFF["neg"]:][:, :P] = np.where(j <= i, 0, -1e30)
    c[:, C_OFF["iota"]:][:, :P] = i
    for s in [1] + LEVELS:
        c[:, C_OFF[f"lv{s}"]:][:, :P] = (i // (2 * s) == j // (2 * s)) & (i // s % 2 == 1) & (j // s % 2 == 0)
    c[:, C_RESET:C_RESET + T] = np.arange(T) % P != 0
    c[:, C_EPS] = EPS
    rows = 16
    sel = np.zeros((rows, rows, P), np.float32)
    sel[np.arange(rows), np.arange(rows)] = 1
    return c, sel.reshape(rows, rows * P)


def build(nc, a, out, debug=None):
    debug = debug or {}
    made, names, numbers = {}, [], []

    def S(name):
        if name not in made:
            made[name] = nc.alloc_semaphore(name, num=numbers.pop(0)) if numbers else nc.alloc_semaphore(name)
        return made[name]

    def clear_since(before):
        done = [n for n in made if n not in before]
        nums = sorted(made[n].num for n in done)
        assert nums == list(range(nums[0], nums[0] + len(nums)))
        nc.all_engine_barrier(sems_to_clear=range(nums[0], nums[-1] + 1))
        for n in done:
            nc.release_semaphore(made.pop(n))
        numbers[:] = sorted(numbers + nums)

    def row(t, i):
        return t[:, bass.ds(i, 1), :].rearrange("p a n -> p (a n)")

    g_dram = nc.dram_tensor("routing", (P, T // GT, KEYS, GT), F32, kind="Internal").ap()
    hid_dram = nc.dram_tensor("hidden", (HEAD, P, T), F32, kind="Internal").ap()

    ctx = ExitStack()
    with ctx:
        def sb(stack, name, shape, dt=F32):
            names.append(name)
            return stack.enter_context(nc.sbuf_tensor(f"{name}_{len(names)}", shape, dt))

        bank = [ctx.enter_context(nc.psum_tensor(f"bank{i}", [P, T], F32)) for i in range(8)]
        xT = sb(ctx, "xT", [P, KD, T])
        cst = sb(ctx, "cst", [P, NCONST])
        cact = sb(ctx, "cact", [P, KD])
        vec = sb(ctx, "vec", [P, NV])
        fnw = sb(ctx, "fnw", [P, KD])
        mod = sb(ctx, "mod", [P, 6 * KD])
        gain = sb(ctx, "gain", [P, 2 * KD])
        rinv = sb(ctx, "rinv", [P, T])

        def C(name, n=P):
            return cst[0:n, C_OFF[name]:C_OFF[name] + n]

        def v(name, i=0, n=None):
            lo, hi = V[name]
            return vec[:, lo + i:(lo + i + n) if n else hi]

        eps = cst[:, C_EPS:C_EPS + 1]
        zero = cst[:, C_EPS + 1:C_EPS + 2]

        with nc.Block() as block:
            @block.sync
            def _(sp):
                for dst, src in ((xT[:], a["x"]), (cst[:], a["consts"]), (cact[:], a["c"]), (fnw[:], a["fnw"])):
                    sp.dma_start(dst, src).then_inc(S("start_loaded"), 16)

            @block.scalar
            def _(act):
                act.wait_ge(S("start_loaded"), 64)
                nc.scalar.activation(cact[:], cact[:], ACT.Silu, bias=zero).then_inc(S("c_silu"), 1)
                act.wait_ge(S("c_silu"), 1)

        def mm3(dst, w, x, start, stop):
            nc.tensor.matmul(dst, w[0], x[0], start=start, stop=False)
            nc.tensor.matmul(dst, w[0], x[1], start=False, stop=False)
            return nc.tensor.matmul(dst, w[1], x[0], start=False, stop=stop)

        def norm(hT, tag, g=None, shift=None, split=None):
            sq, ss, mm, rt, rc, nm, dn = (S(f"{tag}_{x}") for x in ("sq", "ss", "mm", "root", "rinv", "scaled", "done"))
            with nc.Block() as block:
                @block.scalar
                def _(act):
                    for k in range(KD):
                        nc.scalar.activation(hT[:, k, :], xT[:, k, :], ACT.Square, bias=zero).then_inc(sq, 1)
                    act.wait_ge(mm, 1)
                    nc.scalar.activation(rinv[:], bank[0][:], ACT.Sqrt, bias=eps, scale=1.0 / D).then_inc(rt, 1)
                    for k in range(KD):
                        act.wait_ge(nm, k + 1)
                        if shift is None:
                            nc.scalar.activation(hT[:, k, :], hT[:, k, :], ACT.Identity, bias=zero,
                                                 scale=g[:, k:k + 1]).then_inc(dn, 1)
                        else:
                            nc.scalar.activation(hT[:, k, :], hT[:, k, :], ACT.Identity, bias=shift[:, k:k + 1],
                                                 scale=g[:, k:k + 1]).then_inc(dn, 1)
                    act.wait_ge(dn, KD)

                @block.tensor
                def _(pe):
                    for k in range(KD):
                        pe.wait_ge(sq, k + 1)
                        last = nc.tensor.matmul(bank[0][:], C("ones"), hT[:, k, :], start=k == 0, stop=k == KD - 1)
                    last.then_inc(mm, 1)

                @block.vector
                def _(dve):
                    dve.wait_ge(rt, 1)
                    nc.vector.reciprocal(rinv[:], rinv[:]).then_inc(rc, 1)
                    dve.wait_ge(rc, 1)
                    for k in range(KD):
                        nc.vector.tensor_tensor(hT[:, k, :], xT[:, k, :], rinv[:], ALU.mult).then_inc(nm, 1)
                    if split:
                        hi, lo = split
                        for k in range(KD):
                            dve.wait_ge(dn, k + 1)
                            nc.vector.tensor_copy(hi[:, k, :], hT[:, k, :]).then_inc(S(f"{tag}_hi"), 1)
                            dve.wait_ge(S(f"{tag}_hi"), k + 1)
                            nc.vector.tensor_tensor(lo[:, k, :], hT[:, k, :], hi[:, k, :].bitcast(F32), ALU.subtract
                                                    ).then_inc(S(f"{tag}_lo"), 1)
                        dve.wait_ge(S(f"{tag}_lo"), KD)

        with nc.Fori(0, DEPTH) as layer:
            outside = set(made)

            def lay(name):
                t = a[name]
                dims = " ".join(f"d{i}" for i in range(len(t.shape)))
                rest = dims[3:]
                return t[bass.ds(layer, 1)].rearrange(f"{dims} -> (d0 {rest.split(' ')[0]}) {' '.join(rest.split(' ')[1:])}")

            w_ada = lay("w_ada")
            with ExitStack() as ph, nc.Block() as block:
                wa = [sb(ph, f"wa{u}", [P, 2 * D]) for u in range(4)]
                wsum = sb(ph, "wsum", [P, 2 * D])

                @block.sync
                def _(sp):
                    sp.dma_start(vec[:], lay("vecs")).then_inc(S("vec_loaded"), 16)
                    for k in range(KD):
                        if k >= 4:
                            sp.wait_ge(S("ada_row"), k - 3)
                        sp.dma_start(wa[k % 4][:], w_ada[k, :, 0:2 * D]).then_inc(S(f"ada_loaded{k % 4}"), 16)

                @block.vector
                def _(dve):
                    for k in range(KD):
                        dve.wait_ge(S(f"ada_loaded{k % 4}"), 16 * (k // 4) + 16)
                        if k == 0:
                            nc.vector.tensor_scalar(wsum[:], wa[0][:], cact[:, 0:1], None, ALU.mult).then_inc(S("ada_row"), 1)
                        else:
                            dve.wait_ge(S("ada_row"), k)
                            nc.vector.scalar_tensor_tensor(wsum[:], wa[k % 4][:], cact[:, k:k + 1], wsum[:], ALU.mult, ALU.add
                                                           ).then_inc(S("ada_row"), 1)
                    dve.wait_ge(S("vec_loaded"), 16)
                    dve.wait_ge(S("ada_mm"), 1)
                    nc.vector.tensor_tensor(mod[:, 0:2 * KD], bank[0][:, 0:2 * KD], v("b_ada", 0, 2 * KD), ALU.add).then_inc(S("mod_done"), 1)
                    dve.wait_ge(S("mod_done"), 1)
                    nc.vector.scalar_tensor_tensor(gain[:, 0:KD], mod[:, KD:2 * KD], 1.0, v("nmix"), ALU.add, ALU.mult
                                                   ).then_inc(S("gain_done"), 1)
                    dve.wait_ge(S("gain_done"), 1)

                @block.tensor
                def _(pe):
                    pe.wait_ge(S("ada_row"), KD)
                    for m in range(2 * KD):
                        last = nc.tensor.matmul(bank[0][:, m:m + 1], wsum[:, m * P:(m + 1) * P], cst[:, C_OFF["ones"]:C_OFF["ones"] + 1],
                                                start=True, stop=True)
                    last.then_inc(S("ada_mm"), 1)

            mix = ExitStack()
            hT = sb(mix, "hT", [P, KD, T])
            clear_since(outside)
            norm(hT, "nmix", gain[:, 0:KD], mod[:, 0:KD])
            ch = sb(mix, "ch", [P, N_CH, T])
            mixers = ExitStack()
            zt = sb(mixers, "zt", [P, 4, NC, WIDTH])
            wsm = sb(mixers, "wsm", [P, KD, SMALL])
            small = sb(mixers, "small", [P, NC, 16])
            low = sb(mixers, "low", [RANK, T])

            with ExitStack() as ph, nc.Block() as block:
                wc = [sb(ph, f"wc{u}", [P, KD, P]) for u in range(2)]
                wz = sb(ph, "wz", [P, 4, KD, P])
                raw = [sb(ph, f"raw{u}", [P, T + 3]) for u in range(2)]
                y = [sb(ph, f"y{u}", [P, T]) for u in range(2)]
                w_ch, w_zt = lay("w_ch"), lay("w_zt")
                wa = [sb(ph, f"wa{u}", [P, 2 * D]) for u in range(2)]
                wsum = sb(ph, "wsum", [P, 2, 2 * D])

                @block.sync
                def _(sp):
                    sp.sem_inc(S("wc_free"), 2)
                    sp.sem_inc(S("wz_free"), 1)
                    sp.dma_start(wsm[:], lay("w_small")).then_inc(S("wsm_loaded"), 16)
                    sp.sem_inc(S("ada_free"), 2)

                    def load(i, u):
                        sp.wait_ge(S("wc_free"), 2 * i + u + 1)
                        sp.dma_start(wc[u][:].rearrange("p k n -> p (k n)"),
                                     w_ch[bass.ds(2 * i + u, 1)].rearrange("g p n -> (g p) n")
                                     ).then_inc(S(f"wc_loaded{u}"), 16)

                    with sp.Fori(0, KD) as i:
                        for u in range(2):
                            load(i, u)
                        for u in range(2):
                            sp.wait_ge(S("ada_free"), 2 * i + u + 1)
                            sp.dma_start(wa[u][:], w_ada[bass.ds(i, 1), :, 2 * D * (u + 1):2 * D * (u + 2)].rearrange("k p n -> (k p) n")
                                         ).then_inc(S(f"ada_loaded{u}"), 16)
                    with sp.Fori(KD, N_CH // 2) as i:
                        for u in range(2):
                            load(i, u)
                    with sp.Fori(0, 4) as i:
                        sp.wait_ge(S("wz_free"), i + 1)
                        sp.dma_start(wz[:].rearrange("p a k n -> p (a k n)"),
                                     w_zt[bass.ds(i, 1)].rearrange("g p n -> (g p) n")).then_inc(S("wz_loaded"), 16)

                @block.tensor
                def _(pe):
                    pe.sem_inc(S("ch_bank_free"), 2)
                    with pe.Fori(0, N_CH // 2) as i:
                        for u in range(2):
                            pe.wait_ge(S(f"wc_loaded{u}"), 16 * i + 16)
                            pe.wait_ge(S("ch_bank_free"), 2 * i + u + 1)
                            for k in range(KD):
                                last = nc.tensor.matmul(bank[u][:], wc[u][:, k, :], hT[:, k, :], start=k == 0, stop=k == KD - 1)
                            last.then_inc(S("ch_mm"), 1)
                    pe.wait_ge(S("wsm_loaded"), 16)
                    for t in range(NC):
                        for k in range(KD):
                            last = nc.tensor.matmul(bank[6][:, t * 16:t * 16 + 16], hT[:, k, t * P:(t + 1) * P],
                                                    wsm[:, k, 0:16], start=k == 0, stop=k == KD - 1)
                    last.then_inc(S("small_mm"), 1)
                    for k in range(KD):
                        last = nc.tensor.matmul(bank[7][0:RANK, :], wsm[:, k, 16:32], hT[:, k, :], start=k == 0, stop=k == KD - 1)
                    last.then_inc(S("low_mm"), 1)
                    pe.sem_inc(S("zt_bank_free"), 4)
                    with pe.Fori(0, 4) as i:
                        pe.wait_ge(S("wz_loaded"), 16 * i + 16)
                        for t in range(NC):
                            pe.wait_ge(S("zt_bank_free"), 4 * i + t + 1)
                            for k in range(KD):
                                last = nc.tensor.matmul(bank[2 + t][:], hT[:, k, t * P:(t + 1) * P], wz[:, :, k, :],
                                                        start=k == 0, stop=k == KD - 1)
                            last.then_inc(S("zt_mm"), 1)
                    pe.wait_ge(S("ada_row"), 2 * KD)
                    for m in range(4 * KD):
                        last = nc.tensor.matmul(bank[0][:, m:m + 1], wsum[:, m // (2 * KD), m % (2 * KD) * P:(m % (2 * KD) + 1) * P], cst[:, C_OFF["ones"]:C_OFF["ones"] + 1],
                                                start=True, stop=True)
                    last.then_inc(S("ada_mm"), 1)

                @block.scalar
                def _(act):
                    act.sem_inc(S("raw_free"), 2)

                    def evacuate(n, u):
                        act.wait_ge(S("ch_mm"), n + 1)
                        act.wait_ge(S("raw_free"), n + 1)
                        nc.scalar.activation(raw[u][:, 3:], bank[u][:], ACT.Copy).then_inc(S("ch_bank_free"), 1)
                        act.wait_ge(S("ch_bank_free"), n + 3)
                        act.sem_inc(S("wc_free"), 1)
                        act.sem_inc(S("raw_ready"), 1)

                    with act.Fori(0, N_SILU // 2) as i:
                        for u in range(2):
                            evacuate(2 * i + u, u)
                        for u in range(2):
                            act.wait_ge(S("conv_done"), 2 * i + u + 1)
                            nc.scalar.activation(row(ch, 2 * i + u), y[u][:], ACT.Silu, bias=zero).then_inc(S("y_free"), 1)
                    with act.Fori(N_SILU // 2, N_CONV // 2) as i:
                        for u in range(2):
                            evacuate(2 * i + u, u)
                    with act.Fori(N_CONV // 2, N_CH // 2) as i:
                        for u in range(2):
                            act.wait_ge(S("ch_mm"), 2 * i + u + 1)
                            nc.scalar.activation(row(ch, 2 * i + u), bank[u][:], ACT.Copy).then_inc(S("ch_bank_free"), 1)
                            act.wait_ge(S("ch_bank_free"), 2 * i + u + 3)
                            act.sem_inc(S("wc_free"), 1)
                    act.wait_ge(S("low_mm"), 1)
                    nc.scalar.activation(low[:], bank[7][0:RANK, :], ACT.Copy).then_inc(S("low_done"), 1)
                    with act.Fori(0, 4) as i:
                        for t in range(NC):
                            act.wait_ge(S("zt_mm"), 4 * i + t + 1)
                            nc.scalar.activation(zt[:, bass.ds(i, 1), t, :].rearrange("p a n -> p (a n)"), bank[2 + t][:], ACT.Copy
                                                 ).then_inc(S("zt_bank_free"), 1)
                        act.wait_ge(S("zt_bank_free"), 4 * i + 8)
                        act.sem_inc(S("wz_free"), 1)

                @block.vector
                def _(dve):
                    for u in range(2):
                        nc.vector.memset(raw[u][:, 0:3], 0.0).then_inc(S("pad_zero"), 1)
                    dve.wait_ge(S("pad_zero"), 2)
                    dve.sem_inc(S("y_free"), 2)
                    first, bias = V["taps"][0], V["cbias"][0]

                    def conv(n, u, dst, reuse):
                        dve.wait_ge(S("raw_ready"), n + 1)
                        if reuse:
                            dve.wait_ge(S("y_free"), n + 1)
                        nc.vector.tensor_scalar(dst, raw[u][:, 3:], vec[:, bass.ds(first + 4 * n + 3, 1)],
                                                vec[:, bass.ds(bias + n, 1)], ALU.mult, ALU.add).then_inc(S("tap_done"), 1)
                        for j in range(3):
                            dve.wait_ge(S("tap_done"), 3 * n + j + 1)
                            ins = nc.vector.scalar_tensor_tensor(dst, raw[u][:, j:j + T], vec[:, bass.ds(first + 4 * n + j, 1)],
                                                                 dst, ALU.mult, ALU.add)
                            ins.then_inc(S("tap_done") if j < 2 else S("conv_done"), 1)
                        dve.wait_ge(S("conv_done"), n + 1)
                        dve.sem_inc(S("raw_free"), 1)

                    nc.vector.memset(wsum[:], 0.0).then_inc(S("wsum_zero"), 1)
                    dve.wait_ge(S("wsum_zero"), 1)
                    with dve.Fori(0, KD) as i:
                        for u in range(2):
                            conv(2 * i + u, u, y[u][:], True)
                        for u in range(2):
                            dve.wait_ge(S(f"ada_loaded{u}"), 16 * i + 16)
                            nc.vector.scalar_tensor_tensor(wsum[:, u, :], wa[u][:], cact[:, bass.ds(i, 1)], wsum[:, u, :], ALU.mult, ALU.add
                                                           ).then_inc(S("ada_row"), 1)
                            dve.wait_ge(S("ada_row"), 2 * i + u + 1)
                            dve.sem_inc(S("ada_free"), 1)
                    for n in range(2 * KD, N_SILU):
                        conv(n, n % 2, y[n % 2][:], True)
                    with dve.Fori(N_SILU // 2, N_CONV // 2) as i:
                        for u in range(2):
                            conv(2 * i + u, u, row(ch, 2 * i + u), False)
                    dve.wait_ge(S("small_mm"), 1)
                    nc.vector.tensor_copy(small[:].rearrange("p t n -> p (t n)"), bank[6][:, 0:NC * 16]).then_inc(S("small_done"), 1)
                    dve.wait_ge(S("ada_mm"), 1)
                    nc.vector.tensor_tensor(mod[:, 2 * KD:], bank[0][:, 0:4 * KD], v("b_ada", 2 * KD, 4 * KD), ALU.add).then_inc(S("mod_done"), 1)
                    dve.wait_ge(S("mod_done"), 1)
                    nc.vector.scalar_tensor_tensor(gain[:, KD:], mod[:, 4 * KD:5 * KD], 1.0, v("nffn"), ALU.add, ALU.mult
                                                   ).then_inc(S("gain_done"), 1)
                    dve.wait_ge(S("gain_done"), 1)

            clear_since(outside)

            sm = ExitStack()
            dec = sb(sm, "dec", [P, NC, 16])
            dts = sb(sm, "dts", [P, NC * NHEAD + 4])
            ecol = sb(sm, "ecol", [P, NC * NHEAD])
            etot = sb(sm, "etot", [P, NC * NHEAD])
            rows = sb(sm, "rows", [16, T])
            sel = sb(sm, "sel", [16, 16 * P])
            NS = NC * NHEAD
            with ExitStack() as ph, nc.Block() as block:
                t = [sb(ph, f"sp{i}", [P, NS + 4]) for i in range(7)]
                x, nab, z, w, ln, one, den = (q[:] for q in t)
                ea = sb(ph, "ea", [P, NHEAD])
                da = sb(ph, "da", [P, NS])
                per_head = [P, NC, NHEAD]

                @block.sync
                def _(sp):
                    sp.dma_start(sel[:], a["sel"]).then_inc(S("sel_loaded"), 16)
                    sp.wait_ge(S("sel_loaded"), 16)

                @block.vector
                def _(dve):
                    nc.vector.tensor_tensor(x[:, 0:NS].rearrange("p (t h) -> p t h", t=NC), small[:, :, 0:NHEAD],
                                            v("dt_bias").unsqueeze(1).to_broadcast(per_head), ALU.add).then_inc(S("sp_x"), 1)
                    nc.vector.tensor_scalar(x[:, NS:], v("lru_lam"), -1.0, None, ALU.mult).then_inc(S("sp_x"), 1)
                    dve.wait_ge(S("sp_x"), 2)
                    nc.vector.scalar_tensor_tensor(nab, x, -1.0, x, ALU.mult, ALU.min).then_inc(S("sp_nab"), 1)
                    dve.wait_ge(S("sp_z"), 1)
                    nc.vector.tensor_scalar(w, z, 1.0, None, ALU.add).then_inc(S("sp_w"), 1)
                    dve.wait_ge(S("sp_w"), 1)
                    nc.vector.tensor_scalar(one, w, 1.0, None, ALU.is_equal).then_inc(S("sp_d"), 1)
                    dve.wait_ge(S("sp_d"), 1)
                    nc.vector.scalar_tensor_tensor(den, w, -1.0, one, ALU.add, ALU.add).then_inc(S("sp_d"), 1)
                    dve.wait_ge(S("sp_d"), 2)
                    nc.vector.reciprocal(den, den).then_inc(S("sp_d"), 1)
                    dve.wait_ge(S("sp_ln"), 1)
                    nc.vector.tensor_tensor(ln, ln, one, ALU.add).then_inc(S("sp_d"), 1)
                    dve.wait_ge(S("sp_d"), 4)
                    nc.vector.tensor_tensor(ln, ln, den, ALU.mult).then_inc(S("sp_d"), 1)
                    dve.wait_ge(S("sp_d"), 5)
                    nc.vector.tensor_tensor(ln, ln, z, ALU.mult).then_inc(S("sp_d"), 1)
                    dve.wait_ge(S("sp_d"), 6)
                    nc.vector.scalar_tensor_tensor(dts[:], x, 0.0, ln, ALU.max, ALU.add).then_inc(S("sp_d"), 1)
                    dve.wait_ge(S("sp_d"), 7)
                    dve.wait_ge(S("ea_done"), 1)
                    nc.vector.scalar_tensor_tensor(da[:].rearrange("p (t h) -> p t h", t=NC),
                                                   dts[:, 0:NS].rearrange("p (t h) -> p t h", t=NC), -1.0,
                                                   ea[:].unsqueeze(1).to_broadcast(per_head), ALU.mult, ALU.mult
                                                   ).then_inc(S("da_done"), 1)
                    dve.wait_ge(S("decay_mm"), 2)
                    nc.vector.tensor_copy(dec[:, :, 0:NHEAD], bank[0][:, 0:NS].rearrange("p (t h) -> p t h", t=NC)
                                          ).then_inc(S("dec_done"), 1)
                    dve.wait_ge(S("decay_mm"), 3)
                    nc.vector.tensor_copy(rows[:], bank[2][0:16, :]).then_inc(S("rows_done"), 1)
                    dve.wait_ge(S("rows_done"), 1)

                @block.scalar
                def _(act):
                    nc.scalar.activation(ea[:], v("a_log"), ACT.Exp, bias=zero).then_inc(S("ea_done"), 1)
                    act.wait_ge(S("sp_nab"), 1)
                    nc.scalar.activation(z, nab, ACT.Exp, bias=zero).then_inc(S("sp_z"), 1)
                    act.wait_ge(S("sp_w"), 1)
                    nc.scalar.activation(ln, w, ACT.Ln, bias=zero).then_inc(S("sp_ln"), 1)
                    act.wait_ge(S("decay_mm"), 2)
                    act.wait_ge(S("dec_done"), 1)
                    nc.scalar.activation(ecol[:], dec[:, :, 0:NHEAD], ACT.Exp, bias=zero).then_inc(S("ecol_done"), 1)
                    nc.scalar.activation(etot[:], bank[1][:, 0:NS], ACT.Exp, bias=zero).then_inc(S("ecol_done"), 1)
                    nc.scalar.activation(dec[:, :, NHEAD:16], small[:, :, NHEAD:16], ACT.Sigmoid, bias=zero).then_inc(S("beta_done"), 1)

                @block.tensor
                def _(pe):
                    pe.wait_ge(S("da_done"), 1)
                    nc.tensor.matmul(bank[0][:, 0:NS], C("tri"), da[:], start=True, stop=True).then_inc(S("decay_mm"), 1)
                    nc.tensor.matmul(bank[1][:, 0:NS], C("ones"), da[:], start=True, stop=True).then_inc(S("decay_mm"), 1)
                    pe.wait_ge(S("dec_done"), 1)
                    pe.wait_ge(S("beta_done"), 1)
                    for c in range(NC):
                        last = nc.tensor.transpose(bank[2][0:16, c * P:(c + 1) * P], dec[:, c, :], C("ident"))
                    last.then_inc(S("decay_mm"), 1)

            def decays(tmp, DT, first, n, tag, EG=None):
                def pe_part(pe):
                    for h in range(n):
                        if h >= 4:
                            pe.wait_ge(S(f"{tag}_bc_free"), h - 3)
                        nc.tensor.matmul(bank[4 + h % 4][:], sel[:, (first + h) * P:(first + h + 1) * P], rows[:],
                                         start=True, stop=True).then_inc(S(f"{tag}_bc"), 1)

                def dve_part(dve):
                    for h in range(n):
                        dve.wait_ge(S(f"{tag}_bc"), h + 1)
                        if EG is not None:
                            dve.wait_ge(S(f"{tag}_eg"), h + 1)
                        if h >= 2:
                            dve.wait_ge(S(f"{tag}_dt"), h - 1)
                        for c in range(NC):
                            last = nc.vector.scalar_tensor_tensor(tmp[h % 2][:, c * P:(c + 1) * P], bank[4 + h % 4][:, c * P:(c + 1) * P],
                                                                  dec[:, c, first + h:first + h + 1], C("neg"),
                                                                  ALU.subtract, ALU.add)
                        last.then_inc(S(f"{tag}_bc_free"), 1)

                def act_part(act):
                    for h in range(n):
                        if EG is not None:
                            act.wait_ge(S(f"{tag}_bc"), h + 1)
                            nc.scalar.activation(EG[:, h, :], bank[4 + h % 4][:], ACT.Exp, bias=zero).then_inc(S(f"{tag}_eg"), 1)
                        act.wait_ge(S(f"{tag}_bc_free"), h + 1)
                        nc.scalar.activation(DT[:, h, :], tmp[h % 2], ACT.Exp, bias=zero).then_inc(S(f"{tag}_dt"), 1)
                return pe_part, dve_part, act_part

            def finish(o, zi, groups, after_gate, nw, dst, tag):
                n = WIDTH // groups
                with ExitStack() as ph, nc.Block() as block:
                    sq = [sb(ph, f"sq{u}", [P, WIDTH]) for u in range(2)]
                    ms = sb(ph, "ms", [P, NC * groups])

                    @block.scalar
                    def _(act):
                        for c in range(NC):
                            nc.scalar.activation(zt[:, zi, c, :], zt[:, zi, c, :], ACT.Silu, bias=zero).then_inc(S(f"{tag}_sz"), 1)
                        act.wait_ge(S(f"{tag}_ms"), NC)
                        nc.scalar.activation(ms[:], ms[:], ACT.Sqrt, bias=eps, scale=1.0 / n).then_inc(S(f"{tag}_rms"), 1)
                        for m in range(NW):
                            act.wait_ge(S(f"{tag}_yt"), m + 1)
                            nc.scalar.activation(ch[:, dst + m, :], bank[m][:], ACT.Identity, bias=zero,
                                                 scale=nw[:, m:m + 1] if groups == 1 else nw[:, 0:1]).then_inc(S(f"{tag}_y"), 1)
                        act.wait_ge(S(f"{tag}_y"), NW)

                    @block.vector
                    def _(dve):
                        def gate(c):
                            dve.wait_ge(S(f"{tag}_sz"), c + 1)
                            nc.vector.tensor_tensor(o[:, c, :], o[:, c, :], zt[:, zi, c, :], ALU.mult).then_inc(S(f"{tag}_gated"), 1)

                        for c in range(NC):
                            if after_gate:
                                gate(c)
                                dve.wait_ge(S(f"{tag}_gated"), c + 1)
                            if c >= 2:
                                dve.wait_ge(S(f"{tag}_ms"), c - 1)
                            nc.vector.tensor_tensor(sq[c % 2][:], o[:, c, :], o[:, c, :], ALU.mult).then_inc(S(f"{tag}_sq"), 1)
                            if not after_gate:
                                dve.wait_ge(S(f"{tag}_sq"), c + 1)
                                gate(c)
                            dve.wait_ge(S(f"{tag}_sq"), c + 1)
                            nc.vector.tensor_reduce(ms[:, c * groups:(c + 1) * groups],
                                                    sq[c % 2][:].rearrange("p (g n) -> p g n", g=groups), AX.X, ALU.add
                                                    ).then_inc(S(f"{tag}_ms"), 1)
                        dve.wait_ge(S(f"{tag}_rms"), 1)
                        nc.vector.reciprocal(ms[:], ms[:]).then_inc(S(f"{tag}_rinv"), 1)
                        dve.wait_ge(S(f"{tag}_rinv"), 1)
                        dve.wait_ge(S(f"{tag}_gated"), NC)
                        for c in range(NC):
                            if groups == 1:
                                ins = nc.vector.tensor_scalar(o[:, c, :], o[:, c, :], ms[:, c:c + 1], None, ALU.mult)
                            else:
                                r = ms[:, c * groups:(c + 1) * groups].unsqueeze(2).to_broadcast([P, groups, n])
                                og = o[:, c, :].rearrange("p (g n) -> p g n", g=groups)
                                ins = nc.vector.tensor_tensor(og, og, r, ALU.mult)
                            ins.then_inc(S(f"{tag}_normed"), 1)

                    @block.tensor
                    def _(pe):
                        pe.wait_ge(S(f"{tag}_normed"), NC)
                        for m in range(NW):
                            for c in range(NC):
                                last = nc.tensor.transpose(bank[m][:, c * P:(c + 1) * P], o[:, c, m * P:(m + 1) * P], C("ident"))
                            last.then_inc(S(f"{tag}_yt"), 1)

            clear_since(outside)

            with ExitStack() as ssd:
                DT = sb(ssd, "ssd_DT", [P, SSM_H, T])
                xw = sb(ssd, "xw", [P, NC, WIDTH])
                o = xw
                G4 = SSM_H // SSM_G
                with ExitStack() as ph, nc.Block() as block:
                    xdt = sb(ph, "xdt", [P, NC, WIDTH])
                    btok = sb(ph, "btok", [P, NC, P])
                    cb = sb(ph, "cb", [P, NC * SSM_G, P])
                    dskip = sb(ph, "dskip", [P, NW, P])
                    st = sb(ph, "st", [P, NC - 1, SSM_G, G4 * SSM_P])
                    at = [sb(ph, f"at{u}", [P, SSM_H, P]) for u in range(2)]
                    tmp = [q[:, 0:4, :].rearrange("p h n -> p (h n)") for q in at]
                    pe_dt, dve_dt, act_dt = decays(tmp, DT, 0, SSM_H, "ssd")
                    chunk = [slice(c * P, (c + 1) * P) for c in range(NC)]
                    half = [slice(g * SSM_P, (g + 1) * SSM_P) for g in range(SSM_G)]
                    GW = G4 * SSM_P

                    @block.tensor
                    def _(pe):
                        for c in range(NC):
                            for m in range(NW):
                                last = nc.tensor.transpose(bank[c][:, m * P:(m + 1) * P], ch[:, m, chunk[c]], C("ident"))
                            last.then_inc(S("ssd_xt"), 1)
                        pe_dt(pe)
                        pe.wait_ge(S("ssd_bc_free"), SSM_H)
                        for c in range(NC):
                            last = nc.tensor.transpose(bank[4][:, chunk[c]], ch[:, 4, chunk[c]], C("ident"))
                        last.then_inc(S("ssd_bt"), 1)
                        for c in range(NC):
                            for g in range(SSM_G):
                                last = nc.tensor.matmul(bank[5 + g][:, chunk[c]], ch[half[g], 4, chunk[c]],
                                                        ch[half[g], 5, chunk[c]], start=True, stop=True)
                        last.then_inc(S("ssd_cb"), 1)
                        pe.wait_ge(S("ssd_btok"), 1)
                        pe.wait_ge(S("ssd_xdt"), NC)
                        for c in range(NC - 1):
                            pe.wait_ge(S("ssd_xw"), c + 1)
                            for g in range(SSM_G):
                                last = nc.tensor.matmul(bank[c // 2][half[g], (c % 2) * GW:(c % 2 + 1) * GW], btok[:, c, half[g]],
                                                        xw[:, c, g * GW:(g + 1) * GW], start=True, stop=True)
                        last.then_inc(S("ssd_st_mm"), 1)
                        pe.wait_ge(S("ssd_skip"), NW)
                        pe.wait_ge(S("ssd_cbs"), 2)
                        for c in range(NC):
                            if c >= 2:
                                pe.wait_ge(S("ssd_o"), c - 1)
                            if c >= 1:
                                pe.wait_ge(S("ssd_state"), 2 * c)
                                nc.tensor.matmul(bank[5 + c % 2][:], ch[:, 5, chunk[c]], st[:, c - 1].rearrange("p g n -> p (g n)"),
                                                 start=True, stop=True).then_inc(S("ssd_yoff"), 1)
                            for m in range(NW):
                                nc.tensor.matmul(bank[2 + c % 2][:, m * P:(m + 1) * P], ch[:, m, chunk[c]], dskip[:, m, :],
                                                 start=m == 0, stop=False, skip_group_check=True)
                            pe.wait_ge(S("ssd_at"), 2 * c + 2)
                            for h in range(SSM_H):
                                last = nc.tensor.matmul(bank[2 + c % 2][:, h * SSM_P:(h + 1) * SSM_P], at[c % 2][:, h, :],
                                                        xdt[:, c, h * SSM_P:(h + 1) * SSM_P], start=False, stop=h == SSM_H - 1,
                                                        skip_group_check=True)
                            last.then_inc(S("ssd_ydiag"), 1)

                    @block.scalar
                    def _(act):
                        act_dt(act)
                        act.wait_ge(S("ssd_bt"), 1)
                        nc.scalar.activation(btok[:].rearrange("p c n -> p (c n)"), bank[4][:], ACT.Copy).then_inc(S("ssd_btok"), 1)
                        act.wait_ge(S("ssd_cb"), 1)
                        for b in range(2):
                            nc.scalar.activation(cb[:, 4 * b:4 * b + 4, :].rearrange("p c n -> p (c n)"), bank[5 + b][:], ACT.Copy
                                                 ).then_inc(S("ssd_cbs"), 1)

                    @block.vector
                    def _(dve):
                        for m in range(NW):
                            nc.vector.tensor_scalar(dskip[:, m, :], C("ident"), v("ssm_d", m, 1), None, ALU.mult).then_inc(S("ssd_skip"), 1)
                        per = [P, SSM_H, SSM_P]
                        for c in range(NC):
                            dve.wait_ge(S("ssd_xt"), c + 1)
                            nc.vector.tensor_tensor(xdt[:, c, :].rearrange("p (h n) -> p h n", h=SSM_H),
                                                    bank[c][:].rearrange("p (h n) -> p h n", h=SSM_H),
                                                    dts[:, c * NHEAD:c * NHEAD + SSM_H].unsqueeze(2).to_broadcast(per), ALU.mult
                                                    ).then_inc(S("ssd_xdt"), 1)
                        dve_dt(dve)
                        dve.wait_ge(S("ssd_dt"), SSM_H)
                        dve.wait_ge(S("ssd_xdt"), NC)
                        for c in range(NC - 1):
                            nc.vector.tensor_tensor(xw[:, c, :].rearrange("p (h n) -> p h n", h=SSM_H),
                                                    xdt[:, c, :].rearrange("p (h n) -> p h n", h=SSM_H),
                                                    DT[:, :, c * P + P - 1:c * P + P].to_broadcast(per), ALU.mult
                                                    ).then_inc(S("ssd_xw"), 1)
                        nc.vector.memset(st[:], 0.0).then_inc(S("ssd_zero"), 1)
                        dve.wait_ge(S("ssd_zero"), 1)
                        dve.wait_ge(S("ssd_st_mm"), 1)
                        for g in range(SSM_G):
                            nc.vector.tensor_copy(st[half[g], 0, g, :], bank[0][half[g], 0:GW]).then_inc(S("ssd_state"), 1)
                        n = 0
                        for c in range(1, NC - 1):
                            dve.wait_ge(S("ssd_state"), 2 * c)
                            for g in range(SSM_G):
                                e = etot[half[g], c * NHEAD + g * G4:c * NHEAD + (g + 1) * G4].unsqueeze(2).to_broadcast([SSM_P, G4, SSM_P])
                                nc.vector.tensor_tensor(st[half[g], c, g, :].rearrange("p (h n) -> p h n", h=G4),
                                                        st[half[g], c - 1, g, :].rearrange("p (h n) -> p h n", h=G4), e, ALU.mult
                                                        ).then_inc(S("ssd_decayed"), 1)
                            n += 2
                            dve.wait_ge(S("ssd_decayed"), n)
                            for g in range(SSM_G):
                                nc.vector.tensor_tensor(st[half[g], c, g, :], st[half[g], c, g, :],
                                                        bank[c // 2][half[g], (c % 2) * GW:(c % 2 + 1) * GW], ALU.add
                                                        ).then_inc(S("ssd_state"), 1)
                        dve.wait_ge(S("ssd_cbs"), 2)
                        for c in range(NC):
                            if c >= 2:
                                dve.wait_ge(S("ssd_ydiag"), c - 1)
                            for g in range(SSM_G):
                                nc.vector.tensor_tensor(at[c % 2][:, g * G4:(g + 1) * G4, :], DT[:, g * G4:(g + 1) * G4, chunk[c]],
                                                        cb[:, NC * g + c, :].unsqueeze(1).to_broadcast([P, G4, P]), ALU.mult
                                                        ).then_inc(S("ssd_at"), 1)
                            if c >= 1:
                                dve.wait_ge(S("ssd_yoff"), c)
                                nc.vector.tensor_tensor(o[:, c, :].rearrange("p (h n) -> p h n", h=SSM_H),
                                                        bank[5 + c % 2][:].rearrange("p (h n) -> p h n", h=SSM_H),
                                                        ecol[:, c * NHEAD:c * NHEAD + SSM_H].unsqueeze(2).to_broadcast(per), ALU.mult
                                                        ).then_inc(S("ssd_yo"), 1)
                                dve.wait_ge(S("ssd_yo"), c)
                            dve.wait_ge(S("ssd_ydiag"), c + 1)
                            if c == 0:
                                nc.vector.tensor_copy(o[:, c, :], bank[2][:]).then_inc(S("ssd_o"), 1)
                            else:
                                nc.vector.tensor_tensor(o[:, c, :], o[:, c, :], bank[2 + c % 2][:], ALU.add).then_inc(S("ssd_o"), 1)
                finish(o, 0, 1, True, v("ssm_nw"), T_SSM, "ssdf")

            clear_since(outside)

            with ExitStack() as gdn:
                DT = sb(gdn, "gdn_DT", [P, GDN_H, T])
                qg = sb(gdn, "qg", [P, GDN_H, T])
                MT = sb(gdn, "MT", [P, GDN_H, T])
                XT = sb(gdn, "XT", [P, GDN_H, T])
                X = zt[:, 0]
                MS = sb(gdn, "MS", [P, GDN_H, T])
                Y = sb(gdn, "Y", [P, GDN_H, T])
                q_t, k_t, v_t = T_GDN, T_GDN + 4, T_GDN + 8
                with ExitStack() as ph, nc.Block() as block:
                    sq = [sb(ph, f"sq{u}", [P, T]) for u in range(2)]
                    rn = [sb(ph, f"rn{u}", [P, T]) for u in range(2)]

                    @block.scalar
                    def _(act):
                        for n in range(8):
                            if n >= 2:
                                act.wait_ge(S("qk_ss"), n - 1)
                            nc.scalar.activation(sq[n % 2][:], ch[:, T_GDN + n, :], ACT.Square, bias=zero).then_inc(S("qk_sq"), 1)
                            if n >= 1:
                                act.wait_ge(S("qk_ss"), n)
                                if n >= 3:
                                    act.wait_ge(S("qk_done"), n - 2)
                                nc.scalar.activation(rn[(n - 1) % 2][:], bank[(n - 1) % 2][:], ACT.Sqrt, bias=eps).then_inc(S("qk_root"), 1)
                        act.wait_ge(S("qk_ss"), 8)
                        act.wait_ge(S("qk_done"), 6)
                        nc.scalar.activation(rn[1][:], bank[1][:], ACT.Sqrt, bias=eps).then_inc(S("qk_root"), 1)

                    @block.tensor
                    def _(pe):
                        for n in range(8):
                            pe.wait_ge(S("qk_sq"), n + 1)
                            if n >= 2:
                                pe.wait_ge(S("qk_root"), n - 1)
                            nc.tensor.matmul(bank[n % 2][:], C("ones"), sq[n % 2][:], start=True, stop=True).then_inc(S("qk_ss"), 1)

                    @block.vector
                    def _(dve):
                        for n in range(8):
                            dve.wait_ge(S("qk_root"), n + 1)
                            nc.vector.reciprocal(rn[n % 2][:], rn[n % 2][:]).then_inc(S("qk_rinv"), 1)
                            dve.wait_ge(S("qk_rinv"), n + 1)
                            nc.vector.scalar_tensor_tensor(ch[:, T_GDN + n, :], ch[:, T_GDN + n, :], float(P) ** -0.5 if n < 4 else 1.0,
                                                           rn[n % 2][:], ALU.mult, ALU.mult).then_inc(S("qk_done"), 1)
                        dve.wait_ge(S("qk_done"), 8)

                with ExitStack() as ph, nc.Block() as block:
                    tmp = [sb(ph, f"dtmp{u}", [P, T])[:] for u in range(2)]
                    pe_dt, dve_dt, act_dt = decays(tmp, DT, SSM_H, GDN_H, "gdn", EG=qg)

                    @block.tensor
                    def _(pe):
                        pe_dt(pe)
                        for h in range(GDN_H):
                            for c in range(NC):
                                last = nc.tensor.matmul(bank[h][:, c * P:(c + 1) * P], ch[:, k_t + h, c * P:(c + 1) * P],
                                                        ch[:, k_t + h, c * P:(c + 1) * P], start=True, stop=True)
                            last.then_inc(S("gdn_kk"), 1)
                        for h in range(GDN_H):
                            pe.wait_ge(S("gdn_bc_free"), h + 1)
                            nc.tensor.matmul(bank[4 + h][:], sel[:, (NHEAD + h) * P:(NHEAD + h + 1) * P], rows[:],
                                             start=True, stop=True).then_inc(S("gdn_beta"), 1)
                        for h in range(GDN_H):
                            pe.wait_ge(S("gdn_x1"), h + 1)
                            for c in range(NC):
                                last = nc.tensor.transpose(bank[h][:, c * P:(c + 1) * P], XT[:, h, c * P:(c + 1) * P], C("ident"))
                            last.then_inc(S("gdn_x1t"), 1)

                    @block.scalar
                    def _(act):
                        act_dt(act)
                        for h in range(GDN_H):
                            act.wait_ge(S("gdn_x1t"), h + 1)
                            nc.scalar.activation(X[:, h, :], bank[h][:], ACT.Copy).then_inc(S("gdn_x"), 1)
                        act.wait_ge(S("gdn_x"), GDN_H)

                    @block.vector
                    def _(dve):
                        dve_dt(dve)
                        for h in range(GDN_H):
                            nc.vector.tensor_tensor(qg[:, h, :], qg[:, h, :], ch[:, q_t + h, :], ALU.mult).then_inc(S("gdn_qg"), 1)
                        for h in range(GDN_H):
                            dve.wait_ge(S("gdn_kk"), h + 1)
                            dve.wait_ge(S("gdn_dt"), h + 1)
                            nc.vector.tensor_tensor(MT[:, h, :], DT[:, h, :], bank[h][:], ALU.mult).then_inc(S("gdn_m"), 1)
                            dve.wait_ge(S("gdn_m"), 2 * h + 1)
                            dve.wait_ge(S("gdn_beta"), h + 1)
                            nc.vector.tensor_tensor(MT[:, h, :], MT[:, h, :], bank[4 + h][:], ALU.mult).then_inc(S("gdn_m"), 1)
                            dve.wait_ge(S("gdn_m"), 2 * h + 2)
                            per = [P, NC, P]
                            m4 = MT[:, h, :].rearrange("p (c n) -> p c n", c=NC)
                            x4 = XT[:, h, :].rearrange("p (c n) -> p c n", c=NC)
                            nc.vector.tensor_tensor(x4, m4, C("lv1").unsqueeze(1).to_broadcast(per), ALU.mult).then_inc(S("gdn_lv1"), 1)
                            dve.wait_ge(S("gdn_lv1"), h + 1)
                            nc.vector.tensor_tensor(x4, C("ident").unsqueeze(1).to_broadcast(per), x4, ALU.subtract).then_inc(S("gdn_x1"), 1)
                        dve.wait_ge(S("gdn_x1"), GDN_H)

                with nc.Block() as block:
                    N_LV = len(LEVELS)

                    @block.tensor
                    def _(pe):
                        for n, s in enumerate(LEVELS):
                            for h in range(GDN_H):
                                pe.wait_ge(S("inv_ms"), GDN_H * n + h + 1)
                                if n:
                                    pe.wait_ge(S("inv_x"), GDN_H * (n - 1) + h + 1)
                                for c in range(NC):
                                    cc = slice(c * P, (c + 1) * P)
                                    last = nc.tensor.matmul(bank[h][:, cc], MS[:, h, cc], X[:, h, cc], start=True, stop=True)
                                last.then_inc(S("inv_y_mm"), 1)
                            for h in range(GDN_H):
                                pe.wait_ge(S("inv_y"), GDN_H * n + h + 1)
                                if n:
                                    pe.wait_ge(S("inv_xt"), GDN_H * (n - 1) + h + 1)
                                for c in range(NC):
                                    cc = slice(c * P, (c + 1) * P)
                                    last = nc.tensor.matmul(bank[4 + h][:, cc], Y[:, h, cc], XT[:, h, cc], start=True, stop=True)
                                last.then_inc(S("inv_xt_mm"), 1)
                                if n < N_LV - 1:
                                    for c in range(NC):
                                        cc = slice(c * P, (c + 1) * P)
                                        last = nc.tensor.matmul(bank[h][:, cc], XT[:, h, cc], Y[:, h, cc], start=True, stop=True)
                                    last.then_inc(S("inv_x_mm"), 1)

                    @block.scalar
                    def _(act):
                        for n in range(N_LV):
                            for h in range(GDN_H):
                                act.wait_ge(S("inv_y_mm"), GDN_H * n + h + 1)
                                if n:
                                    act.wait_ge(S("inv_x_mm"), GDN_H * (n - 1) + h + 1)
                                nc.scalar.activation(Y[:, h, :], bank[h][:], ACT.Copy).then_inc(S("inv_y"), 1)

                    @block.vector
                    def _(dve):
                        for n, s in enumerate(LEVELS):
                            for h in range(GDN_H):
                                if n:
                                    dve.wait_ge(S("inv_y_mm"), GDN_H * (n - 1) + h + 1)
                                nc.vector.tensor_tensor(MS[:, h, :].rearrange("p (c n) -> p c n", c=NC),
                                                        MT[:, h, :].rearrange("p (c n) -> p c n", c=NC),
                                                        C(f"lv{s}").unsqueeze(1).to_broadcast([P, NC, P]), ALU.mult).then_inc(S("inv_ms"), 1)
                            for h in range(GDN_H):
                                if n < N_LV - 1:
                                    dve.wait_ge(S("inv_x_mm"), GDN_H * n + h + 1)
                                    nc.vector.tensor_tensor(X[:, h, :], X[:, h, :], bank[h][:], ALU.subtract).then_inc(S("inv_x"), 1)
                                dve.wait_ge(S("inv_xt_mm"), GDN_H * n + h + 1)
                                if n < N_LV - 1:
                                    dve.wait_ge(S("inv_x_mm"), GDN_H * n + h + 1)
                                nc.vector.tensor_tensor(XT[:, h, :], XT[:, h, :], bank[4 + h][:], ALU.subtract).then_inc(S("inv_xt"), 1)
                        dve.wait_ge(S("inv_xt"), GDN_H * N_LV)

                AT, KB, WT, o = MS, MT, X, Y
                KD_, VB = ch[:, k_t:k_t + GDN_H, :], ch[:, v_t:v_t + GDN_H, :]
                with ExitStack() as ph, nc.Block() as block:
                    vn = sb(ph, "vn", [P, T])
                    sg = sb(ph, "sg", [P, T])
                    eb = sb(ph, "eb", [P, NC, GDN_H])
                    per = [P, NC, P]

                    def byc(t):
                        return t.rearrange("p (c n) -> p c n", c=NC)

                    @block.tensor
                    def _(pe):
                        def grid(b, left, right, sem):
                            for c in range(NC):
                                cc = slice(c * P, (c + 1) * P)
                                last = nc.tensor.matmul(bank[b][:, cc], left[:, cc], right[:, cc], start=True, stop=True)
                            last.then_inc(S(sem), 1)

                        for h in range(GDN_H):
                            if h:
                                pe.wait_ge(S("gdn_at"), h)
                            grid(0, ch[:, k_t + h, :], ch[:, q_t + h, :], "gdn_kq")
                            if h:
                                pe.wait_ge(S("gdn_kd"), h)
                                pe.wait_ge(S("gdn_vb"), h)
                            for b, t in ((1, k_t), (2, v_t)):
                                for c in range(NC):
                                    cc = slice(c * P, (c + 1) * P)
                                    last = nc.tensor.transpose(bank[b][:, cc], ch[:, t + h, cc], C("ident"))
                                last.then_inc(S("gdn_kvt"), 1)
                            pe.wait_ge(S("gdn_kb"), h + 1)
                            if h:
                                pe.wait_ge(S("gdn_wt"), h)
                            grid(3, KB[:, h, :], XT[:, h, :], "gdn_w_mm")
                        for c in range(NC):
                            cc = slice(c * P, (c + 1) * P)
                            if c:
                                pe.wait_ge(S("gdn_state"), c)
                            else:
                                pe.wait_ge(S("gdn_wt"), GDN_H)
                                pe.wait_ge(S("gdn_vb"), GDN_H)
                            for h in range(GDN_H):
                                hh = slice(h * P, (h + 1) * P)
                                last = nc.tensor.matmul(bank[4][:, hh], XT[:, h, cc], VB[:, h, cc], start=True, stop=c == 0)
                                if c:
                                    last = nc.tensor.matmul(bank[4][:, hh], WT[:, h, cc], sg[:, hh], start=False, stop=True)
                            last.then_inc(S("gdn_vn_mm"), 1)
                            pe.wait_ge(S("gdn_vn"), c + 1)
                            if c:
                                pe.wait_ge(S("gdn_o"), c)
                            for h in range(GDN_H):
                                hh = slice(h * P, (h + 1) * P)
                                last = nc.tensor.matmul(bank[6][:, hh], KD_[:, h, cc], vn[:, hh], start=True, stop=True)
                            last.then_inc(S("gdn_s_mm"), 1)
                            for h in range(GDN_H):
                                hh = slice(h * P, (h + 1) * P)
                                last = nc.tensor.matmul(bank[5][:, hh], AT[:, h, cc], vn[:, hh], start=True, stop=c == 0)
                                if c:
                                    last = nc.tensor.matmul(bank[5][:, hh], qg[:, h, cc], sg[:, hh], start=False, stop=True)
                            last.then_inc(S("gdn_o_mm"), 1)

                    @block.scalar
                    def _(act):
                        for h in range(GDN_H):
                            act.wait_ge(S("gdn_w_mm"), h + 1)
                            nc.scalar.activation(WT[:, h, :], bank[3][:], ACT.Copy, scale=-1.0).then_inc(S("gdn_wt"), 1)
                        for c in range(NC):
                            act.wait_ge(S("gdn_vn_mm"), c + 1)
                            if c:
                                act.wait_ge(S("gdn_o_mm"), c)
                            nc.scalar.activation(vn[:], bank[4][:], ACT.Copy).then_inc(S("gdn_vn"), 1)
                            act.wait_ge(S("gdn_o_mm"), c + 1)
                            nc.scalar.activation(o[:, c, :], bank[5][:], ACT.Copy).then_inc(S("gdn_o"), 1)
                        act.wait_ge(S("gdn_o"), NC)

                    @block.vector
                    def _(dve):
                        nc.vector.tensor_tensor(eb[:], dec[:, :, NHEAD:16],
                                                ecol[:].rearrange("p (c h) -> p c h", c=NC)[:, :, SSM_H:NHEAD], ALU.mult).then_inc(S("gdn_eb"), 1)
                        dve.wait_ge(S("gdn_eb"), 1)
                        for h in range(GDN_H):
                            dve.wait_ge(S("gdn_kq"), h + 1)
                            nc.vector.tensor_tensor(AT[:, h, :], DT[:, h, :], bank[0][:], ALU.mult).then_inc(S("gdn_at"), 1)
                            dve.wait_ge(S("gdn_kvt"), 2 * h + 2)
                            nc.vector.tensor_tensor(byc(KB[:, h, :]), byc(bank[1][:]), eb[:, :, h:h + 1].to_broadcast(per), ALU.mult
                                                    ).then_inc(S("gdn_kb"), 1)
                            nc.vector.tensor_tensor(byc(KD_[:, h, :]), byc(bank[1][:]), DT[:, h, P - 1:T:P].unsqueeze(2).to_broadcast(per),
                                                    ALU.mult).then_inc(S("gdn_kd"), 1)
                            nc.vector.tensor_tensor(byc(VB[:, h, :]), byc(bank[2][:]), dec[:, :, NHEAD + h:NHEAD + h + 1].to_broadcast(per),
                                                    ALU.mult).then_inc(S("gdn_vb"), 1)
                        for c in range(NC - 1):
                            dve.wait_ge(S("gdn_s_mm"), c + 1)
                            if c == 0:
                                nc.vector.tensor_copy(sg[:], bank[6][:]).then_inc(S("gdn_state"), 1)
                            else:
                                dve.wait_ge(S("gdn_o_mm"), c + 1)
                                dve.wait_ge(S("gdn_state"), c)
                                for h in range(GDN_H):
                                    hh = slice(h * P, (h + 1) * P)
                                    e = c * NHEAD + SSM_H + h
                                    last = nc.vector.scalar_tensor_tensor(sg[:, hh], sg[:, hh], etot[:, e:e + 1], bank[6][:, hh],
                                                                          ALU.mult, ALU.add)
                                last.then_inc(S("gdn_state"), 1)
                finish(o, 1, GDN_H, False, v("gdn_nw"), T_GDN, "gdnf")

            clear_since(outside)

            with ExitStack() as gla:
                o = sb(gla, "gla_o", [P, NC, WIDTH])
                G2 = [P, 2 * NC, P]
                with ExitStack() as ph, nc.Block() as block:
                    wg = sb(ph, "wg", [RANK, 2 * P])
                    G = sb(ph, "G", [P, 2, T])
                    nab = sb(ph, "nab", [P, 2, T])
                    e1 = sb(ph, "e1", [P, 2, T])
                    e2 = sb(ph, "e2", [P, 2, T])
                    qe = sb(ph, "qe", [P, 2, T])
                    ke = sb(ph, "ke", [P, 2, T])
                    qs = sb(ph, "qs", [P, 2, T])
                    kd = sb(ph, "kd", [P, 2, T])
                    kt = sb(ph, "kt", [P, NC, 2 * P])
                    at = zt[:, 0]
                    gs = sb(ph, "gs", [P, NC - 1, 2, 2, P])
                    ed = sb(ph, "ed", [P, 2 * NC])
                    q2, k2 = ch[:, T_GLAQ:T_GLAQ + 2, :], ch[:, T_GLAQ + 2:T_GLAQ + 4, :]

                    def by(t):
                        return t.rearrange("p m (c n) -> p (m c) n", c=NC)

                    def tok(m):
                        return by(G[:])[:, :, m:m + 1].to_broadcast(G2)

                    @block.gpsimd
                    def _(pool):
                        nc.gpsimd.memset(gs[:], 0.0).then_inc(S("gla_zero"), 1)

                    @block.sync
                    def _(sp):
                        sp.dma_start(wg[:], lay("w_gate")).then_inc(S("wg_loaded"), 16)

                    @block.tensor
                    def _(pe):
                        pe.wait_ge(S("wg_loaded"), 16)
                        for m in range(2):
                            nc.tensor.matmul(bank[m][:], wg[:, m * P:(m + 1) * P], low[:], start=True, stop=True).then_inc(S("gla_pre"), 1)
                        pe.wait_ge(S("gla_kd"), 1)
                        for c in range(NC):
                            for m in range(2):
                                last = nc.tensor.transpose(bank[2 + c // 2][:, (c % 2 * 2 + m) * P:(c % 2 * 2 + m + 1) * P],
                                                           kd[:, m, c * P:(c + 1) * P], C("ident"))
                        last.then_inc(S("gla_kdt"), 1)
                        pe.wait_ge(S("gla_ke"), 2)
                        for h in range(GLA_H):
                            r = slice(h % 2 * GLA_K, (h % 2 + 1) * GLA_K)
                            for c in range(NC):
                                cc = slice(c * P, (c + 1) * P)
                                last = nc.tensor.matmul(bank[4 + h][:, cc], ke[r, h // 2, cc], qe[r, h // 2, cc], start=True, stop=True)
                            last.then_inc(S("gla_qk"), 1)
                        pe.wait_ge(S("gla_kt"), 2)
                        for c in range(NC - 1):
                            for h in range(GLA_H):
                                r = slice(h % 2 * GLA_K, (h % 2 + 1) * GLA_K)
                                m = (c % 2) * 2 + h // 2
                                last = nc.tensor.matmul(bank[c // 2][r, m * P:(m + 1) * P], kt[:, c, h * GLA_K:(h + 1) * GLA_K],
                                                        zt[:, 3, c, h * P:(h + 1) * P], start=True, stop=True)
                        last.then_inc(S("gla_s_mm"), 1)
                        for c in range(NC):
                            cc = slice(c * P, (c + 1) * P)
                            if c:
                                pe.wait_ge(S("gla_state"), c)
                            else:
                                pe.wait_ge(S("gla_at"), GLA_H)
                            if c >= 2:
                                pe.wait_ge(S("gla_o"), c - 1)
                            for m in range(2) if c else ():
                                nc.tensor.matmul(bank[2 + c % 2][:, 2 * m * P:2 * (m + 1) * P], qs[:, m, cc],
                                                 gs[:, c - 1, m].rearrange("p h n -> p (h n)"), start=m == 0, stop=False,
                                                 skip_group_check=True)
                            for h in range(GLA_H):
                                hh = slice(h * P, (h + 1) * P)
                                last = nc.tensor.matmul(bank[2 + c % 2][:, hh], at[:, h, cc], zt[:, 3, c, hh], start=c == 0 and h == 0,
                                                        stop=h == GLA_H - 1, skip_group_check=True)
                            last.then_inc(S("gla_o_mm"), 1)

                    @block.scalar
                    def _(act):
                        act.wait_ge(S("gla_nab"), 2)
                        nc.scalar.activation(e1[:], nab[:], ACT.Exp, bias=zero).then_inc(S("gla_z"), 1)
                        act.wait_ge(S("gla_z"), 1)
                        nc.scalar.activation(e1[:], e1[:], ACT.Ln, bias=cst[:, C_OFF["ones"]:C_OFF["ones"] + 1]).then_inc(S("gla_ln"), 1)
                        act.wait_ge(S("gla_mid"), 1)
                        nc.scalar.activation(e1[:], nab[:], ACT.Exp, bias=zero).then_inc(S("gla_e"), 1)
                        nc.scalar.activation(e2[:], nab[:], ACT.Exp, bias=zero, scale=-1.0).then_inc(S("gla_e"), 1)
                        nc.scalar.activation(qs[:], G[:], ACT.Exp, bias=zero).then_inc(S("gla_eg"), 1)
                        nc.scalar.activation(ed[:], by(G[:])[:, :, P - 1], ACT.Exp, bias=zero).then_inc(S("gla_ed"), 1)
                        act.wait_ge(S("gla_end"), 1)
                        nc.scalar.activation(kd[:], kd[:], ACT.Exp, bias=zero, scale=-1.0).then_inc(S("gla_ekd"), 1)
                        act.wait_ge(S("gla_kdt"), 1)
                        for b in range(2):
                            nc.scalar.activation(kt[:, 2 * b:2 * b + 2, :].rearrange("p c n -> p (c n)"), bank[2 + b][:], ACT.Copy
                                                 ).then_inc(S("gla_kt"), 1)
                        for c in range(NC):
                            act.wait_ge(S("gla_o_mm"), c + 1)
                            nc.scalar.activation(o[:, c, :], bank[2 + c % 2][:], ACT.Copy).then_inc(S("gla_o"), 1)
                        act.wait_ge(S("gla_o"), NC)

                    @block.vector
                    def _(dve):
                        for m in range(2):
                            dve.wait_ge(S("gla_pre"), m + 1)
                            nc.vector.tensor_scalar(G[:, m, :], bank[m][:], v("gla_b", m, 1), None, ALU.add).then_inc(S("gla_x"), 1)
                        dve.wait_ge(S("gla_x"), 2)
                        for m in range(2):
                            nc.vector.scalar_tensor_tensor(nab[:, m, :], G[:, m, :], -1.0, G[:, m, :], ALU.mult, ALU.min).then_inc(S("gla_nab"), 1)
                        dve.wait_ge(S("gla_ln"), 1)
                        nc.vector.scalar_tensor_tensor(e1[:], G[:], 0.0, e1[:], ALU.min, ALU.subtract).then_inc(S("gla_ls"), 1)
                        dve.wait_ge(S("gla_ls"), 1)
                        nc.vector.tensor_scalar(e1[:], e1[:], 1.0 / GLA_TAU, None, ALU.mult).then_inc(S("gla_ls"), 1)
                        dve.wait_ge(S("gla_ls"), 2)
                        for m in range(2):
                            nc.vector.tensor_tensor_scan(G[:, m, :], cst[:, C_RESET:C_RESET + T], e1[:, m, :], 0.0, ALU.mult, ALU.add
                                                         ).then_inc(S("gla_G"), 1)
                        dve.wait_ge(S("gla_G"), 2)
                        nc.vector.tensor_tensor(by(nab[:]), by(G[:]), tok(P // 2 - 1), ALU.subtract).then_inc(S("gla_mid"), 1)
                        nc.vector.tensor_tensor(by(kd[:]), by(G[:]), tok(P - 1), ALU.subtract).then_inc(S("gla_end"), 1)
                        s = float(GLA_K) ** -0.5
                        dve.wait_ge(S("gla_ekd"), 1)
                        nc.vector.tensor_tensor(kd[:], kd[:], k2, ALU.mult).then_inc(S("gla_kd"), 1)
                        dve.wait_ge(S("gla_e"), 2)
                        nc.vector.scalar_tensor_tensor(qe[:], q2, s, e1[:], ALU.mult, ALU.mult).then_inc(S("gla_ke"), 1)
                        nc.vector.tensor_tensor(ke[:], k2, e2[:], ALU.mult).then_inc(S("gla_ke"), 1)
                        dve.wait_ge(S("gla_eg"), 1)
                        nc.vector.scalar_tensor_tensor(qs[:], q2, s, qs[:], ALU.mult, ALU.mult).then_inc(S("gla_qs"), 1)
                        for h in range(GLA_H):
                            dve.wait_ge(S("gla_qk"), h + 1)
                            nc.vector.tensor_tensor(at[:, h, :].rearrange("p (c n) -> p c n", c=NC), bank[4 + h][:].rearrange("p (c n) -> p c n", c=NC),
                                                    C("tri").unsqueeze(1).to_broadcast([P, NC, P]), ALU.mult).then_inc(S("gla_at"), 1)
                        dve.wait_ge(S("gla_s_mm"), 1)
                        dve.wait_ge(S("gla_ed"), 1)
                        dve.wait_ge(S("gla_qs"), 1)
                        dve.wait_ge(S("gla_zero"), 1)
                        for c in range(NC - 1):
                            if c:
                                dve.wait_ge(S("gla_state"), c)
                            for m in range(2):
                                b = (c % 2) * 2 + m
                                for h in range(2):
                                    r = slice(h * GLA_K, (h + 1) * GLA_K)
                                    if c == 0:
                                        last = nc.vector.tensor_copy(gs[r, c, m, h], bank[0][r, m * P:(m + 1) * P])
                                    else:
                                        last = nc.vector.scalar_tensor_tensor(gs[r, c, m, h], gs[r, c - 1, m, h],
                                                                              ed[r, m * NC + c:m * NC + c + 1],
                                                                              bank[c // 2][r, b * P:(b + 1) * P], ALU.mult, ALU.add)
                            last.then_inc(S("gla_state"), 1)
                finish(o, 2, GLA_H, False, v("gla_nw"), T_GLAQ, "glaf")

            clear_since(outside)

            with ExitStack() as ph, nc.Block() as block:
                wl = sb(ph, "wl", [P, 2, NW, P])
                aa = sb(ph, "aa", [P, NW, T])
                gi = sb(ph, "gi", [P, NW, T])
                th = sb(ph, "th", [P, NW, T])
                lam = sb(ph, "lam", [P, NW])
                x4, g4 = ch[:, T_LRUX:T_LRUX + NW, :], ch[:, T_LRUG:T_LRUG + NW, :]

                @block.gpsimd
                def _(pool):
                    nc.gpsimd.memset(wl[:], 0.0).then_inc(S("wl_zero"), 1)

                @block.sync
                def _(sp):
                    sp.wait_ge(S("wl_zero"), 1)
                    w = lay("w_lru")
                    for g in range(2):
                        for half in range(2):
                            r = slice(64 * half, 64 * half + 64)
                            sp.dma_start(wl[r, g, :, r], w[half, :, g]).then_inc(S("wl_loaded"), 16)

                @block.tensor
                def _(pe):
                    pe.wait_ge(S("wl_loaded"), 64)
                    for g in range(2):
                        for m in range(NW):
                            nc.tensor.matmul(bank[4 * g + m][:], wl[:, g, m, :], x4[:, m, :], start=True, stop=True).then_inc(S("lru_mm"), 1)

                @block.scalar
                def _(act):
                    for g, (dst, b) in enumerate(((aa, "lru_ba"), (gi, "lru_bx"))):
                        for m in range(NW):
                            act.wait_ge(S("lru_mm"), 4 * g + m + 1)
                            nc.scalar.activation(dst[:, m, :], bank[4 * g + m][:], ACT.Sigmoid, bias=v(b, m, 1)).then_inc(S("lru_gate"), 1)
                    for m in range(NW):
                        act.wait_ge(S("lru_loga"), m + 1)
                        nc.scalar.activation(th[:, m, :], aa[:, m, :], ACT.Tanh, bias=zero, scale=-1.0).then_inc(S("lru_th"), 1)
                    act.wait_ge(S("lru_th"), NW)
                    for m in range(NW):
                        nc.scalar.activation(aa[:, m, :], aa[:, m, :], ACT.Exp, bias=zero).then_inc(S("lru_a"), 1)
                    for m in range(NW):
                        act.wait_ge(S("lru_u2"), 2 * m + 2)
                        nc.scalar.activation(th[:, m, :], th[:, m, :], ACT.Sqrt, bias=zero).then_inc(S("lru_root"), 1)
                    for m in range(NW):
                        nc.scalar.activation(g4[:, m, :], g4[:, m, :], ACT.Gelu_apprx_tanh, bias=zero).then_inc(S("lru_gelu"), 1)

                @block.vector
                def _(dve):
                    nc.vector.tensor_scalar(lam[:], dts[:, NS:], -LRU_C, None, ALU.mult).then_inc(S("lru_lam"), 1)
                    dve.wait_ge(S("lru_lam"), 1)
                    for m in range(NW):
                        dve.wait_ge(S("lru_gate"), m + 1)
                        nc.vector.tensor_scalar(aa[:, m, :], aa[:, m, :], lam[:, m:m + 1], None, ALU.mult).then_inc(S("lru_loga"), 1)
                    for m in range(NW):
                        dve.wait_ge(S("lru_gate"), NW + m + 1)
                        nc.vector.tensor_tensor(gi[:, m, :], gi[:, m, :], x4[:, m, :], ALU.mult).then_inc(S("lru_gx"), 1)
                    for m in range(NW):
                        dve.wait_ge(S("lru_a"), m + 1)
                        dve.wait_ge(S("lru_gx"), m + 1)
                        nc.vector.tensor_tensor(x4[:, m, :], aa[:, m, :], aa[:, m, :], ALU.mult).then_inc(S("lru_u2"), 1)
                        dve.wait_ge(S("lru_u2"), 2 * m + 1)
                        nc.vector.scalar_tensor_tensor(th[:, m, :], x4[:, m, :], 1.0, th[:, m, :], ALU.add, ALU.mult).then_inc(S("lru_u2"), 1)
                    for m in range(NW):
                        dve.wait_ge(S("lru_root"), m + 1)
                        nc.vector.tensor_tensor(gi[:, m, :], gi[:, m, :], th[:, m, :], ALU.mult).then_inc(S("lru_u"), 1)
                        dve.wait_ge(S("lru_u"), m + 1)
                        dve.wait_ge(S("lru_u2"), 2 * m + 2)
                        nc.vector.tensor_tensor_scan(x4[:, m, :], aa[:, m, :], gi[:, m, :], 0.0, ALU.mult, ALU.add).then_inc(S("lru_h"), 1)
                    for m in range(NW):
                        dve.wait_ge(S("lru_h"), m + 1)
                        dve.wait_ge(S("lru_gelu"), m + 1)
                        nc.vector.tensor_tensor(x4[:, m, :], x4[:, m, :], g4[:, m, :], ALU.mult).then_inc(S("lru_y"), 1)
                    dve.wait_ge(S("lru_y"), NW)
            sm.close()
            mixers.close()
            clear_since(outside)

            branch = (T_SSM, T_GDN, T_GLAQ, T_LRUX)
            with ExitStack() as ph, nc.Block() as block:
                h_hi, h_lo = sb(ph, "h_hi", [P, KD, T], FR), sb(ph, "h_lo", [P, KD, T], FR)
                b_hi, b_lo = sb(ph, "b_hi", [P, NW, T], FR), sb(ph, "b_lo", [P, NW, T], FR)
                wm = [sb(ph, f"wm{u}", [P, KD, P]) for u in range(2)]
                wm_hi = [sb(ph, f"wm_hi{u}", [P, KD, P], FR) for u in range(2)]
                wm_lo = [sb(ph, f"wm_lo{u}", [P, KD, P], FR) for u in range(2)]
                wb = [sb(ph, f"wb{u}", [P, NW, P]) for u in range(2)]
                wb_hi = [sb(ph, f"wb_hi{u}", [P, NW, P], FR) for u in range(2)]
                wb_lo = [sb(ph, f"wb_lo{u}", [P, NW, P], FR) for u in range(2)]
                sg = [sb(ph, f"sig{u}", [P, T]) for u in range(2)]
                mg = sb(ph, "mg", [P, T])
                merged = hT
                w_m, w_b, w_o = lay("w_merge"), lay("w_branch"), lay("w_out")

                @block.sync
                def _(sp):
                    sp.sem_inc(S("wm_free"), 2)
                    with sp.Fori(0, N_MERGE // 2) as i:
                        for u in range(2):
                            sp.wait_ge(S("wm_free"), 2 * i + u + 1)
                            sp.dma_start(wm[u][:].rearrange("p k n -> p (k n)"),
                                         w_m[bass.ds(2 * i + u, 1)].rearrange("g p n -> (g p) n")).then_inc(S(f"wm_loaded{u}"), 16)
                            sp.dma_start(wb[u][:].rearrange("p k n -> p (k n)"),
                                         w_b[bass.ds(2 * i + u, 1)].rearrange("g p n -> (g p) n")).then_inc(S(f"wb_loaded{u}"), 16)
                    with sp.Fori(0, KD // 2) as i:
                        for u in range(2):
                            sp.wait_ge(S("wm_free"), 2 * i + u + N_MERGE + 1)
                            sp.dma_start(wm[u][:].rearrange("p k n -> p (k n)"),
                                         w_o[bass.ds(2 * i + u, 1)].rearrange("g p n -> (g p) n")).then_inc(S(f"wm_loaded{u}"), 16)

                @block.scalar
                def _(act):
                    def wm_high(i, u):
                        act.wait_ge(S(f"wm_loaded{u}"), 16 * i + 16)
                        nc.scalar.activation(wm_hi[u][:], wm[u][:], ACT.Copy).then_inc(S("wm_hi"), 1)

                    def wb_high(i, u):
                        act.wait_ge(S(f"wb_loaded{u}"), 16 * i + 16)
                        nc.scalar.activation(wb_hi[u][:], wb[u][:], ACT.Copy).then_inc(S("wb_hi"), 1)

                    def gates(i, last=False):
                        for u in range(2):
                            n = 2 * i + u
                            act.wait_ge(S("logit_mm"), n + 1)
                            act.wait_ge(S("sig_free"), n + 1)
                            nc.scalar.activation(sg[u][:], bank[u][:], ACT.Sigmoid, bias=zero).then_inc(S("sig_done"), 1)
                            wm_high(i + 1, u)
                            act.wait_ge(S("branch_mm"), n + 1)
                            if not last:
                                wb_high(i + 1, u)

                    act.sem_inc(S("sig_free"), 2)
                    wm_high(0, 0)
                    for k in range(KD):
                        nc.scalar.activation(h_hi[:, k, :], hT[:, k, :], ACT.Copy).then_inc(S("h_hi"), 1)
                    wm_high(0, 1)
                    wb_high(0, 0)
                    wb_high(0, 1)
                    for b in range(4):
                        for k in range(NW):
                            nc.scalar.activation(b_hi[:, k, :], ch[:, branch[b] + k, :], ACT.Copy).then_inc(S("b_hi"), 1)
                        with act.Fori(4 * b, 4 * b + (4 if b < 3 else 3)) as i:
                            gates(i)
                    gates(N_MERGE // 2 - 1, True)
                    for k in range(KD):
                        act.wait_ge(S("merged"), k + 1)
                        nc.scalar.activation(h_hi[:, k, :], merged[:, k, :], ACT.Copy).then_inc(S("h_hi"), 1)
                    with act.Fori(0, KD // 2 - 1) as i:
                        for u in range(2):
                            act.wait_ge(S("out_mm"), 2 * i + u + 1)
                            wm_high(N_MERGE // 2 + 1 + i, u)

                @block.gpsimd
                def _(pool):
                    with pool.Fori(0, N_MERGE // 2) as i:
                        for u in range(2):
                            n = 2 * i + u
                            pool.wait_ge(S("wm_hi"), n + 1)
                            nc.gpsimd.tensor_tensor(wm_lo[u][:], wm[u][:], wm_hi[u][:].bitcast(F32), ALU.subtract).then_inc(S("wm_lo"), 1)
                            pool.wait_ge(S("wb_hi"), n + 1)
                            nc.gpsimd.tensor_tensor(wb_lo[u][:], wb[u][:], wb_hi[u][:].bitcast(F32), ALU.subtract).then_inc(S("wb_lo"), 1)
                            pool.wait_ge(S("wm_lo"), n + 1)
                            pool.wait_ge(S("wb_lo"), n + 1)
                            pool.sem_inc(S("wm_free"), 1)
                    with pool.Fori(N_MERGE // 2, (N_MERGE + KD) // 2) as i:
                        for u in range(2):
                            n = 2 * i + u
                            pool.wait_ge(S("wm_hi"), n + 1)
                            nc.gpsimd.tensor_tensor(wm_lo[u][:], wm[u][:], wm_hi[u][:].bitcast(F32), ALU.subtract).then_inc(S("wm_lo"), 1)
                            pool.wait_ge(S("wm_lo"), n + 1)
                            pool.sem_inc(S("wm_free"), 1)

                @block.tensor
                def _(pe):
                    pe.sem_inc(S("gated"), 2)
                    pe.wait_ge(S("h_lo"), KD)
                    for b in range(4):
                        with pe.Fori(4 * b, 4 * b + 4) as i:
                            for u in range(2):
                                n = 2 * i + u
                                pe.wait_ge(S("wm_lo"), n + 1)
                                pe.wait_ge(S("gated"), n + 1)
                                for k in range(KD):
                                    last = mm3(bank[u][:], (wm_hi[u][:, k, :], wm_lo[u][:, k, :]), (h_hi[:, k, :], h_lo[:, k, :]),
                                               k == 0, k == KD - 1)
                                last.then_inc(S("logit_mm"), 1)
                                pe.wait_ge(S("wb_lo"), n + 1)
                                pe.wait_ge(S("b_lo"), NW * b + NW)
                                for k in range(NW):
                                    last = mm3(bank[2 + u][:], (wb_hi[u][:, k, :], wb_lo[u][:, k, :]), (b_hi[:, k, :], b_lo[:, k, :]),
                                               k == 0, k == NW - 1)
                                last.then_inc(S("branch_mm"), 1)
                    pe.wait_ge(S("h_lo"), 2 * KD)
                    pe.sem_inc(S("out_bank_free"), 2)
                    with pe.Fori(0, KD // 2) as i:
                        for u in range(2):
                            pe.wait_ge(S("wm_lo"), 2 * i + u + N_MERGE + 1)
                            pe.wait_ge(S("out_bank_free"), 2 * i + u + 1)
                            for k in range(KD):
                                last = mm3(bank[4 + u][:], (wm_hi[u][:, k, :], wm_lo[u][:, k, :]), (h_hi[:, k, :], h_lo[:, k, :]),
                                           k == 0, k == KD - 1)
                            last.then_inc(S("out_mm"), 1)

                @block.vector
                def _(dve):
                    def h_low(k, n):
                        dve.wait_ge(S("h_hi"), n + 1)
                        nc.vector.tensor_tensor(h_lo[:, k, :], hT[:, k, :], h_hi[:, k, :].bitcast(F32), ALU.subtract).then_inc(S("h_lo"), 1)

                    for k in range(KD):
                        h_low(k, k)
                    dve.wait_ge(S("h_lo"), KD)
                    for b in range(4):
                        for k in range(NW):
                            dve.wait_ge(S("b_hi"), NW * b + k + 1)
                            nc.vector.tensor_tensor(b_lo[:, k, :], ch[:, branch[b] + k, :], b_hi[:, k, :].bitcast(F32), ALU.subtract
                                                    ).then_inc(S("b_lo"), 1)
                        with dve.Fori(0, KD // 2) as i:
                            for u in range(2):
                                n = 2 * i + u + KD * b
                                sum_ = row(merged, 2 * i + u)
                                dve.wait_ge(S("branch_mm"), n + 1)
                                dve.wait_ge(S("sig_done"), n + 1)
                                nc.vector.tensor_tensor(sum_ if b == 0 else mg[:], sg[u][:], bank[2 + u][:], ALU.mult).then_inc(S("mg_prod"), 1)
                                dve.wait_ge(S("mg_prod"), n + 1)
                                dve.sem_inc(S("gated"), 1)
                                dve.sem_inc(S("sig_free"), 1)
                                if b:
                                    done = S("merged" if b == 3 else f"mg_sum{b}")
                                    nc.vector.tensor_tensor(sum_, sum_, mg[:], ALU.add).then_inc(done, 1)
                                    dve.wait_ge(done, 2 * i + u + 1)
                    for k in range(KD):
                        h_low(k, KD + k)
                    with dve.Fori(0, KD // 2) as i:
                        for u in range(2):
                            dve.wait_ge(S("out_mm"), 2 * i + u + 1)
                            xt = row(xT, 2 * i + u)
                            nc.vector.scalar_tensor_tensor(xt, bank[4 + u][:], mod[:, bass.ds(2 * KD + 2 * i + u, 1)], xt, ALU.mult, ALU.add
                                                           ).then_inc(S("x_mixed"), 1)
                            dve.wait_ge(S("x_mixed"), 2 * i + u + 1)
                            dve.sem_inc(S("out_bank_free"), 1)
            mix.close()

            clear_since(outside)

            peer = ExitStack()
            h_hi, h_lo = sb(peer, "h2_hi", [P, KD, T], FR), sb(peer, "h2_lo", [P, KD, T], FR)
            with ExitStack() as raw_h:
                norm(sb(raw_h, "h2T", [P, KD, T]), "nffn", gain[:, KD:2 * KD], mod[:, 3 * KD:4 * KD], (h_hi, h_lo))
            route = ExitStack()
            qT = sb(route, "qT", [P, QT, T])
            keys = sb(route, "keys", [P, QT, KEYS])
            stage = sb(route, "stage", [P, 2, KEYS, GT])
            with ExitStack() as ph, nc.Block() as block:
                wq = [sb(ph, f"wq{u}", [P, KD, P]) for u in range(2)]
                wh = [sb(ph, f"wq_hi{u}", [P, KD, P], FR) for u in range(2)]
                wl = [sb(ph, f"wq_lo{u}", [P, KD, P], FR) for u in range(2)]
                w_q = lay("w_q")

                @block.sync
                def _(sp):
                    sp.sem_inc(S("wq_free"), 2)
                    sp.dma_start(keys[:], lay("keys")).then_inc(S("keys_loaded"), 16)
                    with sp.Fori(0, QT // 2) as i:
                        for u in range(2):
                            sp.wait_ge(S("wq_free"), 2 * i + u + 1)
                            sp.dma_start(wq[u][:].rearrange("p k n -> p (k n)"),
                                         w_q[bass.ds(2 * i + u, 1)].rearrange("g p n -> (g p) n")).then_inc(S(f"wq_loaded{u}"), 16)
                    sp.wait_ge(S("keys_loaded"), 16)
                    for u in range(2):
                        sp.sem_inc(S(f"stage_stored{u}"), 16)
                        sp.sem_inc(S(f"hid_stored{u}"), 16)

                @block.scalar
                def _(act):
                    act.sem_inc(S("wq_split_free"), 2)
                    with act.Fori(0, QT // 2) as i:
                        for u in range(2):
                            act.wait_ge(S(f"wq_loaded{u}"), 16 * i + 16)
                            act.wait_ge(S("wq_split_free"), 2 * i + u + 1)
                            nc.scalar.activation(wh[u][:], wq[u][:], ACT.Copy).then_inc(S("wq_hi"), 1)

                @block.gpsimd
                def _(pool):
                    with pool.Fori(0, QT // 2) as i:
                        for u in range(2):
                            pool.wait_ge(S("wq_hi"), 2 * i + u + 1)
                            nc.gpsimd.tensor_tensor(wl[u][:], wq[u][:], wh[u][:].bitcast(F32), ALU.subtract).then_inc(S("wq_lo"), 1)
                            pool.wait_ge(S("wq_lo"), 2 * i + u + 1)
                            pool.sem_inc(S("wq_free"), 1)

                @block.tensor
                def _(pe):
                    pe.sem_inc(S("q_bank_free"), 2)
                    with pe.Fori(0, QT // 2) as i:
                        for u in range(2):
                            pe.wait_ge(S("wq_lo"), 2 * i + u + 1)
                            pe.wait_ge(S("q_bank_free"), 2 * i + u + 1)
                            for k in range(KD):
                                last = mm3(bank[u][:], (wh[u][:, k, :], wl[u][:, k, :]), (h_hi[:, k, :], h_lo[:, k, :]),
                                           k == 0, k == KD - 1)
                            last.then_inc(S("q_mm"), 1)

                @block.vector
                def _(dve):
                    with dve.Fori(0, QT // 2) as i:
                        for u in range(2):
                            dve.wait_ge(S("q_mm"), 2 * i + u + 1)
                            dve.sem_inc(S("wq_split_free"), 1)
                            nc.vector.tensor_copy(row(qT, 2 * i + u), bank[u][:]).then_inc(S("q_bank_free"), 1)
                    dve.wait_ge(S("q_bank_free"), QT + 2)

            with nc.Fori(0, NC) as tt:
                before = set(made)
                with ExitStack() as ph, nc.Block() as block:
                    qs = sb(ph, "qs", [P, QT, P])
                    s = sb(ph, "s", [P, QT, KEYS])
                    top = sb(ph, "top", [P, QT, TOPK])
                    idx = sb(ph, "idx", [P, QT, TOPK], U32)
                    idf = sb(ph, "idf", [P, QT, TOPK])
                    cand = sb(ph, "cand", [P, PEER_H, TOPK * TOPK])
                    best = sb(ph, "best", [P, PEER_H, TOPK])
                    pos = sb(ph, "pos", [P, PEER_H, TOPK], U32)
                    pu = sb(ph, "pu", [P, 2, PEER_H, TOPK], U32)
                    pf = sb(ph, "pf", [P, 2, PEER_H, TOPK])
                    chosen = sb(ph, "chosen", [P, 3, NHK])
                    ssum = sb(ph, "ssum", [P, PEER_H])
                    slots = sb(ph, "slots", [P, 3, P])
                    hot = sb(ph, "hot", [P, 8, 2, P])
                    ub = [sb(ph, f"ub{u}", [P, KD, P]) for u in range(2)]
                    u_hi = [sb(ph, f"u_hi{u}", [P, KD, P], FR) for u in range(2)]
                    u_lo = [sb(ph, f"u_lo{u}", [P, KD, P], FR) for u in range(2)]
                    hid = [sb(ph, f"hid{u}", [P, T]) for u in range(2)]
                    hbank = (bank[5], bank[3])
                    u_d = lay("u")
                    eq = s[:].rearrange("p a n -> p (a n)").rearrange("p (h k j) -> p h k j", h=PEER_H, k=TOPK)
                    four = [P, PEER_H, TOPK, TOPK]
                    NEG = -3.0e38

                    @block.tensor
                    def _(pe):
                        def hidden(e, u, ks):
                            if ks[0] == 0:
                                pe.wait_ge(S("u_lo"), e + 1)
                                pe.wait_ge(S("hid_bank_free"), e + 1)
                            for k in ks:
                                last = mm3(hbank[u][:], (u_hi[u][:, k, :], u_lo[u][:, k, :]), (h_hi[:, k, :], h_lo[:, k, :]),
                                           k == 0, k == KD - 1)
                            if ks[-1] == KD - 1:
                                last.then_inc(S("hid_mm"), 1)

                        pe.sem_inc(S("hid_bank_free"), 2)
                        pe.wait_ge(S("qs_done"), 1)
                        for n in range(QT):
                            last = nc.tensor.matmul(bank[n // 4][:, n % 4 * P:(n % 4 + 1) * P], qs[:, n, :], keys[:, n, :],
                                                    start=True, stop=True)
                            if n % 4 == 3:
                                last.then_inc(S("s_mm"), 1)
                        pe.wait_ge(S("s_done"), 4)
                        with pe.Fori(0, HPRE // 2) as i:
                            for u in range(2):
                                hidden(2 * i + u, u, range(KD))
                        for n in range(3):
                            pe.wait_ge(S("chosen_done"), n + 1)
                            last = nc.tensor.transpose(bank[4][:, n * P:(n + 1) * P], chosen[:, n, :], C("ident"))
                        last.then_inc(S("slots_t"), 1)
                        pe.sem_inc(S("g_bank_free"), 2)
                        with pe.Fori(0, P // GT) as j:
                            for q in range(GT // 4):
                                pe.wait_ge(S("hot_ready"), GT // 4 * j + q + 1)
                                pe.wait_ge(S("g_bank_free"), GT // 4 * j + q + 1)
                                for n in range(4):
                                    r = 4 * (q % 2) + n
                                    last = nc.tensor.matmul(bank[6 + q % 2][:, n * P:(n + 1) * P], hot[:, r, 0, :], hot[:, r, 1, :],
                                                            start=True, stop=True)
                                last.then_inc(S("g_mm"), 1)
                                hidden(HPRE + 2 * j + q // 4, q // 4, range(q % 4 * 2, q % 4 * 2 + 2))

                    @block.scalar
                    def _(act):
                        def u_high(e, u):
                            act.wait_ge(S(f"u_loaded{u}"), 16 * (e // 2) + 16)
                            nc.scalar.activation(u_hi[u][:], ub[u][:], ACT.Copy).then_inc(S("u_hi"), 1)

                        def gelu(e, u):
                            act.wait_ge(S("hid_mm"), e + 1)
                            act.wait_ge(S(f"hid_stored{u}"), 16 * (HT // 2) * tt + 16 * (e // 2) + 16)
                            nc.scalar.activation(hid[u][:], hbank[u][:], ACT.Gelu_apprx_tanh, bias=zero).then_inc(S("hid_bank_free"), 1)

                        def store(e, u):
                            act.wait_ge(S("hid_bank_free"), e + 3)
                            act.dma_start(hid_dram[bass.ds(HT * tt + e, 1)].rearrange("g p t -> (g p) t"), hid[u][:]
                                          ).then_inc(S(f"hid_stored{u}"), 16)

                        nc.scalar.activation(qs[:], qT[:, :, bass.ds(tt * P, P)], ACT.Copy).then_inc(S("qs_done"), 1)
                        for b in range(4):
                            act.wait_ge(S("s_mm"), b + 1)
                            nc.scalar.activation(s[:, 4 * b:4 * b + 4, :].rearrange("p a n -> p (a n)"), bank[b][:], ACT.Copy
                                                 ).then_inc(S("s_done"), 1)
                        for e in range(2):
                            u_high(e, e % 2)
                        for e in range(HPRE):
                            gelu(e, e % 2)
                            u_high(e + 2, e % 2)
                            store(e, e % 2)
                        act.wait_ge(S("soft_x"), 1)
                        nc.scalar.activation(best[:], best[:], ACT.Exp, bias=zero).then_inc(S("soft_e"), 1)
                        act.wait_ge(S("slots_t"), 1)
                        nc.scalar.activation(slots[:].rearrange("p a n -> p (a n)"), bank[4][:, 0:3 * P], ACT.Copy).then_inc(S("slots_done"), 1)
                        for j in range(P // GT):
                            act.wait_ge(S(f"stage_stored{j % 2}"), 16 * (P // GT // 2) * tt + 16 * (j // 2) + 16)
                            for q in range(GT // 4):
                                act.wait_ge(S("g_mm"), GT // 4 * j + q + 1)
                                nc.scalar.activation(stage[:, j % 2, :, 4 * q:4 * q + 4],
                                                     bank[6 + q % 2][:].rearrange("p (q n) -> p n q", q=4), ACT.Copy).then_inc(S("g_bank_free"), 1)
                                if q % 4 == 3:
                                    e = HPRE + 2 * j + q // 4
                                    gelu(e, e % 2)
                                    if e + 2 < HT:
                                        u_high(e + 2, e % 2)
                                    store(e, e % 2)

                    @block.gpsimd
                    def _(pool):
                        with pool.Fori(0, HT // 2) as i:
                            for u in range(2):
                                pool.wait_ge(S("u_hi"), 2 * i + u + 1)
                                nc.gpsimd.tensor_tensor(u_lo[u][:], ub[u][:], u_hi[u][:].bitcast(F32), ALU.subtract).then_inc(S("u_lo"), 1)
                                pool.wait_ge(S("u_lo"), 2 * i + u + 1)
                                pool.sem_inc(S("u_free"), 1)

                    @block.sync
                    def _(sp):
                        def load(e, u):
                            sp.wait_ge(S("u_free"), e + 1)
                            sp.dma_start(ub[u][:].rearrange("p k n -> p (k n)"),
                                         u_d[bass.ds(HT * tt + e, 1)].rearrange("g p n -> (g p) n")).then_inc(S(f"u_loaded{u}"), 16)

                        sp.sem_inc(S("u_free"), 2)
                        with sp.Fori(0, HPRE // 2 + 2) as i:
                            for u in range(2):
                                load(2 * i + u, u)
                        for j in range(P // GT):
                            sp.wait_ge(S("g_bank_free"), GT // 4 * (j + 1) + 2)
                            sp.dma_start(g_dram[:, bass.ds(P // GT * tt + j, 1)].rearrange("p b e t -> p (b e t)"),
                                         stage[:, j % 2].rearrange("p e t -> p (e t)")).then_inc(S(f"stage_stored{j % 2}"), 16)
                            for e in range(HPRE + 4 + 2 * j, min(HPRE + 6 + 2 * j, HT)):
                                load(e, e % 2)

                    @block.vector
                    def _(dve):
                        def top16(src, n, vals, where, tag):
                            for m in range(n):
                                if tag == "key" and m % 4 == 0:
                                    dve.wait_ge(S("s_done"), m // 4 + 1)
                                nc.vector.max(vals[:, m, 0:8], src[:, m, :]).then_inc(S(f"{tag}_max"), 1)
                            for m in range(n):
                                dve.wait_ge(S(f"{tag}_max"), m + 1)
                                nc.vector.max_index(where[:, m, 0:8], vals[:, m, 0:8], src[:, m, :]).then_inc(S(f"{tag}_idx"), 1)
                                dve.wait_ge(S(f"{tag}_idx"), m + 1)
                                nc.vector.match_replace(src[:, m, :], vals[:, m, 0:8], src[:, m, :], NEG).then_inc(S(f"{tag}_rep"), 1)
                            for m in range(n):
                                dve.wait_ge(S(f"{tag}_rep"), m + 1)
                                nc.vector.max(vals[:, m, 8:16], src[:, m, :]).then_inc(S(f"{tag}_max"), 1)
                            for m in range(n):
                                dve.wait_ge(S(f"{tag}_max"), n + m + 1)
                                nc.vector.max_index(where[:, m, 8:16], vals[:, m, 8:16], src[:, m, :]).then_inc(S(f"{tag}_idx"), 1)
                            dve.wait_ge(S(f"{tag}_idx"), 2 * n)

                        top16(s, QT, top, idx, "key")
                        nc.vector.tensor_copy(idf[:], idx[:]).then_inc(S("idf_done"), 1)
                        nc.vector.tensor_tensor(cand[:].rearrange("p h (k j) -> p h k j", k=TOPK), top[:, 0:QT:2, :].unsqueeze(3).to_broadcast(four),
                                                top[:, 1:QT:2, :].unsqueeze(2).to_broadcast(four), ALU.add).then_inc(S("cand_done"), 1)
                        dve.wait_ge(S("cand_done"), 1)
                        top16(cand, PEER_H, best, pos, "cand")
                        nc.vector.tensor_scalar(pu[:, 0], pos[:], 4, None, ALU.logical_shift_right).then_inc(S("pu_done"), 1)
                        nc.vector.tensor_scalar(pu[:, 1], pos[:], 15, None, ALU.bitwise_and).then_inc(S("pu_done"), 1)
                        sh = [P, PEER_H, TOPK]
                        nc.vector.tensor_copy(ssum[:], best[:, :, 0]).then_inc(S("soft_m"), 1)
                        dve.wait_ge(S("soft_m"), 1)
                        nc.vector.tensor_tensor(best[:], best[:], ssum[:].unsqueeze(2).to_broadcast(sh), ALU.subtract).then_inc(S("soft_x"), 1)
                        dve.wait_ge(S("pu_done"), 2)
                        nc.vector.tensor_copy(pf[:], pu[:]).then_inc(S("pf_done"), 1)
                        dve.wait_ge(S("soft_e"), 1)
                        nc.vector.tensor_reduce(ssum[:], best[:], AX.X, ALU.add).then_inc(S("soft_m"), 1)
                        dve.wait_ge(S("soft_m"), 2)
                        nc.vector.reciprocal(ssum[:], ssum[:]).then_inc(S("soft_m"), 1)
                        dve.wait_ge(S("soft_m"), 3)
                        nc.vector.tensor_tensor(chosen[:, 0, :].rearrange("p (h k) -> p h k", h=PEER_H), best[:],
                                                ssum[:].unsqueeze(2).to_broadcast(sh), ALU.mult).then_inc(S("chosen_done"), 1)
                        dve.wait_ge(S("pf_done"), 1)
                        dve.wait_ge(S("idf_done"), 1)
                        for n in range(2):
                            dve.wait_ge(S("chosen_done"), n + 1)
                            nc.vector.tensor_tensor(eq, pf[:, n].unsqueeze(3).to_broadcast(four),
                                                    cst[:, C_OFF["iota"]:C_OFF["iota"] + TOPK].unsqueeze(1).unsqueeze(1).to_broadcast(four),
                                                    ALU.is_equal).then_inc(S("pick"), 1)
                            dve.wait_ge(S("pick"), 2 * n + 1)
                            nc.vector.tensor_tensor(eq, eq, idf[:, n:QT:2, :].unsqueeze(2).to_broadcast(four), ALU.mult).then_inc(S("pick"), 1)
                            dve.wait_ge(S("pick"), 2 * n + 2)
                            nc.vector.tensor_reduce(chosen[:, 1 + n, :].rearrange("p (h k) -> p h k", h=PEER_H), eq, AX.X, ALU.add
                                                    ).then_inc(S("chosen_done"), 1)
                        dve.wait_ge(S("slots_done"), 1)
                        dve.sem_inc(S("hot_free"), 2)
                        with dve.Fori(0, P // 8) as i:
                            for w in range(2):
                                dve.wait_ge(S("g_bank_free"), 2 * i + w + 1)
                                for q in range(4):
                                    t = bass.ds(8 * i + 4 * w + q, 1)
                                    nc.vector.tensor_scalar(hot[:, 4 * w + q, 0, :], C("iota"), slots[:, 1, t], slots[:, 0, t],
                                                            ALU.is_equal, ALU.mult)
                                    last = nc.vector.tensor_scalar(hot[:, 4 * w + q, 1, :], C("iota"), slots[:, 2, t], None, ALU.is_equal)
                                last.then_inc(S("hot_ready"), 1)
                clear_since(before)
            route.close()

            turns, v_d = HEAD // NT, a["v"][bass.ds(layer, 1)].rearrange("l i g n -> (l i) g n")
            acc = sb(peer, "acc", [P, KD, T])

            def values(dve, n, w, g, a_hi, a_lo):
                w = w.rearrange("p (b t) -> p b t", t=GT)
                a_hi, a_lo = (x.rearrange("p (b t) -> p b t", t=GT) for x in (a_hi, a_lo))
                nc.vector.tensor_tensor(w, w, g, ALU.mult).then_inc(S("act_prod"), 1)
                dve.wait_ge(S("act_prod"), n + 1)
                nc.vector.tensor_copy(a_hi, w).then_inc(S("act_hi"), 1)
                dve.wait_ge(S("act_hi"), n + 1)
                nc.vector.tensor_tensor(a_lo, w, a_hi.bitcast(F32), ALU.subtract).then_inc(S("act_lo"), 1)

            before = set(made)
            with ExitStack() as ph, nc.Block() as block:
                vb = sb(ph, "vb", [P, NT, D])
                v_hi = [sb(ph, f"v_hi{u}", [P, NT, D], FR) for u in range(2)]
                v_lo = [sb(ph, f"v_lo{u}", [P, NT, D], FR) for u in range(2)]
                gb = sb(ph, "gb", [P, T // GT, NT, GT])
                hb = sb(ph, "hb", [P, NT, T])
                a_hi = [sb(ph, f"a_hi{u}", [P, NT, T], FR) for u in range(2)]
                a_lo = [sb(ph, f"a_lo{u}", [P, NT, T], FR) for u in range(2)]

                @block.sync
                def _(sp):
                    for name in ("v_free", "in_free"):
                        sp.sem_inc(S(name), 1)
                    for u in range(2):
                        sp.wait_ge(S(f"stage_stored{u}"), 16 * (T // GT // 2) + 16)
                        sp.wait_ge(S(f"hid_stored{u}"), 16 * (HEAD // 2) + 16)
                    sp.sem_inc(S("stores_done"), 1)
                    with sp.Fori(0, turns) as i:
                        sp.wait_ge(S("v_free"), i + 1)
                        sp.dma_start(vb[:].rearrange("p a n -> p (a n)"), v_d[:, bass.ds(i, 1), :].rearrange("p g n -> p (g n)")
                                     ).then_inc(S("v_loaded"), 16)
                        sp.wait_ge(S("in_free"), i + 1)
                        sp.dma_start(gb[:], g_dram[:, :, bass.ds(NT * i, NT), :]).then_inc(S("in_loaded"), 16)
                        sp.dma_start(hb[:], hid_dram[bass.ds(NT * i, NT)].rearrange("g p t -> p g t")).then_inc(S("in_loaded"), 16)

                @block.scalar
                def _(act):
                    act.sem_inc(S("v_split_free"), 2)
                    with act.Fori(0, turns // 2) as i:
                        for u in range(2):
                            act.wait_ge(S("v_loaded"), 16 * (2 * i + u) + 16)
                            act.wait_ge(S("v_split_free"), 2 * i + u + 1)
                            for e in range(NT):
                                nc.scalar.activation(v_hi[u][:, e, :], vb[:, e, :], ACT.Copy).then_inc(S("v_hi"), 1)

                @block.tensor
                def _(pe):
                    pe.sem_inc(S("acc_bank_free"), KD)
                    with pe.Fori(0, turns // 2) as i:
                        for u in range(2):
                            n = 2 * i + u
                            for half in range(2):
                                for e in range(NT):
                                    if half == 0:
                                        pe.wait_ge(S("v_lo"), NT * n + e + 1)
                                        pe.wait_ge(S("act_lo"), NT * n + e + 1)
                                    for m in range(4):
                                        d = 4 * half + m
                                        if e == 0:
                                            pe.wait_ge(S("acc_bank_free"), KD * n + d + 1)
                                        dd = slice(d * P, (d + 1) * P)
                                        last = mm3(bank[d][:], (v_hi[u][:, e, dd], v_lo[u][:, e, dd]), (a_hi[u][:, e, :], a_lo[u][:, e, :]),
                                                   e == 0, e == NT - 1)
                                        if e == NT - 1:
                                            last.then_inc(S("out_tile"), 1)

                @block.vector
                def _(dve):
                    def prepare(n, u):
                        for e in range(NT):
                            dve.wait_ge(S("v_hi"), NT * n + e + 1)
                            nc.vector.tensor_tensor(v_lo[u][:, e, :], vb[:, e, :], v_hi[u][:, e, :].bitcast(F32), ALU.subtract
                                                    ).then_inc(S("v_lo"), 1)
                        dve.wait_ge(S("v_lo"), NT * n + NT)
                        dve.sem_inc(S("v_free"), 1)
                        dve.wait_ge(S("in_loaded"), 32 * n + 32)
                        for e in range(NT):
                            values(dve, NT * n + e, hb[:, e, :], gb[:, :, e, :], a_hi[u][:, e, :], a_lo[u][:, e, :])
                        dve.wait_ge(S("act_lo"), NT * n + NT)
                        dve.sem_inc(S("in_free"), 1)

                    def add(n):
                        for d in range(KD):
                            dve.wait_ge(S("out_tile"), KD * n + d + 1)
                            if d == KD - 1:
                                dve.sem_inc(S("v_split_free"), 1)
                            nc.vector.tensor_tensor(acc[:, d, :], acc[:, d, :], bank[d][:], ALU.add).then_inc(S("acc_bank_free"), 1)
                        dve.wait_ge(S("acc_bank_free"), KD * (n + 2))

                    dve.wait_ge(S("stores_done"), 1)
                    nc.vector.memset(acc[:], 0.0).then_inc(S("acc_zero"), 1)
                    dve.wait_ge(S("acc_zero"), 1)
                    prepare(0, 0)
                    with dve.Fori(0, turns // 2 - 1) as i:
                        prepare(2 * i + 1, 1)
                        add(2 * i)
                        prepare(2 * i + 2, 0)
                        add(2 * i + 1)
                    prepare(turns - 1, 1)
                    add(turns - 2)
                    add(turns - 1)
            clear_since(before)

            with ExitStack() as ph, nc.Block() as block:
                ub = sb(ph, "ub", [P, NT, KD, P])
                vb = sb(ph, "vb", [P, NT, D])
                u_hi, u_lo = sb(ph, "u_hi", [P, NT, KD, P], FR), sb(ph, "u_lo", [P, NT, KD, P], FR)
                v_hi, v_lo = sb(ph, "v_hi", [P, NT, D], FR), sb(ph, "v_lo", [P, NT, D], FR)
                gb = sb(ph, "gb", [P, T // GT, NT, GT])
                act_w = sb(ph, "act_w", [P, 2, T])
                a_hi, a_lo = sb(ph, "a_hi", [P, NT, T], FR), sb(ph, "a_lo", [P, NT, T], FR)
                u_d = lay("u")

                @block.sync
                def _(sp):
                    for name in ("u_free", "v_free", "gb_free"):
                        sp.sem_inc(S(name), 1)
                    with sp.Fori(0, turns) as i:
                        sp.wait_ge(S("u_free"), i + 1)
                        sp.dma_start(ub[:].rearrange("p a k n -> p a (k n)"), u_d[bass.ds(HEAD + NT * i, NT)].rearrange("g p n -> p g n")
                                     ).then_inc(S("u_loaded"), 16)
                        sp.wait_ge(S("v_free"), i + 1)
                        sp.dma_start(vb[:].rearrange("p a n -> p (a n)"), v_d[:, bass.ds(turns + i, 1), :].rearrange("p g n -> p (g n)")
                                     ).then_inc(S("v_loaded"), 16)
                        sp.wait_ge(S("gb_free"), i + 1)
                        sp.dma_start(gb[:], g_dram[:, :, bass.ds(HEAD + NT * i, NT), :]).then_inc(S("gb_loaded"), 16)

                @block.tensor
                def _(pe):
                    pe.sem_inc(S("hid_bank_free"), 2)
                    pe.sem_inc(S("acc_bank_free"), 4)
                    with pe.Fori(0, turns) as i:
                        for e in range(NT):
                            pe.wait_ge(S("u_lo"), NT * i + e + 1)
                            pe.wait_ge(S("hid_bank_free"), NT * i + e + 1)
                            for k in range(KD):
                                last = mm3(bank[e % 2][:], (u_hi[:, e, k, :], u_lo[:, e, k, :]), (h_hi[:, k, :], h_lo[:, k, :]),
                                           k == 0, k == KD - 1)
                            last.then_inc(S("hid_mm"), 1)
                        for half in range(2):
                            for e in range(NT):
                                if half == 0:
                                    pe.wait_ge(S("v_lo"), NT * i + e + 1)
                                    pe.wait_ge(S("act_lo"), NT * i + e + 1)
                                for m in range(4):
                                    d = 4 * half + m
                                    if e == 0:
                                        pe.wait_ge(S("acc_bank_free"), KD * i + d + 1)
                                    dd = slice(d * P, (d + 1) * P)
                                    last = mm3(bank[2 + m][:], (v_hi[:, e, dd], v_lo[:, e, dd]), (a_hi[:, e, :], a_lo[:, e, :]),
                                               e == 0, e == NT - 1)
                                    if e == NT - 1:
                                        last.then_inc(S("out_tile"), 1)

                @block.scalar
                def _(act):
                    def u_high(i):
                        act.wait_ge(S("u_loaded"), 16 * i + 16)
                        for e in range(NT):
                            nc.scalar.activation(u_hi[:, e], ub[:, e], ACT.Copy).then_inc(S("u_hi"), 1)

                    def turn(i, last=False):
                        act.wait_ge(S("v_loaded"), 16 * i + 16)
                        act.wait_ge(S("v_split_free"), i + 1)
                        for e in range(NT):
                            nc.scalar.activation(v_hi[:, e, :], vb[:, e, :], ACT.Copy).then_inc(S("v_hi"), 1)
                        for e in range(NT):
                            act.wait_ge(S("hid_mm"), NT * i + e + 1)
                            act.wait_ge(S("act_free"), NT * i + e + 1)
                            nc.scalar.activation(act_w[:, e % 2, :], bank[e % 2][:], ACT.Gelu_apprx_tanh, bias=zero).then_inc(S("hid_bank_free"), 1)
                        if not last:
                            u_high(i + 1)

                    act.sem_inc(S("v_split_free"), 1)
                    u_high(0)
                    with act.Fori(0, turns - 1) as i:
                        turn(i)
                    turn(turns - 1, True)

                @block.vector
                def _(dve):
                    def u_low(i):
                        for e in range(NT):
                            dve.wait_ge(S("u_hi"), NT * i + e + 1)
                            nc.vector.tensor_tensor(u_lo[:, e], ub[:, e], u_hi[:, e].bitcast(F32), ALU.subtract).then_inc(S("u_lo"), 1)
                        dve.wait_ge(S("u_lo"), NT * i + NT)
                        dve.sem_inc(S("u_free"), 1)

                    def turn(i, last=False):
                        for e in range(NT):
                            dve.wait_ge(S("v_hi"), NT * i + e + 1)
                            nc.vector.tensor_tensor(v_lo[:, e, :], vb[:, e, :], v_hi[:, e, :].bitcast(F32), ALU.subtract).then_inc(S("v_lo"), 1)
                        dve.wait_ge(S("v_lo"), NT * i + NT)
                        dve.sem_inc(S("v_free"), 1)
                        dve.wait_ge(S("gb_loaded"), 16 * i + 16)
                        for e in range(NT):
                            dve.wait_ge(S("hid_bank_free"), NT * i + e + 3)
                            values(dve, NT * i + e, act_w[:, e % 2, :], gb[:, :, e, :], a_hi[:, e, :], a_lo[:, e, :])
                            dve.wait_ge(S("act_lo"), NT * i + e + 1)
                            dve.sem_inc(S("act_free"), 1)
                        dve.sem_inc(S("gb_free"), 1)
                        if not last:
                            u_low(i + 1)
                        for d in range(KD):
                            dve.wait_ge(S("out_tile"), KD * i + d + 1)
                            if d == KD - 1:
                                dve.sem_inc(S("v_split_free"), 1)
                            nc.vector.tensor_tensor(acc[:, d, :], acc[:, d, :], bank[2 + d % 4][:], ALU.add).then_inc(S("acc_bank_free"), 1)
                        dve.wait_ge(S("acc_bank_free"), KD * i + KD + 4)

                    dve.sem_inc(S("act_free"), 2)
                    u_low(0)
                    with dve.Fori(0, turns - 1) as i:
                        turn(i)
                    turn(turns - 1, True)
                    for d in range(KD):
                        nc.vector.scalar_tensor_tensor(xT[:, d, :], acc[:, d, :], mod[:, 5 * KD + d:5 * KD + d + 1], xT[:, d, :],
                                                       ALU.mult, ALU.add).then_inc(S("x_ffn"), 1)
                    dve.wait_ge(S("x_ffn"), KD)
            peer.close()
            clear_since(outside)

        with ExitStack() as ph:
            hT = sb(ph, "yT", [P, KD, T])
            norm(hT, "nfin", fnw)
            with nc.Block() as block:
                @block.sync
                def _(sp):
                    sp.dma_start(out, hT[:]).then_inc(S("out_stored"), 16)
                    sp.wait_ge(S("out_stored"), 16)


def _tiles(w):
    L, d, n = w.shape
    return w.reshape(L, d // P, P, n // P, P).transpose(0, 3, 2, 1, 4)


def _col(w):
    return w.reshape(w.shape[0], -1, P).transpose(0, 2, 1)


def _over(w):
    return np.broadcast_to(w[:, None, :], (w.shape[0], P, w.shape[1]))


def layout(i):
    L, B = DEPTH, WIDTH
    w_in = i["w_in"]
    sizes = (B, 768, SSM_H, 3 * B, B, 4, 4, 256, 256, B, B, RANK, B, B, 4 * D)
    at = np.concatenate([[0], np.cumsum(sizes)])
    part = [w_in[:, :, at[n]:at[n + 1]] for n in range(len(sizes))]
    ssm_z, xbc, dt, qkv, gdn_z, beta, decay, gq, gk, gv, gr, glow, lx, lg, merge = part
    cat = np.concatenate
    taps = cat([i["ssm_conv_w"], i["gdn_conv_w"], i["lru_conv_w"]], 2)
    taps = taps.reshape(L, 4, N_CONV, P).transpose(0, 3, 2, 1).reshape(L, P, N_CONV * 4)
    cbias = cat([i["ssm_conv_b"], np.zeros((L, 3 * B), np.float32), i["lru_conv_b"]], 1)
    vecs = cat([_col(i["b_ada"]), _col(i["norm_mix_w"]), _col(i["norm_ffn_w"]), taps, _col(cbias), _col(i["gla_b_gate"]),
                _col(i["lru_b_a"]), _col(i["lru_b_x"]), _col(i["lru_lambda"]), _col(np.repeat(i["ssm_d"], SSM_P, 1)),
                _col(i["ssm_norm_w"]), _col(i["gdn_norm_w"]), _col(i["gla_norm_w"]),
                _over(cat([i["ssm_dt_bias"], i["gdn_dt_bias"]], 1)), _over(cat([i["ssm_a_log"], i["gdn_a_log"]], 1))], 2)
    consts, sel = constants()
    return {
        "x": i["x"][0].T.reshape(KD, P, T).transpose(1, 0, 2),
        "c": i["c"][0].reshape(KD, P).T,
        "fnw": i["final_norm_w"].reshape(KD, P).T,
        "consts": consts, "sel": sel, "vecs": vecs,
        "w_ada": i["w_ada"].reshape(L, KD, P, 6 * D),
        "w_ch": _tiles(cat([xbc, qkv, lx, gq, gk, lg], 2)).reshape(L, N_CH, P, KD * P),
        "w_zt": _tiles(cat([ssm_z, gdn_z, gr, gv], 2)).reshape(L, 4, 4, P, KD * P).transpose(0, 1, 3, 2, 4).reshape(L, 4, P, 4 * KD * P),
        "w_small": cat([dt, decay, beta, glow], 2).reshape(L, KD, P, SMALL).transpose(0, 2, 1, 3),
        "w_merge": _tiles(merge).reshape(L, N_MERGE, P, KD * P),
        "w_gate": i["gla_w_gate"],
        "w_lru": np.stack([i["lru_w_a"], i["lru_w_x"]], 1).reshape(L, 2, 4, 2, 64, 64).transpose(0, 3, 4, 1, 2, 5),
        "w_branch": i["w_branch"].reshape(L, 4, NW, P, KD, P).transpose(0, 1, 4, 3, 2, 5).reshape(L, N_MERGE, P, NW * P),
        "w_out": _tiles(i["w_out"]).reshape(L, KD, P, KD * P),
        "w_q": _tiles(i["peer_w_q"]).reshape(L, QT, P, KD * P),
        "keys": i["peer_sub_keys"].reshape(L, QT, KEYS, P).transpose(0, 3, 1, 2),
        "u": i["peer_u"].reshape(L, KEYS, KEYS, KD, P).transpose(0, 2, 4, 3, 1).reshape(L, KEYS, P, KD * P),
        "v": i["peer_v"].reshape(L, KEYS, KEYS // 4, 4 * D),
    }


def kernel(**inputs):
    import concourse.bacc as bacc
    from concourse.bass_utils import run_bass_kernel_spmd as run

    nc = bacc.Bacc("TRN2", target_bir_lowering=False, num_devices=1)
    arrays, dram = {}, {}
    for name, x in layout({k: np.asarray(x) for k, x in inputs.items()}).items():
        arrays[f"in_{name}"] = np.ascontiguousarray(x)
        dram[name] = nc.dram_tensor(f"in_{name}", x.shape, F32, kind="ExternalInput").ap()
    out = nc.dram_tensor("out", (P, KD, T), F32, kind="ExternalOutput").ap()
    build(nc, dram, out)
    got = run(nc, [arrays], core_ids=[0]).results[0]["out"]
    return np.ascontiguousarray(got.transpose(1, 0, 2).reshape(D, T).T)[None]
```
